# Optimizing a Trainium2 kernel written in Bass

```python
import jax, jax.numpy as jnp
from jax import lax
import numpy as np

D_MODEL = 1024
BATCH = 1
SEQ = 1024
DEPTH = 1
DEC_BATCH = 8
DEC_SEQ = 1
PAST_LEN = 4096
PAGE_SIZE = 128

CONV_WIDTH = D_MODEL // 2
ATTN_WIDTH = D_MODEL - CONV_WIDTH
HEAD_DIM = 64
N_HEADS = ATTN_WIDTH // HEAD_DIM
N_KV_HEADS = 2
Q_PER_KV = N_HEADS // N_KV_HEADS
KV_WIDTH = N_KV_HEADS * HEAD_DIM
CONV_K = 3
CMP_BLOCK = 32
CMP_STRIDE = 16
CMP_CHUNKS = CMP_BLOCK // CMP_STRIDE
CMP_HIDDEN = 2 * HEAD_DIM
SEL_BLOCK = 64
N_SEL = 16
WINDOW = 512
Q_BLOCK = 128
ROPE_THETA = 10000.0
N_GROUPS = 4
EXPERTS_PER_GROUP = 8
N_EXPERTS = N_GROUPS * EXPERTS_PER_GROUP
D_EXPERT = D_MODEL // 2
TOP_K_IN_GROUP = 2
MOE_BLOCK = 128
NORM_EPS = 1e-6
NEG_INF = -1e30
FORCE_SCORE = 1e4
IN_SPLITS = (CONV_WIDTH, CONV_WIDTH, CONV_WIDTH, ATTN_WIDTH, 2 * KV_WIDTH, 2 * KV_WIDTH, 2 * KV_WIDTH, 3 * N_HEADS)
D_IN = sum(IN_SPLITS)

kernel_name = 'hymba_conv_nsa_hmoe_step'

def rms_norm(x, g):
    xf = x.astype(jnp.float32)
    y = xf * lax.rsqrt(jnp.mean(xf * xf, axis=-1, keepdims=True) + NORM_EPS)
    return (y * g.astype(jnp.float32)).astype(x.dtype)

def rope(x, pos):
    half = HEAD_DIM // 2
    inv = ROPE_THETA ** (-jnp.arange(half, dtype=jnp.float32) / half)
    ang = pos.astype(jnp.float32)[:, None] * inv[None, :]
    cos = jnp.cos(ang)[:, None, :]
    sin = jnp.sin(ang)[:, None, :]
    xf = x.astype(jnp.float32)
    x1, x2 = xf[..., :half], xf[..., half:]
    return jnp.concatenate([x1 * cos - x2 * sin, x1 * sin + x2 * cos], axis=-1).astype(x.dtype)

def rope_kv(kv, pos):
    return jnp.stack([rope(kv[:, :, 0], pos), kv[:, :, 1]], axis=2)

def adaln(c, w_ada, b_ada):
    m = jax.nn.silu(c) @ w_ada + b_ada
    return jnp.split(m[:, None, :], 6, axis=-1)

def project(h, w_in):
    B, T, _ = h.shape
    z = h @ w_in
    cuts = np.cumsum(IN_SPLITS)[:-1].tolist()
    b_g, c_g, u, q, kvc, kvs, kvw, gl = jnp.split(z, cuts, axis=-1)
    kv = lambda t: t.reshape(B, T, 2, N_KV_HEADS, HEAD_DIM)
    gates = jax.nn.sigmoid(gl.astype(jnp.float32)).reshape(B, T, 3, N_KV_HEADS, Q_PER_KV)
    return b_g, c_g, u, q.reshape(B, T, N_HEADS, HEAD_DIM), kv(kvc), kv(kvs), kv(kvw), gates

def short_conv(b_g, c_g, u, prev, w_conv):
    v = c_g * u
    ext = jnp.concatenate([prev, v], axis=1)
    T = v.shape[1]
    y = sum(w_conv[j] * ext[:, j:j + T] for j in range(CONV_K))
    return b_g * y, ext[:, -(CONV_K - 1):]

def compress_blocks(kv_raw, cmp_pos, cmp_w1, cmp_b1, cmp_w2, cmp_b2):
    B, L = kv_raw.shape[:2]
    n_chunk = L // CMP_STRIDE
    n_cmp = n_chunk - CMP_CHUNKS + 1
    chunks = kv_raw[:, :n_chunk * CMP_STRIDE].reshape(B, n_chunk, CMP_STRIDE, 2, N_KV_HEADS, HEAD_DIM)
    w1 = cmp_w1.reshape(2, CMP_CHUNKS, CMP_STRIDE, HEAD_DIM, CMP_HIDDEN)
    proj = jnp.einsum('bnsckd,crsdh->bnrckh', chunks, w1)
    hid = sum(proj[:, m:m + n_cmp, m] for m in range(CMP_CHUNKS))
    bias = jnp.einsum('cld,cldh->ch', cmp_pos, cmp_w1) + cmp_b1
    hid = jax.nn.gelu(hid + bias[:, None, :])
    return jnp.einsum('bnckh,chd->bnckd', hid, cmp_w2) + cmp_b2[:, None, :]

def nsa_keys(kv_cmp_raw, kv_sel, cmp_params):
    B, L = kv_sel.shape[:2]
    comp = compress_blocks(kv_cmp_raw, *cmp_params)
    n_cmp = comp.shape[1]
    cmp_end = (jnp.arange(n_cmp, dtype=jnp.int32) + CMP_CHUNKS) * CMP_STRIDE - 1
    ck = rope(comp[:, :, 0], cmp_end)
    cv = comp[:, :, 1]
    n_sel = -(-L // SEL_BLOCK)
    sel = jnp.pad(kv_sel, ((0, 0), (0, n_sel * SEL_BLOCK - L), (0, 0), (0, 0), (0, 0)))
    sel = sel.reshape(B, n_sel, SEL_BLOCK, 2, N_KV_HEADS, HEAD_DIM).transpose(0, 4, 1, 2, 3, 5)
    return ck, cv, cmp_end, sel

def cmp_to_sel(imp, n_sel):
    r = SEL_BLOCK // CMP_STRIDE
    f = CMP_CHUNKS - 1
    n_cmp = imp.shape[-1]
    pad_back = r * (n_sel + 1) - f - n_cmp
    p = jnp.pad(imp, [(0, 0)] * (imp.ndim - 1) + [(f, pad_back)])
    p = p.reshape(imp.shape[:-1] + (n_sel + 1, r))
    return p[..., :n_sel, :].sum(-1) + p[..., 1:, :f].sum(-1)

def nsa_attend(q, q_pos, gates, ck, cv, cmp_end, sel_blocks, win_kv, win_pos):
    B, Tq = q.shape[:2]
    scale = HEAD_DIM ** -0.5
    qg = q.reshape(B, Tq, N_KV_HEADS, Q_PER_KV, HEAD_DIM)
    s_c = jnp.einsum('btgqd,bngd->btgqn', qg, ck).astype(jnp.float32) * scale
    valid_c = (cmp_end[None, :] <= q_pos[:, None])[None, :, None, None, :]
    p_c = jax.nn.softmax(jnp.where(valid_c, s_c, NEG_INF), axis=-1) * valid_c
    o_c = jnp.einsum('btgqn,bngd->btgqd', p_c.astype(cv.dtype), cv)
    n_sel = sel_blocks.shape[2]
    imp = cmp_to_sel(p_c.sum(axis=3), n_sel)
    blk = jnp.arange(n_sel, dtype=jnp.int32)[None, :]
    cur = (q_pos // SEL_BLOCK)[:, None]
    causal_blk = blk * SEL_BLOCK <= q_pos[:, None]
    forced = causal_blk & ((blk == 0) | (blk == cur) | (blk == cur - 1))
    score = jnp.where(forced[None, :, None, :], FORCE_SCORE,
                      jnp.where(causal_blk[None, :, None, :], imp, -1.0))
    _, idx = lax.top_k(score, min(N_SEL, n_sel))
    gathered = jax.vmap(jax.vmap(lambda blocks, ix: blocks[ix]))(sel_blocks, idx.transpose(0, 2, 1, 3))
    s_s = jnp.einsum('btgqd,bgtnkd->btgqnk', qg, gathered[..., 0, :]).astype(jnp.float32) * scale
    tok_pos = idx[..., None] * SEL_BLOCK + jnp.arange(SEL_BLOCK, dtype=jnp.int32)
    valid_s = (tok_pos <= q_pos[None, :, None, None, None])[:, :, :, None]
    s_s = jnp.where(valid_s, s_s, NEG_INF)
    p_s = jax.nn.softmax(s_s.reshape(s_s.shape[:4] + (-1,)), axis=-1).reshape(s_s.shape)
    o_s = jnp.einsum('btgqnk,bgtnkd->btgqd', p_s.astype(gathered.dtype), gathered[..., 1, :])
    s_w = jnp.einsum('btgqd,bsgd->btgqs', qg, win_kv[:, :, 0]).astype(jnp.float32) * scale
    dist = q_pos[:, None] - win_pos[None, :]
    valid_w = ((dist >= 0) & (dist <= WINDOW) & (win_pos[None, :] >= 0))[None, :, None, None, :]
    p_w = jax.nn.softmax(jnp.where(valid_w, s_w, NEG_INF), axis=-1)
    o_w = jnp.einsum('btgqs,bsgd->btgqd', p_w.astype(win_kv.dtype), win_kv[:, :, 1])
    g = gates.astype(q.dtype)[..., None]
    o = g[:, :, 0] * o_c + g[:, :, 1] * o_s + g[:, :, 2] * o_w
    return o.reshape(B, Tq, ATTN_WIDTH)

def merge_groups(conv_out, attn_out, g_out_conv, g_out_attn, w_out):
    return jnp.concatenate([rms_norm(conv_out, g_out_conv), rms_norm(attn_out, g_out_attn)], axis=-1) @ w_out

def mixer_prompt(h, w_in, w_conv, cmp_params, g_out_conv, g_out_attn, w_out):
    B, T, _ = h.shape
    b_g, c_g, u, q, kvc, kvs, kvw, gates = project(h, w_in)
    conv_out, conv_state = short_conv(b_g, c_g, u, jnp.zeros((B, CONV_K - 1, CONV_WIDTH), h.dtype), w_conv)
    pos = jnp.arange(T, dtype=jnp.int32)
    q = rope(q, pos)
    kvs = rope_kv(kvs, pos)
    kvw = rope_kv(kvw, pos)
    ck, cv, cmp_end, sel_blocks = nsa_keys(kvc, kvs, cmp_params)
    win_pad = jnp.pad(kvw, ((0, 0), (WINDOW, 0), (0, 0), (0, 0), (0, 0)))

    def query_block(i):
        start = i * Q_BLOCK
        sl = lambda t: lax.dynamic_slice_in_dim(t, start, Q_BLOCK, axis=1)
        win = lax.dynamic_slice_in_dim(win_pad, start, WINDOW + Q_BLOCK, axis=1)
        q_pos = start + jnp.arange(Q_BLOCK, dtype=jnp.int32)
        win_pos = start - WINDOW + jnp.arange(WINDOW + Q_BLOCK, dtype=jnp.int32)
        return nsa_attend(sl(q), q_pos, sl(gates), ck, cv, cmp_end, sel_blocks, win, win_pos)

    attn = lax.map(query_block, jnp.arange(T // Q_BLOCK, dtype=jnp.int32))
    attn = attn.transpose(1, 0, 2, 3).reshape(B, T, ATTN_WIDTH)
    y = merge_groups(conv_out, attn, g_out_conv, g_out_attn, w_out)
    return y, kvc, kvs, kvw[:, -min(WINDOW, T):], conv_state

def mixer_sample(h, cache_cmp, cache_sel, cache_win, conv_prev, page_table, w_in, w_conv, cmp_params,
                 g_out_conv, g_out_attn, w_out):
    B, T, _ = h.shape
    past = page_table.shape[1] * PAGE_SIZE
    b_g, c_g, u, q, kvc, kvs, kvw, gates = project(h, w_in)
    conv_out, conv_state = short_conv(b_g, c_g, u, conv_prev, w_conv)
    pos = past + jnp.arange(T, dtype=jnp.int32)
    q = rope(q, pos)
    kvs = rope_kv(kvs, pos)
    kvw = rope_kv(kvw, pos)
    gather_past = lambda pool: pool[page_table].reshape((B, past) + pool.shape[2:])
    full_cmp = jnp.concatenate([gather_past(cache_cmp), kvc], axis=1)
    full_sel = jnp.concatenate([gather_past(cache_sel), kvs], axis=1)
    ck, cv, cmp_end, sel_blocks = nsa_keys(full_cmp, full_sel, cmp_params)
    wb = cache_win.shape[1]
    win = jnp.concatenate([cache_win, kvw], axis=1)
    win_pos = past - wb + jnp.arange(wb + T, dtype=jnp.int32)
    attn = nsa_attend(q, pos, gates, ck, cv, cmp_end, sel_blocks, win, win_pos)
    y = merge_groups(conv_out, attn, g_out_conv, g_out_attn, w_out)
    return y, kvc, kvs, win[:, -min(WINDOW, wb + T):], conv_state

def grouped_experts(x, expert, weights, w_gate, w_up, w_down):
    T, D = x.shape
    K = expert.shape[1]
    M = T * K
    flat_e = expert.reshape(-1)
    order = jnp.argsort(flat_e)
    se = flat_e[order]
    tok = order // K
    sw = weights.reshape(-1)[order]
    counts = jnp.bincount(flat_e, length=N_EXPERTS)
    padded = (counts + MOE_BLOCK - 1) // MOE_BLOCK * MOE_BLOCK
    pad_end = jnp.cumsum(padded)
    pad_start = pad_end - padded
    start = jnp.cumsum(counts) - counts
    dest = pad_start[se] + jnp.arange(M, dtype=jnp.int32) - start[se]
    n_blocks = -(-(M + N_EXPERTS * (MOE_BLOCK - 1)) // MOE_BLOCK)
    slot_tok = jnp.full((n_blocks * MOE_BLOCK,), T, jnp.int32).at[dest].set(tok)
    xb = jnp.concatenate([x, jnp.zeros((1, D), x.dtype)], axis=0)[slot_tok].reshape(n_blocks, MOE_BLOCK, D)
    blk_e = jnp.minimum(jnp.searchsorted(pad_end, jnp.arange(n_blocks) * MOE_BLOCK, side='right'), N_EXPERTS - 1)

    def expert_block(args):
        xs, e = args
        return (jax.nn.silu(xs @ w_gate[e]) * (xs @ w_up[e])) @ w_down[e]

    yb = lax.map(expert_block, (xb, blk_e)).reshape(n_blocks * MOE_BLOCK, D)
    y = yb[dest] * sw[:, None].astype(yb.dtype)
    return jax.ops.segment_sum(y, tok, num_segments=T)

def hier_moe(x, w_rg, b_rg, w_re, b_re, w_gate, w_up, w_down):
    T = x.shape[0]
    rows = jnp.arange(T)
    lg = (x @ w_rg).astype(jnp.float32) + b_rg
    grp = jnp.argmax(lg, axis=-1)
    p_grp = jax.nn.softmax(lg, axis=-1)[rows, grp]
    le = ((x @ w_re).astype(jnp.float32) + b_re).reshape(T, N_GROUPS, EXPERTS_PER_GROUP)[rows, grp]
    top_v, top_i = lax.top_k(le, TOP_K_IN_GROUP)
    weights = p_grp[:, None] * jax.nn.softmax(top_v, axis=-1)
    expert = grp[:, None].astype(jnp.int32) * EXPERTS_PER_GROUP + top_i
    return grouped_experts(x, expert, weights, w_gate, w_up, w_down)

def setup_inputs(seed: int = 0) -> dict:
    key = jax.random.key(seed)
    ks = iter(jax.random.split(key, 40))
    nrm = lambda shape, s: jax.random.normal(next(ks), shape, jnp.float32) * s
    n_pages = PAST_LEN // PAGE_SIZE
    n_used = DEC_BATCH * n_pages
    n_pool = n_used + max(1, n_used // 4)
    win_buf = min(WINDOW, PAST_LEN)
    kv_row = (2, N_KV_HEADS, HEAD_DIM)
    page_table = jax.random.permutation(next(ks), n_pool)[:n_used].reshape(DEC_BATCH, n_pages).astype(jnp.int32)
    return {
        'x_prompt': nrm((BATCH, SEQ, D_MODEL), 1.0),
        'x_sample': nrm((DEC_BATCH, DEC_SEQ, D_MODEL), 1.0),
        'c_prompt': nrm((BATCH, D_MODEL), 1.0),
        'c_sample': nrm((DEC_BATCH, D_MODEL), 1.0),
        'cache_cmp_kv': nrm((DEPTH, n_pool, PAGE_SIZE) + kv_row, 1.0),
        'cache_sel_kv': nrm((DEPTH, n_pool, PAGE_SIZE) + kv_row, 1.0),
        'cache_win_kv': nrm((DEPTH, DEC_BATCH, win_buf) + kv_row, 1.0),
        'state_conv': nrm((DEPTH, DEC_BATCH, CONV_K - 1, CONV_WIDTH), 1.0),
        'page_table': page_table,
        'ln1_g': 1.0 + nrm((DEPTH, D_MODEL), 0.05),
        'ln2_g': 1.0 + nrm((DEPTH, D_MODEL), 0.05),
        'w_ada': nrm((DEPTH, D_MODEL, 6 * D_MODEL), 0.5 * D_MODEL ** -0.5),
        'b_ada': nrm((DEPTH, 6 * D_MODEL), 0.02),
        'w_in': nrm((DEPTH, D_MODEL, D_IN), D_MODEL ** -0.5),
        'w_conv': nrm((DEPTH, CONV_K, CONV_WIDTH), CONV_K ** -0.5),
        'cmp_pos': nrm((DEPTH, 2, CMP_BLOCK, HEAD_DIM), 0.1),
        'cmp_w1': nrm((DEPTH, 2, CMP_BLOCK, HEAD_DIM, CMP_HIDDEN), (CMP_BLOCK * HEAD_DIM) ** -0.5),
        'cmp_b1': nrm((DEPTH, 2, CMP_HIDDEN), 0.02),
        'cmp_w2': nrm((DEPTH, 2, CMP_HIDDEN, HEAD_DIM), CMP_HIDDEN ** -0.5),
        'cmp_b2': nrm((DEPTH, 2, HEAD_DIM), 0.02),
        'g_out_conv': 1.0 + nrm((DEPTH, CONV_WIDTH), 0.05),
        'g_out_attn': 1.0 + nrm((DEPTH, ATTN_WIDTH), 0.05),
        'w_out': nrm((DEPTH, D_MODEL, D_MODEL), D_MODEL ** -0.5),
        'w_route_group': nrm((DEPTH, D_MODEL, N_GROUPS), D_MODEL ** -0.5),
        'b_route_group': nrm((DEPTH, N_GROUPS), 0.01),
        'w_route_expert': nrm((DEPTH, D_MODEL, N_EXPERTS), D_MODEL ** -0.5),
        'b_route_expert': nrm((DEPTH, N_EXPERTS), 0.01),
        'w_gate': nrm((DEPTH, N_EXPERTS, D_MODEL, D_EXPERT), D_MODEL ** -0.5),
        'w_up': nrm((DEPTH, N_EXPERTS, D_MODEL, D_EXPERT), D_MODEL ** -0.5),
        'w_down': nrm((DEPTH, N_EXPERTS, D_EXPERT, D_MODEL), D_EXPERT ** -0.5),
        'final_g': 1.0 + nrm((D_MODEL,), 0.05),
    }

def reference(x_prompt, x_sample, c_prompt, c_sample, cache_cmp_kv, cache_sel_kv, cache_win_kv, state_conv,
              page_table, ln1_g, ln2_g, w_ada, b_ada, w_in, w_conv, cmp_pos, cmp_w1, cmp_b1, cmp_w2, cmp_b2,
              g_out_conv, g_out_attn, w_out, w_route_group, b_route_group, w_route_expert, b_route_expert,
              w_gate, w_up, w_down, final_g):
    xp, xs = x_prompt, x_sample
    cmp_p, cmp_s, sel_p, sel_s, win_p, win_s, conv_p, conv_s = [], [], [], [], [], [], [], []
    for l in range(DEPTH):
        sh1p, sc1p, ga1p, sh2p, sc2p, ga2p = adaln(c_prompt, w_ada[l], b_ada[l])
        sh1s, sc1s, ga1s, sh2s, sc2s, ga2s = adaln(c_sample, w_ada[l], b_ada[l])
        cmp_params = (cmp_pos[l], cmp_w1[l], cmp_b1[l], cmp_w2[l], cmp_b2[l])
        hp = rms_norm(xp, ln1_g[l]) * (1 + sc1p) + sh1p
        yp, kvc_p, kvs_p, kvw_p, cs_p = mixer_prompt(hp, w_in[l], w_conv[l], cmp_params,
                                                     g_out_conv[l], g_out_attn[l], w_out[l])
        hs = rms_norm(xs, ln1_g[l]) * (1 + sc1s) + sh1s
        ys, kvc_s, kvs_s, kvw_s, cs_s = mixer_sample(hs, cache_cmp_kv[l], cache_sel_kv[l], cache_win_kv[l],
                                                     state_conv[l], page_table, w_in[l], w_conv[l], cmp_params,
                                                     g_out_conv[l], g_out_attn[l], w_out[l])
        xp = xp + ga1p * yp
        xs = xs + ga1s * ys
        hp2 = rms_norm(xp, ln2_g[l]) * (1 + sc2p) + sh2p
        hs2 = rms_norm(xs, ln2_g[l]) * (1 + sc2s) + sh2s
        n_p = hp2.shape[0] * hp2.shape[1]
        f = hier_moe(jnp.concatenate([hp2.reshape(-1, D_MODEL), hs2.reshape(-1, D_MODEL)], axis=0),
                     w_route_group[l], b_route_group[l], w_route_expert[l], b_route_expert[l],
                     w_gate[l], w_up[l], w_down[l])
        xp = xp + ga2p * f[:n_p].reshape(xp.shape)
        xs = xs + ga2s * f[n_p:].reshape(xs.shape)
        cmp_p.append(kvc_p); cmp_s.append(kvc_s)
        sel_p.append(kvs_p); sel_s.append(kvs_s)
        win_p.append(kvw_p); win_s.append(kvw_s)
        conv_p.append(cs_p); conv_s.append(cs_s)
    y_prompt = rms_norm(xp, final_g)
    y_sample = rms_norm(xs, final_g)
    new_cmp_prompt = jnp.stack(cmp_p)
    new_cmp_sample = jnp.stack(cmp_s)
    new_sel_prompt = jnp.stack(sel_p)
    new_sel_sample = jnp.stack(sel_s)
    new_win_prompt = jnp.stack(win_p)
    new_win_sample = jnp.stack(win_s)
    new_conv_prompt = jnp.stack(conv_p)
    new_conv_sample = jnp.stack(conv_s)
    return (y_prompt, y_sample, new_cmp_prompt, new_cmp_sample, new_sel_prompt, new_sel_sample,
            new_win_prompt, new_win_sample, new_conv_prompt, new_conv_sample)


_drawn_inputs = setup_inputs


def setup_inputs(seed=0):
    import zlib

    import numpy as np

    out = dict(_drawn_inputs(seed))
    spreads = {}
    factors = {'ln2_g': 3.616,
     'cmp_b1': 7.512,
     'cmp_b2': 3.719,
     'g_out_conv': 5.171,
     'g_out_attn': 4.814,
     'b_route_group': 8.0,
     'b_route_expert': 8.0}
    for name, (base, spread) in spreads.items():
        noise = np.random.default_rng([zlib.crc32(name.encode()), seed]).standard_normal(out[name].shape)
        drawn = base * np.exp(spread * noise) if base else spread * noise
        out[name] = __import__('jax').numpy.asarray(drawn.astype(out[name].dtype))
    for name, factor in factors.items():
        out[name] = (out[name] * factor).astype(out[name].dtype)
    return out
```

```python
from contextlib import ExitStack

import concourse.bass as bass
import numpy as np
from concourse import mybir

ALU = mybir.AluOpType
ACT = mybir.ActivationFunctionType
F32 = mybir.dt.float32
I32 = mybir.dt.int32
U32 = mybir.dt.uint32
F32R = mybir.dt.float32r
AX = mybir.AxisListType.X

P = 128
D = 1024
KT = D // P
T = 1024
NT = T // P
NB = 8
PAST = 4096
CW = 512
CJ = CW // P
HD = 64
NH = 8
NG = 2
QG = NH // NG
TOK = 1304
QO, CO, SO, WO, GO = 0, 512, 768, 1024, 1280
EPS = 1e-6
NEG = -1e30
NE = 32
NGR = 4
EPG = NE // NGR
DE = 512
NTOK = T + NB
TT = NT + 1
ZROW = NTOK
NOV = 16
NBLK = NE + NOV
NPAGE = PAST // 128
ADA1 = 2 * D // 512
ADA = 6 * D // 512
NCH = PAST // 16
NCMP = NCH - 1
NSB = 15


def wait(eng, sem, value):
    if not (isinstance(value, int) and value <= 0):
        eng.wait_ge(sem, value)


def rows_of(t):
    return P if t < NT else NB


class Chain:

    def __init__(self, eng, sem):
        self.eng, self.sem, self.n = eng, sem, 0

    def __call__(self, ins):
        self.n += 1
        ins.then_inc(self.sem, 1)
        self.eng.wait_ge(self.sem, self.n)


class Scope:

    def __init__(self, nc, name):
        self.nc, self.name, self.stack, self.sems = nc, name, ExitStack(), []

    def __enter__(self):
        return self

    def __exit__(self, *a):
        self.stack.close()
        self.nc.clear_and_free_semaphores(self.sems)
        self.nc.all_engine_barrier()

    def sb(self, name, shape, dt=F32):
        return self.stack.enter_context(self.nc.sbuf_tensor(f"{self.name}_{name}", shape, dt))

    def ps(self, name, shape, dt=F32):
        return self.stack.enter_context(self.nc.psum_tensor(f"{self.name}_{name}", shape, dt))

    def sem(self, name):
        self.sems.append(self.nc.alloc_semaphore(name=f"{self.name}_{name}"))
        return self.sems[-1]

    def block(self):
        return self.stack.enter_context(self.nc.Block())


def stage_ada(nc, a):
    NC = ADA1
    NBUF = 4
    with Scope(nc, "ada") as s:
        c9 = s.sb("c9", [9, D])
        sc9 = s.sb("sc9", [9, D])
        cT = s.sb("cT", [P, KT, 9])
        ident = s.sb("ident", [P, P])
        bias = s.sb("bias", [9, 2 * D])
        g9 = s.sb("g9", [9, D])
        mrow = s.sb("mrow", [9, 2 * D])
        wa = [s.sb(f"wa{i}", [P, KT, 512]) for i in range(NBUF)]
        pT = s.ps("pT", [P, KT, 9])
        pm = [s.ps(f"pm{i}", [9, 512]) for i in range(2)]
        loaded = s.sem("loaded")
        rows_in = s.sem("rows_in")
        w_in = [s.sem(f"w_in{i}") for i in range(NBUF)]
        silu_done = s.sem("silu_done")
        cT_psum = s.sem("cT_psum")
        cT_done = s.sem("cT_done")
        prod = s.sem("prod")
        added = s.sem("added")
        scaled = s.sem("scaled")
        stored = s.sem("stored")
        block = s.block()

        @block.sync
        def _(sp):
            sp.dma_start(c9[0:NB, :], a["c_sample"]).then_inc(loaded, 16)
            sp.dma_start(c9[NB:9, :], a["c_prompt"]).then_inc(loaded, 16)
            sp.dma_start(ident[:, :], a["c_ident"]).then_inc(loaded, 16)
            for n in range(NC):
                if n >= NBUF:
                    sp.wait_ge(prod, n - NBUF + 1)
                sp.dma_start(wa[n % NBUF][:, :, :],
                             a["w_ada"][0, :, n * 512:(n + 1) * 512].rearrange("(k p) n -> p k n", p=P)
                             ).then_inc(w_in[n % NBUF], 16)
                if n == 1:
                    sp.dma_start(bias[:, :], a["b_ada"][:, 0:2 * D].to_broadcast([9, 2 * D])).then_inc(rows_in, 16)
                    sp.dma_start(g9[:, :], a["ln1_g"].to_broadcast([9, D])).then_inc(rows_in, 16)
            sp.wait_ge(cT_done, 1)
            sp.dma_start(a["s_cT"], cT[:, :, :].rearrange("p k n -> p (k n)")).then_inc(stored, 16)
            sp.wait_ge(added, NC)
            sp.wait_ge(scaled, 1)
            sp.dma_start(a["s_mod"][:, 0:2 * D], mrow[:, :]).then_inc(stored, 16)
            sp.wait_ge(stored, 32)

        @block.scalar
        def _(act):
            act.wait_ge(loaded, 48)
            act.activation(sc9[:, :], c9[:, :], ACT.Silu).then_inc(silu_done, 1)

        @block.tensor
        def _(pe):
            pe.wait_ge(loaded, 48)
            pe.wait_ge(silu_done, 1)
            for k in range(KT):
                last = pe.transpose(pT[:, k, :], sc9[:, k * P:(k + 1) * P], ident[0:9, 0:9])
            last.then_inc(cT_psum, 1)
            pe.wait_ge(cT_done, 1)
            for n in range(NC):
                pe.wait_ge(w_in[n % NBUF], 16 * (n // NBUF + 1))
                if n >= 2:
                    pe.wait_ge(added, n - 1)
                for k in range(KT):
                    last = pe.matmul(pm[n % 2][:, :], cT[:, k, :], wa[n % NBUF][:, k, :],
                                     start=(k == 0), stop=(k == KT - 1))
                last.then_inc(prod, 1)

        @block.vector
        def _(dve):
            dve.wait_ge(cT_psum, 1)
            dve.tensor_copy(cT[:, :, :], pT[:, :, :]).then_inc(cT_done, 1)
            dve.wait_ge(rows_in, 32)
            for n in range(NC):
                dve.wait_ge(prod, n + 1)
                dve.tensor_tensor(mrow[:, n * 512:(n + 1) * 512], pm[n % 2][:, :],
                                  bias[:, n * 512:(n + 1) * 512], ALU.add).then_inc(added, 1)
            dve.wait_ge(added, NC)
            dve.scalar_tensor_tensor(out=mrow[:, D:2 * D], in0=mrow[:, D:2 * D], scalar=1.0, in1=g9[:, :],
                                     op0=ALU.add, op1=ALU.mult).then_inc(scaled, 1)


def stage_project(nc, a):
    with Scope(nc, "proj") as s:
        ident = s.sb("ident", [P, P])
        x = [s.sb(f"x{i}", [P, D]) for i in range(3)]
        xn = [s.sb(f"xn{i}", [P, D]) for i in range(2)]
        junk = s.sb("junk", [P, D])
        ss = s.sb("ss", [P, 3 * TT])
        eps = s.sb("eps", [P, 1])
        hT = s.sb("hT", [P, KT, T])
        hTs = s.sb("hTs", [P, KT, NB])
        scol = s.sb("scol", [P, KT])
        bcol = s.sb("bcol", [P, KT])
        srow = s.sb("srow", [NB, 2, D])
        wc = [s.sb(f"wc{i}", [P, KT, 3, P]) for i in range(2)]
        wt = s.sb("wt", [P, KT, TOK])
        wconv = s.sb("wconv", [P, 3, CJ])
        wconvs = s.sb("wconvs", [NB, 3, CW])
        csb = [s.sb(f"csb{i}", [P, 512]) for i in range(2)]
        v = [s.sb(f"v{i}", [P, 2 + T]) for i in range(2)]
        y = s.sb("y", [P, 512])
        co = [s.sb(f"co{i}", [P, T]) for i in range(2)]
        tail = s.sb("tail", [P, CJ, 2])
        zc = s.sb("zc", [NB, 3, CW])
        st = s.sb("st", [NB, 2, CW])
        vs = s.sb("vs", [NB, CW])
        ys = s.sb("ys", [NB, 2, CW])
        z = [s.sb(f"z{i}", [P, TOK]) for i in range(2)]
        r1 = s.sb("r1", [P, 512])
        r2 = s.sb("r2", [P, 512])
        rope = [s.sb(f"rope{i}", [P, 4, HD]) for i in range(2)]
        tp = [s.ps(f"tp{i}", [P, 4, P]) for i in range(2)]
        ps = [s.ps(f"ps{i}", [P, 512]) for i in range(6)]

        const_in = s.sem("const_in")
        x_in = [s.sem(f"x_in{i}") for i in range(3)]
        wc_in = [s.sem(f"wc_in{i}") for i in range(2)]
        wt_in = s.sem("wt_in")
        rope_in = [s.sem(f"rope_in{i}") for i in range(2)]
        summed = s.sem("summed")
        squared = s.sem("squared")
        rstd = s.sem("rstd")
        normed = s.sem("normed")
        turned = s.sem("turned")
        evac_v = s.sem("evac_v")
        evac_a = s.sem("evac_a")
        modded = s.sem("modded")
        group = s.sem("group")
        c_copied = s.sem("c_copied")
        conv_done = s.sem("conv_done")
        sconv_psum = s.sem("sconv_psum")
        sconv_copied = s.sem("sconv_copied")
        z_copied = s.sem("z_copied")
        roped = s.sem("roped")
        vch = s.sem("vch")
        tails = s.sem("tails")
        samp = s.sem("samp")
        co_out = [s.sem(f"co_out{i}") for i in range(2)]
        z_out = [s.sem(f"z_out{i}") for i in range(2)]
        end_out = s.sem("end_out")
        block = s.block()
        NG_CONV = 2 * CJ

        def load_wc(sp, j):
            for r in range(3):
                sp.dma_start(wc[j % 2][:, :, r, :],
                             a["w_in"][0, :, r * CW + j * P:r * CW + (j + 1) * P].rearrange("(k p) n -> p k n", p=P)
                             ).then_inc(wc_in[j % 2], 16)

        def outs_of(t):
            return 4 if t >= NT // 2 else 3

        def store_z(pool, t):
            n = rows_of(t)
            pool.wait_ge(roped, t + 1)
            zt = z[t % 2]
            pool.dma_start(a["s_z"][t * P:t * P + n, :], zt[0:n, :]).then_inc(z_out[t % 2], 16)
            for off, op, os in ((CO, "o_cmp_p", "o_cmp_s"), (SO, "o_sel_p", "o_sel_s")):
                dst = (a[op][0, 0, t * P:(t + 1) * P] if t < NT else a[os][0, :, 0]).rearrange("t c g d -> t (c g d)")
                pool.dma_start(dst, zt[0:n, off:off + 256]).then_inc(z_out[t % 2], 16)
            if t >= NT // 2:
                if t < NT:
                    dst = a["o_win_p"][0, 0, t * P - 512:t * P - 512 + P]
                else:
                    dst = a["o_win_s"][0, :, 511]
                pool.dma_start(dst.rearrange("t c g d -> t (c g d)"), zt[0:n, WO:WO + 256]).then_inc(z_out[t % 2], 16)

        @block.sync
        def _(sp):
            sp.dma_start(x[0][:, :], a["x_prompt"][0, 0:P, :]).then_inc(x_in[0], 16)
            sp.dma_start(ident[:, :], a["c_ident"]).then_inc(const_in, 16)
            with nc.allow_non_contiguous_dma(reason="one column of a small vector"):
                sp.dma_start(scol[:, :], a["s_mod"][NB, D:2 * D].rearrange("(k p) -> p k", p=P)).then_inc(const_in, 16)
                sp.dma_start(bcol[:, :], a["s_mod"][NB, 0:D].rearrange("(k p) -> p k", p=P)).then_inc(const_in, 16)
                for r in range(3):
                    sp.dma_start(wconv[:, r, :], a["w_conv"][0, r].rearrange("(j p) -> p j", p=P)).then_inc(const_in, 16)
            sp.dma_start(srow[:, 0, :], a["s_mod"][0:NB, 0:D]).then_inc(const_in, 16)
            sp.dma_start(srow[:, 1, :], a["s_mod"][0:NB, D:2 * D]).then_inc(const_in, 16)
            sp.dma_start(wconvs[:, :, :].rearrange("p r n -> p (r n)"),
                         a["w_conv"].rearrange("a r n -> a (r n)").to_broadcast([NB, 3 * CW])).then_inc(const_in, 16)
            sp.dma_start(st[:, :, :], a["state_conv"][0]).then_inc(const_in, 16)
            for t in range(1, TT):
                if t >= 3:
                    sp.wait_ge(normed, t - 2)
                src = a["x_prompt"][0, t * P:(t + 1) * P, :] if t < NT else a["x_sample"][:, 0, :]
                sp.dma_start(x[t % 3][0:rows_of(t), :], src).then_inc(x_in[t % 3], 16)
                if t == 2:
                    for j in range(2):
                        load_wc(sp, j)
            sp.dma_start(wt[:, :, :], a["w_in"][0, :, 3 * CW:].rearrange("(k p) n -> p k n", p=P)).then_inc(wt_in, 16)
            for j in range(2, CJ):
                sp.wait_ge(group, 2 * j - 2)
                sp.wait_ge(sconv_psum, j - 1)
                load_wc(sp, j)
            for j in range(CJ):
                sp.wait_ge(conv_done, 2 * j + 2)
                sp.dma_start(a["s_convT"][j], co[j % 2][:, :]).then_inc(co_out[j % 2], 16)

        @block.gpsimd
        def _(pool):
            for t in range(TT):
                n = rows_of(t)
                if t >= 2:
                    pool.wait_ge(roped, t - 1)
                rows = slice(t * P, t * P + n)
                for j in range(4):
                    src = a["c_rope"][j % 2 if j < 2 else 2 + j % 2]
                    pool.dma_start(rope[t % 2][0:n, j, :], src[rows, :]).then_inc(rope_in[t % 2], 16)
                if t >= 1:
                    store_z(pool, t - 1)
            store_z(pool, TT - 1)
            pool.wait_ge(tails, CJ)
            with nc.allow_non_contiguous_dma(reason="two rows of conv state"):
                for r in range(2):
                    pool.dma_start(a["o_conv_p"][0, 0, r].rearrange("(j p) -> p j", p=P),
                                   tail[:, :, r]).then_inc(end_out, 16)
            pool.wait_ge(samp, 1)
            pool.dma_start(a["o_conv_s"][0, :, 0, :], st[:, 1, :]).then_inc(end_out, 16)
            pool.dma_start(a["o_conv_s"][0, :, 1, :], vs[:, :]).then_inc(end_out, 16)
            pool.dma_start(a["s_convs"], ys[:, 1, :]).then_inc(end_out, 16)
            pool.wait_ge(end_out, 16 * 5)
            for i in range(2):
                pool.wait_ge(co_out[i], 16 * (CJ // 2))
                pool.wait_ge(z_out[i], 16 * sum(outs_of(t) for t in range(i, TT, 2)))

        @block.scalar
        def _(act):
            def square(t):
                n = rows_of(t)
                act.wait_ge(x_in[t % 3], 16 * (t // 3 + 1))
                if t:
                    act.wait_ge(squared, t)
                act.activation(junk[0:n, :], x[t % 3][0:n, :], ACT.Square,
                               accum_out=ss[0:n, t:t + 1]).then_inc(summed, 1)
                act.wait_ge(summed, t + 1)
                act.activation(ss[0:n, TT + t:TT + t + 1], ss[0:n, t:t + 1], ACT.Sqrt, bias=eps[0:n, :],
                               scale=1.0 / D).then_inc(squared, 1)

            act.wait_ge(const_in, 16 * 10)
            act.wait_ge(vch, 3)
            square(0)
            for t in range(TT):
                n = rows_of(t)
                if t + 1 < TT:
                    square(t + 1)
                act.wait_ge(rstd, t + 1)
                if t >= 2:
                    act.wait_ge(turned, t - 1)
                act.activation(xn[t % 2][0:n, :], x[t % 3][0:n, :], ACT.Copy,
                               scale=ss[0:n, 2 * TT + t:2 * TT + t + 1]).then_inc(normed, 1)
                if t < NT:
                    act.wait_ge(turned, t + 1)
                    for k in range(4, KT):
                        last = act.activation(hT[:, k, t * P:(t + 1) * P], tp[1][:, k - 4, :], ACT.Identity,
                                              bias=bcol[:, k:k + 1], scale=scol[:, k:k + 1])
                    last.then_inc(evac_a, 1)
                else:
                    act.wait_ge(turned, TT)
                    act.activation(hTs[:, 4:8, :], tp[1][:, :, 0:NB], ACT.Copy).then_inc(evac_a, 1)
            for g in range(NG_CONV):
                act.wait_ge(group, g + 1)
                if g >= 2:
                    act.wait_ge(conv_done, g - 1)
                act.activation(csb[g % 2][:, :], ps[g % 2 * 3 + 1][:, :], ACT.Copy).then_inc(c_copied, 1)
                if g % 2:
                    j = g // 2
                    act.wait_ge(sconv_psum, j + 1)
                    act.activation(zc[:, :, j * P:(j + 1) * P],
                                   tp[j % 2][0:NB, 0:3, :], ACT.Copy).then_inc(sconv_copied, 1)
            for t in range(TT):
                n = rows_of(t)
                g = NG_CONV + t
                act.wait_ge(group, g + 1)
                if t >= 2:
                    act.wait_ge(z_out[t % 2], 16 * sum(outs_of(i) for i in range(t % 2, t, 2)))
                b = g % 2 * 3
                act.activation(z[t % 2][0:n, 0:512], ps[b][0:n, :], ACT.Copy)
                act.activation(z[t % 2][0:n, 512:1024], ps[b + 1][0:n, :], ACT.Copy)
                act.activation(z[t % 2][0:n, 1024:GO], ps[b + 2][0:n, 0:GO - 1024], ACT.Copy)
                act.activation(z[t % 2][0:n, GO:TOK], ps[b + 2][0:n, GO - 1024:TOK - 1024],
                               ACT.Sigmoid).then_inc(z_copied, 1)

        @block.tensor
        def _(pe):
            pe.wait_ge(const_in, 16 * 10)
            for t in range(TT):
                n = rows_of(t)
                if t < NT:
                    pe.wait_ge(normed, t + 1)
                    src = xn[t % 2]
                else:
                    pe.wait_ge(modded, 1)
                    src = junk
                if t:
                    pe.wait_ge(evac_v, t)
                    pe.wait_ge(evac_a, t)
                for k in range(KT):
                    last = pe.transpose(tp[k // 4][:, k % 4, 0:n], src[0:n, k * P:(k + 1) * P], ident[0:n, 0:n])
                last.then_inc(turned, 1)
            pe.wait_ge(evac_v, TT)
            pe.wait_ge(evac_a, TT)
            for g in range(NG_CONV):
                j, half = g // 2, g % 2
                pe.wait_ge(wc_in[j % 2], 48 * (j // 2 + 1))
                if g >= 2:
                    pe.wait_ge(conv_done, g - 1)
                for r in range(3):
                    for k in range(KT):
                        last = pe.matmul(ps[g % 2 * 3 + r][:, :], wc[j % 2][:, k, r, :],
                                         hT[:, k, half * 512:(half + 1) * 512],
                                         start=(k == 0), stop=(k == KT - 1))
                last.then_inc(group, 1)
                if half:
                    if j >= 2:
                        pe.wait_ge(sconv_copied, j - 1)
                    for k in range(KT):
                        last = pe.matmul(tp[j % 2][0:NB, 0:3, :], hTs[:, k, :], wc[j % 2][:, k, :, :],
                                         start=(k == 0), stop=(k == KT - 1))
                    last.then_inc(sconv_psum, 1)
            pe.wait_ge(wt_in, 16)
            for t in range(TT):
                g = NG_CONV + t
                n = rows_of(t)
                if t < 2:
                    pe.wait_ge(conv_done, g - 1)
                else:
                    pe.wait_ge(z_copied, t - 1)
                for c in range(3):
                    w = min(512, TOK - c * 512)
                    for k in range(KT):
                        lhs = hT[:, k, t * P:(t + 1) * P] if t < NT else hTs[:, k, :]
                        last = pe.matmul(ps[g % 2 * 3 + c][0:n, 0:w], lhs, wt[:, k, c * 512:c * 512 + w],
                                         start=(k == 0), stop=(k == KT - 1))
                last.then_inc(group, 1)

        @block.vector
        def _(dve):
            step = Chain(dve, vch)
            for i in range(2):
                step(dve.memset(v[i][:, 0:2], 0.0))
            step(dve.memset(eps[:, :], EPS))
            dve.wait_ge(const_in, 16 * 10)
            for t in range(TT):
                n = rows_of(t)
                dve.wait_ge(squared, t + 1)
                dve.reciprocal(ss[0:n, 2 * TT + t:2 * TT + t + 1], ss[0:n, TT + t:TT + t + 1]).then_inc(rstd, 1)
                if t < NT:
                    dve.wait_ge(turned, t + 1)
                    for k in range(4):
                        last = dve.tensor_scalar(hT[:, k, t * P:(t + 1) * P], tp[0][:, k, :],
                                                 scol[:, k:k + 1], bcol[:, k:k + 1], ALU.mult, ALU.add)
                    last.then_inc(evac_v, 1)
                else:
                    dve.wait_ge(normed, TT)
                    step(dve.tensor_tensor(junk[0:n, :], xn[t % 2][0:n, :], srow[:, 1, :], ALU.mult))
                    dve.tensor_tensor(junk[0:n, :], junk[0:n, :], srow[:, 0, :], ALU.add).then_inc(modded, 1)
                    dve.wait_ge(turned, TT)
                    dve.tensor_copy(hTs[:, 0:4, :], tp[0][:, :, 0:NB]).then_inc(evac_v, 1)
            for g in range(NG_CONV):
                j, half = g // 2, g % 2
                vj, lo = v[j % 2], half * 512
                if j >= 2 and not half:
                    dve.wait_ge(co_out[j % 2], 16)
                dve.wait_ge(c_copied, g + 1)
                step(dve.tensor_tensor(vj[:, 2 + lo:2 + lo + 512], csb[g % 2][:, :], ps[g % 2 * 3 + 2][:, :], ALU.mult))
                step(dve.tensor_scalar(y[:, :], vj[:, lo:lo + 512], wconv[:, 0, j:j + 1], None, ALU.mult))
                for r in (1, 2):
                    step(dve.scalar_tensor_tensor(out=y[:, :], in0=vj[:, lo + r:lo + r + 512], scalar=wconv[:, r, j:j + 1],
                                                  in1=y[:, :], op0=ALU.mult, op1=ALU.add))
                if half:
                    dve.tensor_copy(tail[:, j, :], vj[:, T:T + 2]).then_inc(tails, 1)
                dve.tensor_tensor(co[j % 2][:, lo:lo + 512], y[:, :], ps[g % 2 * 3][:, :], ALU.mult).then_inc(conv_done, 1)
                dve.wait_ge(conv_done, g + 1)
            dve.wait_ge(sconv_copied, CJ)
            step(dve.tensor_tensor(vs[:, :], zc[:, 1, :], zc[:, 2, :], ALU.mult))
            step(dve.tensor_tensor(ys[:, 0, :], st[:, 0, :], wconvs[:, 0, :], ALU.mult))
            step(dve.tensor_tensor(ys[:, 1, :], st[:, 1, :], wconvs[:, 1, :], ALU.mult))
            step(dve.tensor_tensor(ys[:, 0, :], ys[:, 0, :], ys[:, 1, :], ALU.add))
            step(dve.tensor_tensor(ys[:, 1, :], vs[:, :], wconvs[:, 2, :], ALU.mult))
            step(dve.tensor_tensor(ys[:, 0, :], ys[:, 0, :], ys[:, 1, :], ALU.add))
            dve.tensor_tensor(ys[:, 1, :], ys[:, 0, :], zc[:, 0, :], ALU.mult).then_inc(samp, 1)

            for t in range(TT):
                n = rows_of(t)
                dve.wait_ge(z_copied, t + 1)
                dve.wait_ge(rope_in[t % 2], 64 * (t // 2 + 1))
                zt, rt = z[t % 2], rope[t % 2]
                parts = ([(zt[0:n, QO:512].rearrange("p (h d) -> p h d", d=HD), 8, 2)]
                         + [(zt[0:n, o:o + 128].rearrange("p (h d) -> p h d", d=HD), 2, 0) for o in (SO, WO)])
                for i, (zv, h, tab) in enumerate(parts):
                    cos = rt[0:n, tab:tab + 1, :].to_broadcast([n, h, HD])
                    sin = rt[0:n, tab + 1:tab + 2, :].to_broadcast([n, h, HD])
                    a1 = r1[0:n, 0:h * HD].rearrange("p (h d) -> p h d", d=HD)
                    a2 = r2[0:n, 0:h * HD].rearrange("p (h d) -> p h d", d=HD)
                    dve.tensor_tensor(a1, zv, cos, ALU.mult)
                    dve.tensor_tensor(a2[:, :, 0:32], zv[:, :, 32:64], sin[:, :, 0:32], ALU.mult)
                    step(dve.tensor_tensor(a2[:, :, 32:64], zv[:, :, 0:32], sin[:, :, 32:64], ALU.mult))
                    if i < 2:
                        step(dve.tensor_tensor(zv, a1, a2, ALU.add))
                dve.tensor_tensor(zv, a1, a2, ALU.add).then_inc(roped, 1)
                dve.wait_ge(roped, t + 1)


def stage_compress(nc, a):
    PCH = T // 16
    with Scope(nc, "cmp") as s:
        ident = s.sb("ident", [P, P])
        pt = s.sb("pt", [P, 2 * NB], I32)
        c8 = s.sb("c8", [P, 1])
        idxf = s.sb("idxf", [P, 2 * NB])
        idx = s.sb("idx", [P, 2 * NB], U32)
        x = [s.sb(f"x{h}", [P, 16 * 4 * HD]) for h in range(2)]
        xs = [s.sb(f"xs{h}", [P, 4, 16, HD]) for h in range(2)]
        xT = s.sb("xT", [P, 4, 8, NCH])
        w1 = s.sb("w1", [P, 32, P])
        pos = s.sb("pos", [P, 32])
        b1 = s.sb("b1", [P, 2])
        bias = s.sb("bias", [P, 2])
        w2 = s.sb("w2", [P, 2, HD])
        w2r = s.sb("w2r", [P, HD])
        b2 = s.sb("b2", [HD, 2])
        b2v = s.sb("b2v", [P, HD])
        rope = s.sb("rope", [HD, 2, NCMP])
        hid = s.sb("hid", [P, 4, NCMP])
        t1 = s.sb("t1", [HD, NCMP])
        t2 = s.sb("t2", [HD, NCMP])
        ck = s.sb("ck", [HD, NG, NCMP])
        cv = s.sb("cv", [P, 2, NG, HD])
        junk = s.sb("junk", [P, 4])
        bank = [s.ps(f"bank{i}", [P, 4, P]) for i in range(4)]
        hp = [s.ps(f"hp{i}", [P, 512]) for i in range(2)]
        kp = s.ps("kp", [HD, 2, 256])
        vp = s.ps("vp", [P, 2, HD])

        pt_in = s.sem("pt_in")
        const_in = s.sem("const_in")
        idx_ready = s.sem("idx_ready")
        w2r_ready = s.sem("w2r_ready")
        bias_psum = s.sem("bias_psum")
        bias_ready = s.sem("bias_ready")
        x_in = [s.sem(f"x_in{h}") for h in range(2)]
        shuffled = s.sem("shuffled")
        turned_v = s.sem("turned_v")
        turned_a = s.sem("turned_a")
        free_v = s.sem("free_v")
        free_a = s.sem("free_a")
        hid_psum = s.sem("hid_psum")
        hid_free = s.sem("hid_free")
        k_psum = s.sem("k_psum")
        k_free = s.sem("k_free")
        v_psum = s.sem("v_psum")
        v_free = s.sem("v_free")
        tsum = s.sem("tsum")
        out_done = [s.sem(f"out_done{i}") for i in range(2)]
        win_out = s.sem("win_out")
        block = s.block()
        NCONST = 10

        def store(sp, b, i):
            sp.wait_ge(k_free, i * 2 + 3)
            sp.dma_start(a["s_ck"][bass.ds(b, 1), :, :, 0:NCMP].rearrange("o d g n -> (o d) g n"),
                         ck[:, :, :]).then_inc(out_done[0], 16)
            sp.wait_ge(v_free, i * 2 + 3)
            for h, n in ((0, P), (1, NCMP - P)):
                sp.dma_start(a["s_cv"][bass.ds(b, 1), h * P:h * P + n, :].rearrange("o n c -> (o n) c"),
                             cv[0:n, h, :, :].rearrange("p g d -> p (g d)")).then_inc(out_done[1], 16)

        def evac(eng, op, mine, i, h, n, free, turned):
            for q in range(4):
                eng.wait_ge(turned, i * 8 + 4 * h + q + 1)
                grp = 2 * q + mine
                c, sp4 = grp // 2, grp % 2
                op(xT[:, c, 4 * sp4:4 * sp4 + 4, h * P:h * P + n], bank[grp % 4][:, :, 0:n]).then_inc(free, 1)

        @block.sync
        def _(sp):
            sp.dma_start(c8[:, :], a["c_mod8"]).then_inc(pt_in, 16)
            with nc.allow_non_contiguous_dma(reason="columns of small tables"):
                for c in range(8):
                    sp.dma_start(pt[c:P:8, :], a["page_table"].rearrange("b (h g) -> g (b h)", g=16)).then_inc(pt_in, 16)
                sp.dma_start(pos[:, :], a["cmp_pos"][0].rearrange("c (t l) d -> (l d) (c t)", l=2)).then_inc(const_in, 16)
                sp.dma_start(b1[:, :], a["cmp_b1"][0].rearrange("c h -> h c")).then_inc(const_in, 16)
                kb = a["cmp_b2"][0, 0:1, :].rearrange("a d -> d a")
                sp.dma_start(b2[:, 0:1], kb).then_inc(const_in, 16)
                sp.dma_start(b2[0:32, 1:2], kb[32:64, :]).then_inc(const_in, 16)
                sp.dma_start(b2[32:64, 1:2], kb[0:32, :]).then_inc(const_in, 16)
            sp.dma_start(ident[:, :], a["c_ident"]).then_inc(const_in, 16)
            sp.dma_start(rope[:, :, :], a["c_ropec"]).then_inc(const_in, 16)
            sp.dma_start(b2v[:, :], a["cmp_b2"][0, 1:2, :].to_broadcast([P, HD])).then_inc(const_in, 16)
            sp.dma_start(w2[:, :, :], a["cmp_w2"][0].rearrange("c h d -> h c d")).then_inc(const_in, 16)
            sp.dma_start(w1[:, :, :], a["cmp_w1"][0].rearrange("c (t l) d h -> (l d) (c t) h", l=2)).then_inc(const_in, 16)
            sp.dma_start(a["o_win_s"][0, :, 0:511].rearrange("b (x y) c g d -> b x (y c g d)", y=7),
                         a["cache_win_kv"][0, :, 1:512].rearrange("b (x y) c g d -> b x (y c g d)", y=7)
                         ).then_inc(win_out, 16)
            store(sp, 0, 0)
            with sp.Fori(1, NB) as b:
                store(sp, b, b)
            sp.wait_ge(k_free, 2 * NB + 3)
            sp.dma_start(a["s_ck"][NB, :, :, 0:PCH - 1], ck[:, :, 0:PCH - 1]).then_inc(out_done[0], 16)
            sp.wait_ge(v_free, 2 * NB + 3)
            sp.dma_start(a["s_cv"][NB, 0:PCH - 1, :], cv[0:PCH - 1, 0, :, :]).then_inc(out_done[1], 16)
            sp.wait_ge(out_done[0], 16 * (NB + 1))
            sp.wait_ge(out_done[1], 32 * NB + 16)
            sp.wait_ge(win_out, 16)

        @block.gpsimd
        def _(pool):
            chunks = a["cache_cmp_kv"][0].rearrange("n (c s) k g d -> (n c) (s k g d)", s=16)

            def gather(b, h):
                pool.indirect_dma_start(x[h][:, :], None, chunks,
                                        bass.IndirectOffsetOnAxis(ap=idx[:, 2 * b + h:2 * b + h + 1], axis=0)
                                        ).then_inc(x_in[h], 16)

            pool.wait_ge(idx_ready, 1)
            gather(0, 0)
            gather(0, 1)
            for b in range(NB + 1):
                for h in range(2 if b < NB else 1):
                    n = P if b < NB else PCH
                    pool.wait_ge(x_in[h], 16 * (b + 1))
                    if b:
                        pool.wait_ge(turned_a, 8 * b + 4 * h - 4)
                    src = x[h][0:n, :].rearrange("p (s c d) -> p c s d", s=16, d=HD)
                    for c in range(4):
                        last = pool.tensor_copy(xs[h][0:n, c, :, :], src[:, c])
                    last.then_inc(shuffled, 1)
                    pool.wait_ge(shuffled, 2 * b + h + 1)
                    if b + 1 < NB:
                        gather(b + 1, h)
                    elif b + 1 == NB and h == 0:
                        pool.dma_start(x[0][0:PCH, :], a["o_cmp_p"][0, 0].rearrange("(n s) k g d -> n (s k g d)", s=16)
                                       ).then_inc(x_in[0], 16)

        @block.scalar
        def _(act):
            act.wait_ge(const_in, 16 * NCONST)
            for _ in range(2):
                act.activation(junk[:, 2:3], ident[:, 0:1], ACT.Copy).then_inc(free_a, 1)
                act.wait_ge(free_a, _ + 1)
            act.wait_ge(bias_ready, 1)

            def body(i, halves, n):
                for h, w in enumerate(halves):
                    evac(act, lambda o, x_: act.activation(o, x_, ACT.Copy), 1, i, h, w, free_a, turned_a)
                for c in range(4):
                    act.wait_ge(hid_psum, i * 4 + c + 1)
                    act.wait_ge(k_free if c < 2 else v_free, i * 2 + 1)
                    act.activation(hid[:, c, 0:n], hp[c % 2][:, 0:n], ACT.Gelu_apprx_tanh,
                                   bias=bias[:, c // 2:c // 2 + 1]).then_inc(hid_free, 1)

            body(0, (P, P), NCMP)
            with act.Fori(1, NB) as i:
                body(i, (P, P), NCMP)
            body(NB, (PCH,), PCH - 1)

        @block.vector
        def _(dve):
            dve.memset(junk[:, 0:1], 0.0).then_inc(tsum, 1)
            dve.wait_ge(tsum, 1)
            dve.wait_ge(pt_in, 16 * 9)
            dve.tensor_scalar(idxf[:, :], pt[:, :], 8.0, c8[:, 0:1], ALU.mult, ALU.add).then_inc(tsum, 1)
            dve.wait_ge(tsum, 2)
            dve.tensor_copy(idx[:, :], idxf[:, :]).then_inc(idx_ready, 1)
            dve.wait_ge(const_in, 16 * NCONST)
            dve.tensor_copy(w2r[:, 0:32], w2[:, 0, 32:64])
            dve.tensor_copy(w2r[:, 32:64], w2[:, 0, 0:32]).then_inc(w2r_ready, 1)
            dve.wait_ge(bias_psum, 1)
            dve.tensor_tensor(bias[:, :], hp[0][:, 0:2], b1[:, :], ALU.add).then_inc(bias_ready, 1)
            for sem, k in ((free_v, 2), (hid_free, 2), (k_free, 1), (v_free, 1)):
                for j in range(k):
                    dve.memset(junk[:, 0:1], 0.0).then_inc(sem, 1)
                    dve.wait_ge(sem, j + 1)

            def body(i, halves, n):
                for h, w in enumerate(halves):
                    evac(dve, lambda o, x_: dve.tensor_copy(o, x_), 0, i, h, w, free_v, turned_v)
                wait(dve, out_done[0], i * 16)
                for g in range(NG):
                    dve.wait_ge(k_psum, i * 2 + g + 1)
                    dve.scalar_tensor_tensor(out=t1[:, 0:n], in0=kp[:, 0, 0:n], scalar=b2[:, 0:1], in1=rope[:, 0, 0:n],
                                             op0=ALU.add, op1=ALU.mult).then_inc(tsum, 1)
                    dve.scalar_tensor_tensor(out=t2[:, 0:n], in0=kp[:, 1, 0:n], scalar=b2[:, 1:2], in1=rope[:, 1, 0:n],
                                             op0=ALU.add, op1=ALU.mult).then_inc(tsum, 1)
                    dve.wait_ge(tsum, i * 4 + 2 * g + 4)
                    dve.tensor_tensor(ck[:, g, 0:n], t1[:, 0:n], t2[:, 0:n], ALU.add).then_inc(k_free, 1)
                    dve.wait_ge(k_free, i * 2 + g + 2)
                wait(dve, out_done[1], i * 32)
                for g in range(NG):
                    dve.wait_ge(v_psum, i * 2 + g + 1)
                    for h in range(len(halves)):
                        w = min(P, n - h * P)
                        last = dve.tensor_tensor(cv[0:w, h, g, :], vp[0:w, h, :], b2v[0:w, :], ALU.add)
                    last.then_inc(v_free, 1)

            body(0, (P, P), NCMP)
            with dve.Fori(1, NB) as i:
                body(i, (P, P), NCMP)
            body(NB, (PCH,), PCH - 1)

        @block.tensor
        def _(pe):
            pe.wait_ge(const_in, 16 * NCONST)
            for c in range(2):
                for t in range(16):
                    last = pe.matmul(hp[0][:, c:c + 1], w1[:, 16 * c + t, :], pos[:, 16 * c + t:16 * c + t + 1],
                                     start=(t == 0), stop=(t == 15))
            last.then_inc(bias_psum, 1)
            pe.wait_ge(bias_ready, 1)
            pe.wait_ge(w2r_ready, 1)

            def body(i, halves, n):
                for h, w in enumerate(halves):
                    pe.wait_ge(shuffled, i * 2 + h + 1)
                    for grp in range(8):
                        c, sp4 = grp // 2, grp % 2
                        own = grp // 2
                        free, turned = ((free_v, turned_v), (free_a, turned_a))[grp % 2]
                        pe.wait_ge(free, i * 8 + 4 * h + own + 1)
                        for r in range(4):
                            last = pe.transpose(bank[grp % 4][:, r, 0:w], 
                                                xs[h][0:w, c, 8 * sp4 + 2 * r:8 * sp4 + 2 * r + 2, :].rearrange("p l d -> p (l d)"),
                                                ident[0:w, 0:w])
                        last.then_inc(turned, 1)
                    pe.wait_ge(free_v, i * 8 + 4 * h + 6)
                    pe.wait_ge(free_a, i * 8 + 4 * h + 6)

                def second(c):
                    pe.wait_ge(hid_free, i * 4 + c + 3)
                    if c < 2:
                        pe.wait_ge(k_free, i * 2 + c + 1)
                        pe.matmul(kp[:, 0, 0:n], w2[:, 0, :], hid[:, c, 0:n], start=True, stop=True)
                        pe.matmul(kp[:, 1, 0:n], w2r[:, :], hid[:, c, 0:n], start=True, stop=True).then_inc(k_psum, 1)
                    else:
                        pe.wait_ge(v_free, i * 2 + c - 1)
                        for h in range(len(halves)):
                            w = min(P, n - h * P)
                            last = pe.matmul(vp[0:w, h, :], hid[:, c, h * P:h * P + w], w2[:, 1, :], start=True, stop=True)
                        last.then_inc(v_psum, 1)

                for c in range(4):
                    pe.wait_ge(hid_free, i * 4 + c + 1)
                    for r in range(2):
                        for t in range(8):
                            last = pe.matmul(hp[c % 2][:, 0:n], w1[:, 16 * (c // 2) + 8 * r + t, :], xT[:, c, t, r:r + n],
                                             start=(r == 0 and t == 0), stop=(r == 1 and t == 7))
                    last.then_inc(hid_psum, 1)
                    if c:
                        second(c - 1)
                second(3)

            body(0, (P, P), NCMP)
            with pe.Fori(1, NB) as i:
                body(i, (P, P), NCMP)
            body(NB, (PCH,), PCH - 1)


SEL, WIN, CMP = range(3)


def score_chunks(i):
    out = []
    for h in range(NH):
        for k0 in range(0, (i + 1) * P, 512):
            out.append((SEL, h, k0, min(512, (i + 1) * P - k0)))
        j0 = max(0, i - 4) * P
        for k0 in range(j0, (i + 1) * P, 512):
            out.append((WIN, h, k0, min(512, (i + 1) * P - k0)))
        out.append((CMP, h, 0, min(T // 16 - 1, 8 * i + 7)))
    return out


def key_tiles(i):
    out = []
    for br in (CMP, SEL, WIN):
        for g in range(NG):
            tiles = {SEL: range(i + 1), WIN: range(max(0, i - 4), i + 1), CMP: range(1)}[br]
            out.append((br, g, list(tiles)))
    return out


def stage_prompt_attention(nc, a):
    banks = [("k", br, g, half) for br in (SEL, WIN) for g in range(NG) for half in range(2)]
    first_of = []
    for i in range(NT):
        first_of.append(len(banks))
        banks += [("q", i, half) for half in range(2)]
        banks += [("s", i) + c for c in score_chunks(i)]
        banks += [("m", i)]
    first_of.append(len(banks))
    tiles, groups, tile_of, group_of = [], [], [], []
    for i in range(NT):
        tile_of.append(len(tiles))
        group_of.append(len(groups))
        for br, g, js in key_tiles(i):
            for j in js:
                masked = br == CMP or j == i or (br == WIN and j == i - 4)
                tiles.append((i, br, g, j, len(groups), j == js[0], j == js[-1], masked))
            groups.append((i, br, g))
    tile_of.append(len(tiles))
    group_of.append(len(groups))
    masks_before = [sum(t[7] for t in tiles[:n]) for n in range(len(tiles) + 1)]
    last_tile = {t[4]: n for n, t in enumerate(tiles)}
    NST, NPT = 3, 4
    NMR = 32 + 3 * NH
    order = [("fill", n) for n in range(first_of[0])]
    for step in range(NT + 1):
        fills = list(range(first_of[step], first_of[step + 1])) if step < NT else []
        lo, hi = (tile_of[step - 1], tile_of[step]) if step else (0, 0)
        order += [("fill", n) for n in fills[:4]]
        body, last_fill = fills[4:-1], fills[-1:]
        spread, done, backs = max(1, hi - lo - 2), 0, []
        for n in range(lo, hi + 2):
            if n < hi:
                order.append(("scores", n))
            if n - 2 >= lo:
                order.append(("values", n - 2))
                if tiles[n - 2][6]:
                    backs.append((n + 2, tiles[n - 2][4]))
            while backs and backs[0][0] <= n:
                order.append(("back", backs.pop(0)[1]))
            upto = min(len(body), len(body) * (n - lo + 1) // spread)
            order += [("fill", b) for b in body[done:upto]]
            done = max(done, upto)
        order += [("fill", b) for b in body[done:]]
        order += [("back", grp) for _, grp in backs]
        order += [("fill", n) for n in last_fill]

    with Scope(nc, "att") as s:
        ident = s.sb("ident", [P, P])
        zk = s.sb("zk", [P, NT, 2, NG, 2 * HD])
        zv = s.sb("zv", [P, NT, 2, NG * HD])
        kT = [s.sb(f"kT{br}", [2 * HD, NG, T], F32R) for br in range(2)]
        ckt = s.sb("ckt", [2 * HD, NG, T // 16])
        ckT = s.sb("ckT", [2 * HD, NG, T // 16], F32R)
        va = s.sb("va", [P, NT, 2, NG, HD + 1])
        cv = s.sb("cv", [T // 16, NG * HD])
        cva = s.sb("cva", [T // 16, NG, HD + 1])
        q = [s.sb(f"q{i}", [P, NH, 2 * HD]) for i in range(2)]
        gate = s.sb("gate", [P, NT, 24])
        qh = [s.sb(f"qh{i}", [2 * HD, NH, P], F32R) for i in range(2)]
        ql = [s.sb(f"ql{i}", [2 * HD, NH, P], F32R) for i in range(2)]
        pick = s.sb("pick", [NMR, 3 * NH, P], F32R)
        diag = s.sb("diag", [P, P])
        far = s.sb("far", [P, P])
        cmask = s.sb("cmask", [P, 64])
        valid = s.sb("valid", [P, 1])
        masked = s.sb("masked", [P, 4, 2, P])
        cand = s.sb("cand", [P, 24, 4])
        mx = s.sb("mx", [P, 24])
        negm = s.sb("negm", [P, NMR])
        nmT = [s.sb(f"nmT{i}", [NMR, P], F32R) for i in range(2)]
        pT = [s.sb(f"pT{i}", [P, QG, P]) for i in range(NPT)]
        ot = [s.sb(f"ot{i}", [HD + 1, QG, P]) for i in range(2)]
        den = s.sb("den", [P, QG, 1])
        part = s.sb("part", [P, QG, HD])
        acc = [s.sb(f"acc{i}", [P, NH, HD]) for i in range(2)]
        sp_ = [s.ps(f"sp{i}", [P, 512]) for i in range(2)]
        st = [s.ps(f"st{i}", [P, 512]) for i in range(NST)]
        op = [s.ps(f"op{i}", [HD + 1, 512]) for i in range(2)]
        ob = s.ps("ob", [P, QG, HD + 1])

        zero = s.sb("zero", [P, D])

        const_in = s.sem("const_in")
        yb_out = s.sem("yb_out")
        kv_in = s.sem("kv_in")
        q_in = [s.sem(f"q_in{i}") for i in range(2)]
        ready = s.sem("ready")
        bank_full = s.sem("bank_full")
        bank_free = s.sem("bank_free")
        neg_ready = s.sem("neg_ready")
        vch = s.sem("vch")
        st_full = s.sem("st_full")
        exp_done = s.sem("exp_done")
        mask_done = s.sem("mask_done")
        pv_done = s.sem("pv_done")
        ot_ready = s.sem("ot_ready")
        ob_full = s.sem("ob_full")
        ob_free = s.sem("ob_free")
        acc_done = s.sem("acc_done")
        att_out = [s.sem(f"att_out{i}") for i in range(2)]
        split = s.sem("split")
        block = s.block()
        NKV_IN = 14

        @block.sync
        def _(sp):
            def load_q(i):
                for c in range(2):
                    sp.dma_start(q[i % 2][:, :, c * HD:(c + 1) * HD],
                                 a["s_z"][i * P:(i + 1) * P, 0:512].rearrange("t (h d) -> t h d", d=HD)
                                 ).then_inc(q_in[i % 2], 16)

            sp.dma_start(ident[:, :], a["c_ident"]).then_inc(const_in, 16)
            sp.dma_start(diag[:, :], a["c_diag"]).then_inc(const_in, 16)
            sp.dma_start(far[:, :], a["c_far"]).then_inc(const_in, 16)
            sp.dma_start(cmask[:, :], a["c_cmask"]).then_inc(const_in, 16)
            sp.dma_start(valid[:, :], a["c_valid"]).then_inc(const_in, 16)
            for br in range(2):
                at = SO + 256 * br
                for g in range(NG):
                    for c in range(2):
                        sp.dma_start(zk[:, :, br, g, c * HD:(c + 1) * HD],
                                     a["s_z"][0:T, at + g * HD:at + (g + 1) * HD].rearrange("(t p) d -> p t d", p=P)
                                     ).then_inc(kv_in, 16)
                sp.dma_start(zv[:, :, br, :], a["s_z"][0:T, at + 128:at + 256].rearrange("(t p) n -> p t n", p=P)
                             ).then_inc(kv_in, 16)
            for c in range(2):
                sp.dma_start(ckt[c * HD:(c + 1) * HD, :, 0:T // 16 - 1], a["s_ck"][NB, :, :, 0:T // 16 - 1]).then_inc(kv_in, 16)
            sp.dma_start(cv[0:T // 16 - 1, :], a["s_cv"][NB, 0:T // 16 - 1, :]).then_inc(kv_in, 16)
            sp.dma_start(gate[:, :, :], a["s_z"][0:T, GO:GO + 24].rearrange("(t p) n -> p t n", p=P)).then_inc(kv_in, 16)
            load_q(0)
            load_q(1)
            sp.wait_ge(ready, 3)
            for b in range(NE, NBLK):
                sp.dma_start(a["s_yb"][b * P:(b + 1) * P, :], zero[:, :]).then_inc(yb_out, 16)
            for i in range(NT):
                sp.wait_ge(bank_free, first_of[i + 1])
                if i + 2 < NT:
                    load_q(i + 2)
                if i >= 1:
                    sp.wait_ge(acc_done, i)
                    sp.dma_start(a["s_attn"][(i - 1) * P:i * P, :], acc[(i - 1) % 2][:, :, :].rearrange("p h d -> p (h d)")
                                 ).then_inc(att_out[(i - 1) % 2], 16)
            sp.wait_ge(acc_done, NT)
            sp.dma_start(a["s_attn"][T - P:T, :], acc[(NT - 1) % 2][:, :, :].rearrange("p h d -> p (h d)")
                         ).then_inc(att_out[(NT - 1) % 2], 16)
            sp.wait_ge(yb_out, 16 * NOV)
            sp.wait_ge(att_out[0], 16 * (NT // 2))
            sp.wait_ge(att_out[1], 16 * (NT // 2))

        @block.gpsimd
        def _(pool):
            ones = Chain(pool, ready)
            ones(pool.memset(va[:, :, :, :, HD:HD + 1], 1.0))
            ones(pool.memset(cva[:, :, HD:HD + 1], 1.0))
            ones(pool.memset(zero[:, :], 0.0))
            for what, n in order:
                if what == "scores" and tiles[n][7]:
                    i, br, g, j, grp, first, final, is_masked = tiles[n]
                    pool.wait_ge(exp_done, n + 1)
                    rows = min(T // 16 - 1, 8 * i + 7) if br == CMP else P
                    pt = pT[n % NPT][0:rows, :, :]
                    if br == CMP:
                        base, mult, sgn = i * P - 31, -16, 1
                    elif j == i:
                        base, mult, sgn = 0, -1, 1
                    else:
                        base, mult, sgn = 0, 1, -1
                    pool.affine_select(out=pt, in_=pt, compare_op=ALU.is_ge, fill=0.0, base=base,
                                       pattern=[[0, QG], [sgn, P]], channel_multiplier=mult).then_inc(mask_done, 1)

        @block.scalar
        def _(act):
            for what, n in order:
                if what == "scores":
                    i, br = tiles[n][0:2]
                    rows = min(T // 16 - 1, 8 * i + 7) if br == CMP else P
                    act.wait_ge(st_full, n + 1)
                    if n >= NPT:
                        act.wait_ge(pv_done, n - NPT + 1)
                    act.activation(pT[n % NPT][0:rows, :, :].rearrange("p h q -> p (h q)"), st[n % NST][0:rows, :],
                                   ACT.Exp).then_inc(exp_done, 1)
                elif what == "values" and tiles[n][6]:
                    grp = tiles[n][4]
                    act.wait_ge(pv_done, n + 1)
                    if grp >= 2:
                        act.wait_ge(ob_full, grp - 1)
                    act.activation(ot[grp % 2][:, :, :].rearrange("p h q -> p (h q)"), op[grp % 2][:, :], ACT.Copy
                                   ).then_inc(ot_ready, 1)

        @block.tensor
        def _(pe):
            pe.wait_ge(const_in, 80)
            pe.wait_ge(kv_in, 16 * NKV_IN)
            pe.wait_ge(ready, 2)
            pe.wait_ge(split, 2)

            def fill(n):
                b = banks[n]
                dst = sp_[n % 2]
                if n >= 2:
                    pe.wait_ge(bank_free, n - 1)
                if b[0] == "k":
                    _, br, g, half = b
                    for t in range(4):
                        last = pe.transpose(dst[:, t * P:(t + 1) * P], zk[:, half * 4 + t, br, g, :], ident[:, :])
                elif b[0] == "q":
                    _, i, half = b
                    if half == 0:
                        pe.wait_ge(q_in[i % 2], 32 * (i // 2 + 1))
                    for t in range(4):
                        h = half * 4 + t
                        last = pe.transpose(dst[:, t * P:(t + 1) * P], q[i % 2][:, h, :], ident[:, :])
                elif b[0] == "s":
                    _, i, br, h, k0, w = b
                    keys = ckT if br == CMP else kT[br]
                    if n < first_of[i] + 4:
                        pe.wait_ge(bank_free, first_of[i] + 2)
                    w += w % 2
                    pe.matmul(dst[:, 0:w], qh[i % 2][:, h, :], keys[:, h // QG, k0:k0 + w], start=True, stop=False)
                    last = pe.matmul(dst[:, 0:w], ql[i % 2][:, h, :], keys[:, h // QG, k0:k0 + w], start=False, stop=True)
                else:
                    pe.wait_ge(neg_ready, b[1] + 1)
                    last = pe.transpose(dst[0:NMR, 0:P], negm[:, :], ident[:, :])
                last.then_inc(bank_full, 1)

            def turn_back(grp):
                pe.wait_ge(ot_ready, grp + 1)
                if grp:
                    pe.wait_ge(ob_free, grp)
                for h in range(QG):
                    last = pe.transpose(ob[:, h, :], ot[grp % 2][:, h, :], ident[0:HD + 1, 0:HD + 1])
                last.then_inc(ob_full, 1)

            def scores(n):
                i, br, g, j, grp, first, final, is_masked = tiles[n]
                if n >= NST:
                    pe.wait_ge(exp_done, n - NST + 1)
                if br == CMP:
                    rows = 8 * i + 8
                    lhs = ckT[:, g, 0:rows]
                else:
                    rows = P
                    lhs = kT[br][:, g, j * P:(j + 1) * P]
                heads = slice(QG * g, QG * g + QG)
                pe.matmul(st[n % NST][0:rows, :], lhs, qh[i % 2][:, heads, :], start=True, stop=False)
                pe.matmul(st[n % NST][0:rows, :], lhs, ql[i % 2][:, heads, :], start=False, stop=False)
                for h in range(QG):
                    last = pe.matmul(st[n % NST][0:rows, h * P:(h + 1) * P], pick[:, br * NH + QG * g + h, 0:rows],
                                     nmT[i % 2][:, :], start=False, stop=(h == QG - 1))
                last.then_inc(st_full, 1)

            def values(n):
                i, br, g, j, grp, first, final, is_masked = tiles[n]
                pe.wait_ge(exp_done, n + 1)
                if is_masked:
                    pe.wait_ge(mask_done, masks_before[n + 1])
                if first and grp >= 2:
                    pe.wait_ge(ot_ready, grp - 1)
                if br == CMP:
                    rows = min(T // 16 - 1, 8 * i + 7)
                    lhs = cva[0:rows, g, :]
                else:
                    rows = P
                    lhs = va[:, j, br, g, :]
                mm = pe.matmul(op[grp % 2][:, :], lhs, pT[n % NPT][0:rows, :, :], start=first, stop=final)
                mm.then_inc(pv_done, 1)

            for what, n in order:
                if what == "fill":
                    fill(n)
                elif what == "scores":
                    i = tiles[n][0]
                    if n == tile_of[i]:
                        pe.wait_ge(bank_free, first_of[i + 1])
                    scores(n)
                elif what == "values":
                    values(n)
                else:
                    turn_back(n)

        @block.vector
        def _(dve):
            step_ = Chain(dve, vch)
            dve.wait_ge(const_in, 80)
            dve.wait_ge(kv_in, 16 * NKV_IN)
            dve.wait_ge(ready, 2)
            for br in range(2):
                step_(dve.tensor_copy(va[:, :, br, :, 0:HD], zv[:, :, br, :].rearrange("p t (g d) -> p t g d", g=NG)))
            step_(dve.tensor_copy(cva[0:T // 16 - 1, :, 0:HD], cv[0:T // 16 - 1, :].rearrange("p (g d) -> p g d", g=NG)))
            step_(dve.memset(cand[:, :, :], -3e38))
            step_(dve.memset(negm[:, :], 0.0))
            one_of = [ident[0:NMR, c:c + 3 * NH].rearrange("p (n o) -> p n o", o=1).to_broadcast([NMR, 3 * NH, P])
                      for c in (0, 32)]
            dve.tensor_tensor(pick[:, :, :], one_of[0], one_of[1], ALU.add).then_inc(split, 1)

            def split_keys(dst, src):
                step_(dve.tensor_copy(dst[:, :], src[:, :]))
                return dve.tensor_tensor(dst[HD:2 * HD, :], src[HD:2 * HD, :], dst[HD:2 * HD, :], ALU.subtract)

            step_(dve.memset(ckt[:, :, T // 16 - 1:], 0.0))
            for g in range(NG):
                last = split_keys(ckT[:, g, :], ckt[:, g, :])
            last.then_inc(split, 1)

            def empty(n):
                b = banks[n]
                src = sp_[n % 2]
                dve.wait_ge(bank_full, n + 1)
                if b[0] == "k":
                    _, br, g, half = b
                    last = split_keys(kT[br][:, g, half * 512:(half + 1) * 512], src)
                elif b[0] == "q":
                    _, i, half = b
                    h4, l4 = (x[i % 2][:, half * 4:half * 4 + 4, :].rearrange("p h q -> p (h q)") for x in (qh, ql))
                    step_(dve.tensor_copy(h4, src[:, :]))
                    last = dve.tensor_tensor(l4, src[:, :], h4, ALU.subtract)
                elif b[0] == "s":
                    _, i, br, h, k0, w = b
                    col = cand[:, br * NH + h, :]
                    c = 0
                    if br == CMP:
                        spans = [(0, w, cmask[:, 57 - 8 * i:57 - 8 * i + w])]
                    else:
                        spans = []
                        lo, hi = 0, w
                        if br == WIN and i >= 4 and k0 == (i - 4) * P:
                            spans.append((0, P, far[:, :]))
                            lo = P
                        if k0 + w == (i + 1) * P:
                            spans.append((w - P, w, diag[:, :]))
                            hi = w - P
                        if hi > lo:
                            spans.append((lo, hi, None))
                    base = 2 if br == SEL and k0 or (br == WIN and i >= 4 and k0 > (i - 4) * P) else 0
                    dve.wait_ge(bank_free, n - 3)
                    for x0, x1, m in spans:
                        if m is None:
                            last = dve.tensor_reduce(col[:, base + c:base + c + 1], src[:, x0:x1], AX, ALU.max)
                        else:
                            last = dve.tensor_tensor_reduce(masked[:, n % 4, c % 2, 0:x1 - x0], src[:, x0:x1], m, 1.0, -3e38,
                                                            ALU.add, ALU.max, col[:, base + c:base + c + 1])
                        c += 1
                else:
                    nm = nmT[b[1] % 2]
                    step_(dve.tensor_copy(nm[:, :], src[0:NMR, 0:P]))
                    last = dve.tensor_tensor(nm[32:NMR, :], src[32:NMR, 0:P], nm[32:NMR, :], ALU.subtract)
                last.then_inc(bank_free, 1)

            def combine(grp):
                i, br, g = groups[grp]
                dve.wait_ge(ob_full, grp + 1)
                step_(dve.tensor_scalar(den[:, :, :], ob[:, :, HD:HD + 1], 1e-30, None, ALU.max))
                step_(dve.reciprocal(den[:, :, :], den[:, :, :]))
                kind = {CMP: 0, SEL: 1, WIN: 2}[br]
                w = gate[:, i, kind * NH + g * QG:kind * NH + (g + 1) * QG].rearrange("p (h o) -> p h o", o=1)
                step_(dve.tensor_tensor(den[:, :, :], den[:, :, :], w, ALU.mult))
                dst = acc[i % 2][:, g * QG:(g + 1) * QG, :]
                if br == CMP:
                    if i >= 2 and g == 0:
                        dve.wait_ge(att_out[i % 2], 16 * (i // 2))
                    dve.tensor_tensor(dst, ob[:, :, 0:HD], den[:, :, :].to_broadcast([P, QG, HD]), ALU.mult).then_inc(ob_free, 1)
                    dve.wait_ge(ob_free, grp + 1)
                else:
                    dve.tensor_tensor(part[:, :, :], ob[:, :, 0:HD], den[:, :, :].to_broadcast([P, QG, HD]),
                                      ALU.mult).then_inc(ob_free, 1)
                    dve.wait_ge(ob_free, grp + 1)
                    if br == WIN and g == NG - 1:
                        dve.tensor_tensor(dst, dst, part[:, :, :], ALU.add).then_inc(acc_done, 1)
                        dve.wait_ge(acc_done, i + 1)
                    else:
                        step_(dve.tensor_tensor(dst, dst, part[:, :, :], ALU.add))

            for what, n in order:
                if what == "fill":
                    if banks[n][0] == "m":
                        step = banks[n][1]
                        dve.wait_ge(bank_free, n)
                        step_(dve.tensor_reduce(mx[:, :], cand[:, :, :], AX, ALU.max))
                        step_(dve.memset(cand[:, :, :], -3e38))
                        if step == 0:
                            step_(dve.tensor_scalar(mx[:, CMP * NH:], mx[:, CMP * NH:], valid[:, 0:1], None, ALU.mult))
                        step_(dve.tensor_scalar(negm[:, 0:3 * NH], mx[:, :], -1.0, None, ALU.mult))
                        dve.tensor_scalar(negm[:, 32:NMR], mx[:, :], -1.0, None, ALU.mult).then_inc(neg_ready, 1)
                    empty(n)
                elif what == "back":
                    combine(n)


def stage_sample_attention(nc, a):
    NR = NB * NH
    NP_ = NB * NG
    NW = 512
    NS = NSB * 64
    NSEL = 64
    NKV = 4
    widths = (NCMP, NS, NW)
    spans = tuple([(c, min(P, n - c)) for c in range(0, n, P)] for n in widths)
    C_, S_, W_ = range(3)
    with Scope(nc, "smp") as s:
        ident = s.sb("ident", [P, P])
        q = s.sb("q", [NR, HD])
        new = s.sb("new", [NR, 2, 2, HD])
        gate = s.sb("gate", [NR, 3])
        qT = s.sb("qT", [HD, NR])
        qblk = s.sb("qblk", [HD, NP_ * (NR + QG)])
        ck = [s.sb(f"ck{i}", [HD, NG, NCMP]) for i in range(2)]
        cv = s.sb("cv", [P, NB, 2, NG * HD])
        cw = s.sb("cw", [P, NB, 4, 4 * HD])
        kvs = s.sb("kvs", [P, NKV, 8 * 4 * HD])
        kv = [kvs[:, i, :].rearrange("p (t c) -> p t c", c=4 * HD) for i in range(NKV)]
        vs = s.sb("vs", [P, NP_, 8, HD])
        kT = [s.sb(f"kT{i}", [HD, 8 * P]) for i in range(2)]
        pr = [s.sb(f"pr{i}", [NR, n]) for i, n in enumerate(widths)]
        pT = s.sb("pT", [P, 8, NR])
        pn = s.sb("pn", [NR, NCMP])
        stat = s.sb("stat", [NR, 3, 8])
        prod = s.sb("prod", [NR, HD])
        member = s.sb("member", [NR, NP_])
        imp = s.sb("imp", [NP_, 264])
        sc = s.sb("sc", [NP_, 65])
        sc5 = s.sb("sc5", [NP_, 65])
        bigs = vs[0:NP_, :, :, :].rearrange("p u t d -> p (u t d)")
        big1, big2 = (bigs[:, i * NSEL * NSEL:(i + 1) * NSEL * NSEL].rearrange("p (n m) -> p n m", n=NSEL)
                      for i in range(2))
        tri = kvs[0:NP_, 0:2, :].rearrange("p i c -> p (i c)").rearrange("p (n m) -> p n m", n=NSEL)
        cT = s.sb("cT", [P, KT, 9])
        ones9 = s.sb("ones9", [1, 9])
        wa = [s.sb(f"wa{i}", [P, KT, 512]) for i in range(2)]
        ba = [s.sb(f"ba{i}", [1, 512]) for i in range(2)]
        mrow = [s.sb(f"mrow{i}", [9, 512]) for i in range(2)]
        rank = s.sb("rank", [NP_, NSEL])
        slots = s.sb("slots", [NP_, 16])
        ptr = s.sb("ptr", [NP_, NPAGE], I32)
        base = s.sb("base", [NP_, NPAGE, 2])
        half64 = s.sb("half64", [NP_, 2])
        slotb = s.sb("slotb", [NP_, 16])
        spread = s.sb("spread", [NP_, NP_, 16])
        ones = s.sb("ones", [NP_, P])
        p64 = s.sb("p64", [P, 1])
        idxf = s.sb("idxf", [P, NP_, 8])
        idx = s.sb("idx", [P, NP_ * 8], U32)
        oT = s.sb("oT", [HD, 3, NR])
        o = s.sb("o", [NR, 3, HD])
        A = [s.ps(f"A{i}", [HD, 4, P]) for i in range(2)]
        SC = s.ps("SC", [NR, 512])
        SW = s.ps("SW", [NR, 512])
        SS = [s.ps(f"SS{i}", [NR, 512]) for i in range(2)]
        O = s.ps("O", [HD, 3, NR])
        M = s.ps("M", [P, 512])

        const_in = s.sem("const_in")
        row_in = s.sem("row_in")
        ck_in = [s.sem(f"ck_in{i}") for i in range(2)]
        cw_in = s.sem("cw_in")
        cv_in = s.sem("cv_in")
        q_turned = s.sem("q_turned")
        qblk_ready = s.sem("qblk_ready")
        c_read = s.sem("c_read")
        keys_full = s.sem("keys_full")
        keys_v = s.sem("keys_v")
        keys_a = s.sem("keys_a")
        keys_read = s.sem("keys_read")
        scored = [s.sem(f"scored{i}") for i in range(3)]
        neg_ready = [s.sem(f"neg_ready{i}") for i in range(3)]
        probs = [s.sem(f"probs{i}") for i in range(3)]
        pn_ready = s.sem("pn_ready")
        imp_psum = s.sem("imp_psum")
        spread_ready = s.sem("spread_ready")
        idx_psum = s.sem("idx_psum")
        idx_ready = s.sem("idx_ready")
        kv_in = [s.sem(f"kv_in{i}") for i in range(NKV)]
        v_kept = s.sem("v_kept")
        pT_psum = s.sem("pT_psum")
        pT_ready = s.sem("pT_ready")
        o_psum = s.sem("o_psum")
        oT_ready = s.sem("oT_ready")
        back_psum = s.sem("back_psum")
        cT_in = s.sem("cT_in")
        wa_in = [s.sem(f"wa_in{i}") for i in range(2)]
        ones_set = s.sem("ones_set")
        mod_psum = s.sem("mod_psum")
        mod_ready = s.sem("mod_ready")
        mod_out = [s.sem(f"mod_out{i}") for i in range(2)]
        vch = s.sem("vch")
        done = s.sem("done")
        out_done = s.sem("out_done")
        block = s.block()
        NROW = 4 + NP_
        MOD1 = 4
        mod_after = (3, 6, 9, 12)

        def key_unit(pe, u, src, n_tiles, width):
            for half in range(2):
                if u or half:
                    pe.wait_ge((keys_v, keys_a)[half], u)
                for t in range(n_tiles // 2):
                    tt = half * (n_tiles // 2) + t
                    n = min(P, width - tt * P)
                    last = pe.transpose(A[half][:, t, 0:n], src(tt, n), ident[0:n, 0:n])
                last.then_inc(keys_full, 1)

        @block.sync
        def _(sp):
            sp.dma_start(q[:, :], a["s_z"][T:NTOK, 0:512].rearrange("b (h d) -> b h d", d=HD)).then_inc(row_in, 16)
            with nc.allow_non_contiguous_dma(reason="gates of a row"):
                for k in range(3):
                    sp.dma_start(gate[:, k:k + 1], a["s_z"][T:NTOK, GO + 8 * k:GO + 8 * k + 8].rearrange("b (h o) -> b h o", o=1)
                                 ).then_inc(row_in, 16)
            for b in range(NB):
                for g in range(NG):
                    src = a["s_z"][T + b:T + b + 1, SO:SO + 512].rearrange("o (n g d) -> o n g d", g=NG, d=HD)[:, :, g, :]
                    r = (b * NG + g) * QG
                    sp.dma_start(new[r:r + QG, :, :, :].rearrange("p a b d -> p (a b) d"),
                                 src.to_broadcast([QG, 4, HD])).then_inc(row_in, 16)
            sp.dma_start(ident[:, :], a["c_ident"]).then_inc(const_in, 16)
            sp.dma_start(member[:, :], a["c_member"]).then_inc(const_in, 16)
            sp.dma_start(tri[:, :, :], a["c_tri64"].to_broadcast([NP_, NSEL, NSEL])).then_inc(const_in, 16)
            sp.dma_start(slots[:, :], a["c_iota"][:, 0:16].to_broadcast([NP_, 16])).then_inc(const_in, 16)
            sp.dma_start(half64[:, :], a["c_half64"].to_broadcast([NP_, 2])).then_inc(const_in, 16)
            sp.dma_start(p64[:, :], a["c_mod64"]).then_inc(const_in, 16)
            sp.dma_start(ones[:, :], a["c_ones"][0:NP_, :]).then_inc(const_in, 16)
            for g in range(NG):
                sp.dma_start(ptr[g:NP_:NG, :], a["page_table"]).then_inc(const_in, 16)
            for b in range(NB):
                if b >= 2:
                    sp.wait_ge(c_read, b - 1)
                sp.dma_start(ck[b % 2][:, :, :], a["s_ck"][b, :, :, 0:NCMP]).then_inc(ck_in[b % 2], 16)
            for b in range(NB):
                sp.dma_start(cw[:, b, :, :], a["cache_win_kv"][0, b].rearrange("(t p) k g d -> p t (k g d)", p=P)
                             ).then_inc(cw_in, 16)
            for h, (c0, n) in enumerate(spans[C_]):
                sp.dma_start(cv[0:n, :, h, :], a["s_cv"][0:NB, c0:c0 + n, :].rearrange("b n c -> n b c")).then_inc(cv_in, 16)
            sp.dma_start(cT[:, :, :].rearrange("p k n -> p (k n)"), a["s_cT"]).then_inc(cT_in, 16)
            for m in range(ADA - ADA1):
                if m >= 2:
                    sp.wait_ge(mod_psum, m - 1)
                n = slice((ADA1 + m) * 512, (ADA1 + m + 1) * 512)
                sp.dma_start(wa[m % 2][:, :, :], a["w_ada"][0, :, n].rearrange("(k p) n -> p k n", p=P)
                             ).then_inc(wa_in[m % 2], 16)
                sp.dma_start(ba[m % 2][:, :], a["b_ada"][:, n]).then_inc(wa_in[m % 2], 16)
            sp.wait_ge(mod_out[0], 16 * (ADA - ADA1) // 2)
            sp.wait_ge(mod_out[1], 16 * (ADA - ADA1) // 2)
            sp.wait_ge(done, 1)
            sp.dma_start(a["s_attn"][T:NTOK, :].rearrange("b (h d) -> b h d", d=HD), o[:, 0, :]).then_inc(out_done, 16)
            sp.wait_ge(out_done, 16)

        @block.gpsimd
        def _(pool):
            rows = a["cache_sel_kv"][0].rearrange("n s k g d -> (n s) (k g d)")
            pool.wait_ge(idx_ready, 1)
            for u in range(NP_):
                if u >= NKV:
                    pool.wait_ge(v_kept, u - NKV + 1)
                    pool.wait_ge(keys_full, 2 * (NP_ + u - NKV + 1))
                for t in range(8):
                    n = P if t < 7 else 64
                    pool.indirect_dma_start(kv[u % NKV][0:n, t, :], None, rows,
                                            bass.IndirectOffsetOnAxis(ap=idx[0:n, 8 * u + t:8 * u + t + 1], axis=0)
                                            ).then_inc(kv_in[u % NKV], 16)

        @block.tensor
        def _(pe):
            pe.wait_ge(const_in, 16 * 9)
            pe.wait_ge(row_in, 16 * NROW)
            pe.transpose(M[0:HD, 0:NR], q[:, :], ident[0:NR, 0:NR]).then_inc(q_turned, 1)
            pe.wait_ge(qblk_ready, 1)
            blk = [qblk[:, u * NR:(u + 1) * NR] for u in range(NP_)]
            for b in range(NB):
                pe.wait_ge(ck_in[b % 2], 16 * (b // 2 + 1))
                for g in range(NG):
                    u = b * NG + g
                    last = pe.matmul(SC[:, 0:NCMP], blk[u], ck[b % 2][:, g, :], start=(u == 0), stop=(u == NP_ - 1))
                last.then_inc(c_read, 1)
            pe.wait_ge(cw_in, 16 * NB)

            def score_unit(u, out, width):
                pe.wait_ge(keys_v, u + 1)
                pe.wait_ge(keys_a, u + 1)
                v = u % NP_
                for c in range(0, width, 512):
                    w = min(512, width - c)
                    last = pe.matmul(out[c // 512][:, 0:w], blk[v], kT[u % 2][:, c:c + w],
                                     start=(v == 0), stop=(v == NP_ - 1))
                last.then_inc(keys_read, 1)

            def win_src(u):
                return lambda t, n: cw[0:n, u // NG, t, (u % NG) * HD:(u % NG + 1) * HD]

            def sel_src(u):
                return lambda t, n: kv[u % NKV][0:n, t, (u % NG) * HD:(u % NG + 1) * HD]

            for u in range(NP_):
                key_unit(pe, u, win_src(u), 4, NW)
                if u:
                    score_unit(u - 1, [SW], NW)
            score_unit(NP_ - 1, [SW], NW)
            pe.wait_ge(pn_ready, 1)
            pe.matmul(M[0:NP_, 0:NCMP], member[:, :], pn[:, :], start=True, stop=True).then_inc(imp_psum, 1)

            def condition(m):
                bank = (SC, SW)[m % 2]
                pe.wait_ge(wa_in[m % 2], 32 * (m // 2 + 1))
                if m >= 2:
                    pe.wait_ge(mod_ready, m - 1)
                for k in range(KT):
                    pe.matmul(bank[0:9, :], cT[:, k, :], wa[m % 2][:, k, :], start=(k == 0), stop=False)
                pe.matmul(bank[0:9, :], ones9[:, :], ba[m % 2][:, :], start=False, stop=True).then_inc(mod_psum, 1)

            pe.wait_ge(cT_in, 16)
            pe.wait_ge(ones_set, 1)
            pe.wait_ge(probs[W_], 1)
            for m in range(MOD1):
                condition(m)
            pe.wait_ge(spread_ready, 1)
            pe.matmul(M[:, 0:256], ones[:, :], spread[:, :, :].rearrange("p u s -> p (u s)"),
                      start=True, stop=True).then_inc(idx_psum, 1)

            def values(k, br):
                pe.wait_ge(probs[br], 1)
                for i, (c0, n) in enumerate(spans[br]):
                    last = pe.transpose(M[0:n, i * NR:(i + 1) * NR], pr[br][:, c0:c0 + n], ident[0:NR, 0:NR])
                last.then_inc(pT_psum, 1)
                pe.wait_ge(pT_ready, k + 1)
                for u in range(NP_):
                    b, g = u // NG, u % NG
                    for i, (c0, n) in enumerate(spans[br]):
                        if br == C_:
                            v = cv[0:n, b, i, g * HD:(g + 1) * HD]
                        elif br == W_:
                            v = cw[0:n, b, i, 128 + g * HD:128 + (g + 1) * HD]
                        else:
                            v = vs[0:n, u, i, :]
                        last = pe.matmul(O[:, br, u * QG:(u + 1) * QG], v, pT[0:n, i, u * QG:(u + 1) * QG],
                                         start=(i == 0), stop=(i == len(spans[br]) - 1))
                last.then_inc(o_psum, 1)

            pe.wait_ge(idx_ready, 1)
            pe.wait_ge(cv_in, 32)
            values(0, C_)
            values(1, W_)
            for u in range(NP_):
                pe.wait_ge(kv_in[u % NKV], 128 * (u // NKV + 1))
                key_unit(pe, NP_ + u, sel_src(u), 8, NS)
                if u:
                    score_unit(NP_ + u - 1, SS, NS)
                if u in mod_after:
                    condition(MOD1 + mod_after.index(u))
            score_unit(2 * NP_ - 1, SS, NS)
            pe.wait_ge(v_kept, NP_)
            values(2, S_)
            pe.wait_ge(oT_ready, 1)
            for br in range(3):
                last = pe.transpose(M[0:NR, br * HD:(br + 1) * HD], oT[:, br, :], ident[0:HD, 0:HD])
            last.then_inc(back_psum, 1)

        @block.scalar
        def _(act):
            def copy_keys(u, c0, w):
                act.wait_ge(keys_full, 2 * u + 2)
                if u >= 2:
                    act.wait_ge(keys_read, u - 1)
                act.activation(kT[u % 2][:, c0:c0 + w], A[1][:, :, :].rearrange("p t n -> p (t n)")[:, 0:w],
                               ACT.Copy).then_inc(keys_a, 1)

            def exps(br, parts):
                act.wait_ge(neg_ready[br], 1)
                st = stat[:, br, :]
                c = 0
                for j, (src, w) in enumerate(parts):
                    last = act.activation(pr[br][:, c:c + w], src[:, 0:w], ACT.Exp, bias=st[:, 2:3],
                                          accum_out=st[:, 4 + j:5 + j])
                    c += w
                if br != C_:
                    last = act.activation(st[:, 3:4], st[:, 0:1], ACT.Exp, bias=st[:, 2:3])
                last.then_inc(probs[br], 1)

            for u in range(NP_):
                copy_keys(u, 256, 256)
                if u == 1:
                    exps(C_, [(SC, NCMP)])
            exps(W_, [(SW, NW)])

            def keep_mod(m):
                act.wait_ge(mod_psum, m + 1)
                if m >= 2:
                    act.wait_ge(mod_out[m % 2], 16 * (m // 2))
                act.activation(mrow[m % 2][:, :], (SC, SW)[m % 2][0:9, :], ACT.Copy).then_inc(mod_ready, 1)
                act.wait_ge(mod_ready, m + 1)
                act.dma_start(a["s_mod"][:, (ADA1 + m) * 512:(ADA1 + m + 1) * 512], mrow[m % 2][:, :]
                              ).then_inc(mod_out[m % 2], 16)

            for m in range(MOD1):
                keep_mod(m)
            for u in range(NP_):
                for t0, n, k in ((0, P, 7), (7, 64, 1)):
                    if t0 == 0:
                        act.wait_ge(kv_in[u % NKV], 128 * (u // NKV + 1))
                    last = act.activation(vs[0:n, u, t0:t0 + k, :],
                                          kv[u % NKV][0:n, t0:t0 + k, 128 + (u % NG) * HD:128 + (u % NG + 1) * HD], ACT.Copy)
                last.then_inc(v_kept, 1)
                copy_keys(NP_ + u, 512, NS - 512)
                if u in mod_after:
                    keep_mod(MOD1 + mod_after.index(u))
            exps(S_, [(SS[0], 512), (SS[1], NS - 512)])

        @block.vector
        def _(dve):
            step = Chain(dve, vch)
            dve.memset(ones9[:, :], 1.0).then_inc(ones_set, 1)
            step(dve.memset(qblk[:, :], 0.0))
            step(dve.memset(imp[:, :], 0.0))
            step(dve.memset(stat[:, :, :], 0.0))
            dve.wait_ge(q_turned, 1)
            dve.tensor_copy(qblk[:, :].rearrange("p (u w) -> p u w", w=NR + QG)[:, :, 0:QG],
                            M[0:HD, 0:NR].rearrange("p (u w) -> p u w", w=QG)).then_inc(qblk_ready, 1)
            for br, k in ((S_, 0), (W_, 1)):
                step(dve.tensor_tensor(prod[:, :], q[:, :], new[:, k, 0, :], ALU.mult))
                step(dve.tensor_reduce(stat[:, br, 0:1], prod[:, :], AX, ALU.add))

            def peak(br, parts):
                st = stat[:, br, :]
                c = 1
                for src, w in parts:
                    step(dve.tensor_reduce(st[:, c:c + 1], src[:, 0:w], AX, ALU.max))
                    c += 1
                if len(parts) == 2:
                    step(dve.tensor_tensor(st[:, 1:2], st[:, 1:2], st[:, 2:3], ALU.max))
                if br != C_:
                    step(dve.tensor_tensor(st[:, 1:2], st[:, 1:2], st[:, 0:1], ALU.max))
                dve.tensor_scalar(st[:, 2:3], st[:, 1:2], -1.0, None, ALU.mult).then_inc(neg_ready[br], 1)

            def copy_keys(u):
                dve.wait_ge(keys_full, 2 * u + 1)
                if u >= 2:
                    dve.wait_ge(keys_read, u - 1)
                w = 256 if u < NP_ else 512
                dve.tensor_copy(kT[u % 2][:, 0:w], A[0][:, :, :].rearrange("p t n -> p (t n)")[:, 0:w]).then_inc(keys_v, 1)

            dve.wait_ge(c_read, NB)
            peak(C_, [(SC, NCMP)])
            for u in range(NP_):
                copy_keys(u)
            dve.wait_ge(keys_read, NP_)
            peak(W_, [(SW, NW)])
            dve.wait_ge(probs[C_], 1)
            step(dve.reciprocal(stat[:, C_, 6:7], stat[:, C_, 4:5]))
            dve.tensor_scalar(pn[:, :], pr[C_][:, :], stat[:, C_, 6:7], None, ALU.mult).then_inc(pn_ready, 1)
            dve.wait_ge(imp_psum, 1)
            step(dve.tensor_copy(imp[:, 1:1 + NCMP], M[0:NP_, 0:NCMP]))
            quads = imp[:, :].rearrange("p (n r) -> p n r", r=4)
            step(dve.tensor_reduce(sc[:, :], quads[:, 0:65, :], AX, ALU.add))
            step(dve.tensor_tensor(sc[:, :], sc[:, :], quads[:, 1:66, 0], ALU.add))
            for j in (0, 63):
                step(dve.memset(sc[:, j:j + 1], 1e4))
            s_i = sc[:, 0:NSEL].rearrange("p (o n) -> p o n", o=1).to_broadcast([NP_, NSEL, NSEL])
            s_j = sc[:, 0:NSEL].rearrange("p (n o) -> p n o", o=1).to_broadcast([NP_, NSEL, NSEL])
            step(dve.tensor_tensor(big1[:, :, :], s_i, s_j, ALU.is_equal))
            step(dve.tensor_tensor(big1[:, :, :], big1[:, :, :], tri[:, :, :], ALU.mult))
            step(dve.tensor_tensor(big2[:, :, :], s_i, s_j, ALU.is_gt))
            step(dve.tensor_tensor(big1[:, :, :], big1[:, :, :], big2[:, :, :], ALU.add))
            step(dve.tensor_reduce(rank[:, :], big1[:, :, :], AX, ALU.add))
            for k in range(2):
                step(dve.tensor_scalar(base[:, :, k], ptr[:, :], 128.0, half64[:, k:k + 1], ALU.mult, ALU.add))
            r_j = rank[:, :].rearrange("p (o n) -> p o n", o=1).to_broadcast([NP_, 16, NSEL])
            slot = slots[:, :].rearrange("p (n o) -> p n o", o=1).to_broadcast([NP_, 16, NSEL])
            b_j = base[:, :, :].rearrange("p (o n) k -> p o (n k)", o=1).to_broadcast([NP_, 16, NSEL])
            step(dve.tensor_tensor(big1[:, 0:16, :], r_j, slot, ALU.is_equal))
            step(dve.tensor_tensor(big1[:, 0:16, :], big1[:, 0:16, :], b_j, ALU.mult))
            step(dve.tensor_reduce(slotb[:, :], big1[:, 0:16, :], AX, ALU.add))
            diag = ident[0:NP_, 0:NP_].rearrange("p (u o) -> p u o", o=1).to_broadcast([NP_, NP_, 16])
            sb_u = slotb[:, :].rearrange("p (o s) -> p o s", o=1).to_broadcast([NP_, NP_, 16])
            dve.tensor_tensor(spread[:, :, :], sb_u, diag, ALU.mult).then_inc(spread_ready, 1)
            dve.wait_ge(idx_psum, 1)
            m = M[:, 0:256].rearrange("p (u t k) -> p u t k", u=NP_, k=2)
            for k in range(2):
                r = slice(64 * k, 64 * k + 64)
                step(dve.tensor_scalar(idxf[r, :, :], m[r, :, :, k], p64[r, 0:1], None, ALU.add))
            dve.tensor_copy(idx[:, :], idxf[:, :, :].rearrange("p u t -> p (u t)")).then_inc(idx_ready, 1)

            def turn_probs(k, br):
                dve.wait_ge(pT_psum, k + 1)
                if k:
                    dve.wait_ge(o_psum, k)
                n = len(spans[br])
                full = n if spans[br][-1][1] == P else n - 1
                last = dve.tensor_copy(pT[:, 0:full, :], M[:, 0:full * NR].rearrange("p (c r) -> p c r", r=NR))
                if full < n:
                    w = spans[br][-1][1]
                    last = dve.tensor_copy(pT[0:w, full, :], M[0:w, full * NR:n * NR])
                last.then_inc(pT_ready, 1)

            turn_probs(0, C_)
            turn_probs(1, W_)
            for u in range(NP_):
                copy_keys(NP_ + u)
            dve.wait_ge(keys_read, 2 * NP_)
            peak(S_, [(SS[0], 512), (SS[1], NS - 512)])
            turn_probs(2, S_)
            for br in range(3):
                st = stat[:, br, :]
                dve.wait_ge(probs[br], 1)
                if br == S_:
                    step(dve.tensor_tensor(st[:, 4:5], st[:, 4:5], st[:, 5:6], ALU.add))
                if br != C_:
                    step(dve.tensor_tensor(st[:, 4:5], st[:, 4:5], st[:, 3:4], ALU.add))
                step(dve.reciprocal(st[:, 5:6], st[:, 4:5]))
                step(dve.tensor_tensor(st[:, 6:7], st[:, 5:6], gate[:, br:br + 1], ALU.mult))
            dve.wait_ge(o_psum, 3)
            dve.tensor_copy(oT[:, :, :], O[:, :, :]).then_inc(oT_ready, 1)
            dve.wait_ge(back_psum, 1)
            step(dve.tensor_copy(o[:, :, :].rearrange("p k d -> p (k d)"), M[0:NR, 0:3 * HD]))
            for br, k in ((S_, 0), (W_, 1)):
                step(dve.scalar_tensor_tensor(out=o[:, br, :], in0=new[:, k, 1, :], scalar=stat[:, br, 3:4],
                                              in1=o[:, br, :], op0=ALU.mult, op1=ALU.add))
            step(dve.tensor_scalar(o[:, C_, :], o[:, C_, :], stat[:, C_, 6:7], None, ALU.mult))
            step(dve.scalar_tensor_tensor(out=o[:, C_, :], in0=o[:, S_, :], scalar=stat[:, S_, 6:7], in1=o[:, C_, :],
                                          op0=ALU.mult, op1=ALU.add))
            dve.scalar_tensor_tensor(out=o[:, C_, :], in0=o[:, W_, :], scalar=stat[:, W_, 6:7], in1=o[:, C_, :],
                                     op0=ALU.mult, op1=ALU.add).then_inc(done, 1)


def stage_merge_route(nc, a):
    NL = NGR + NE
    with Scope(nc, "mrg") as s:
        ident = s.sb("ident", [P, P])
        ones = s.sb("ones", [P, P])
        wo = s.sb("wo", [P, KT, D])
        wr = s.sb("wr", [P, KT, NL])
        br = s.sb("br", [P, NL])
        gcol = s.sb("gcol", [P, 2, CJ])
        mod = s.sb("mod", [P, 3, D])
        mods = s.sb("mods", [NB, 3, D])
        g2 = s.sb("g2", [P, D])
        eps = s.sb("eps", [P, 1])
        cT = s.sb("cT", [P, CJ, T])
        crow = s.sb("crow", [NB, CW])
        cTs = s.sb("cTs", [P, CJ, NB])
        at = [s.sb(f"at{i}", [P, 512]) for i in range(2)]
        aT = [s.sb(f"aT{i}", [P, CJ, P]) for i in range(2)]
        sq = s.sb("sq", [P, CJ, T])
        junk = s.sb("junk", [P, D])
        cstat = s.sb("cstat", [P, 3, TT])
        stat = s.sb("stat", [P, TT, 6])
        xt = [s.sb(f"xt{i}", [P, D]) for i in range(2)]
        yc = s.sb("yc", [P, D])
        x2 = [s.sb(f"x2{i}", [P, D]) for i in range(2)]
        h2 = [s.sb(f"h2{i}", [P, D]) for i in range(2)]
        hT = s.sb("hT", [P, KT, P])
        L = s.sb("L", [P, TT, NL])
        zrow = s.sb("zrow", [1, D])
        Pc = [s.ps(f"Pc{i}", [P, 512]) for i in range(2)]
        Pa = [s.ps(f"Pa{i}", [P, 512]) for i in range(2)]
        TA = s.ps("TA", [P, CJ, P])
        TH = [s.ps(f"TH{i}", [P, 4, P]) for i in range(2)]
        M = s.ps("M", [P, 512])

        const_in = s.sem("const_in")
        wo_in = [s.sem(f"wo_in{i}") for i in range(2)]
        tok_in = [s.sem(f"tok_in{i}") for i in range(2)]
        vset = s.sem("vset")
        conv_in = s.sem("conv_in")
        gain_in = s.sem("gain_in")
        row_in = s.sem("row_in")
        sq_ready = s.sem("sq_ready")
        sq_sum = s.sem("sq_sum")
        row_summed = s.sem("row_summed")
        conv_roots = s.sem("conv_roots")
        conv_inv = s.sem("conv_inv")
        roots = s.sem("roots")
        root2 = s.sem("root2")
        turned = s.sem("turned")
        aT_ready = s.sem("aT_ready")
        cT_ready = s.sem("cT_ready")
        product = s.sem("product")
        rinv = s.sem("rinv")
        yc_ready = s.sem("yc_ready")
        x2_ready = s.sem("x2_ready")
        y_read = s.sem("y_read")
        h2_ready = s.sem("h2_ready")
        h2_turned = s.sem("h2_turned")
        hT_v = s.sem("hT_v")
        hT_a = s.sem("hT_a")
        logits = s.sem("logits")
        logits_read = s.sem("logits_read")
        ach = s.sem("ach")
        vch = s.sem("vch")
        x2_out = [s.sem(f"x2_out{i}") for i in range(2)]
        z_out = s.sem("z_out")
        block = s.block()
        NCONST = 11

        @block.sync
        def _(sp):
            def load_tok(t):
                n = rows_of(t)
                src = a["x_prompt"][0, t * P:t * P + n, :] if t < NT else a["x_sample"][:, 0, :]
                sp.dma_start(at[t % 2][0:n, :], a["s_attn"][t * P:t * P + n, :]).then_inc(tok_in[t % 2], 16)
                sp.dma_start(xt[t % 2][0:n, :], src).then_inc(tok_in[t % 2], 16)

            sp.dma_start(crow[:, :], a["s_convs"]).then_inc(row_in, 16)
            sp.dma_start(ident[:, :], a["c_ident"]).then_inc(row_in, 16)
            sp.dma_start(ones[:, :], a["c_ones"]).then_inc(row_in, 16)
            for j in range(CJ):
                sp.dma_start(cT[:, j, :], a["s_convT"][j]).then_inc(conv_in, 16)
                if j == 0:
                    with nc.allow_non_contiguous_dma(reason="gains by channel"):
                        sp.dma_start(gcol[:, 0, :], a["g_out_conv"][0].rearrange("(j p) -> p j", p=P)).then_inc(gain_in, 16)
                        sp.dma_start(gcol[:, 1, :], a["g_out_attn"][0].rearrange("(j p) -> p j", p=P)).then_inc(gain_in, 16)
            load_tok(0)
            for half in range(2):
                sp.dma_start(wo[:, half * CJ:(half + 1) * CJ, :],
                             a["w_out"][0, half * CW:(half + 1) * CW].rearrange("(k p) n -> p k n", p=P)).then_inc(wo_in[half], 16)
            for j, seg in enumerate((2, 4, 3)):
                sp.dma_start(mod[:, j, :], a["s_mod"][NB:NB + 1, seg * D:(seg + 1) * D].to_broadcast([P, D])).then_inc(const_in, 16)
                sp.dma_start(mods[:, j, :], a["s_mod"][0:NB, seg * D:(seg + 1) * D]).then_inc(const_in, 16)
            sp.dma_start(g2[:, :], a["ln2_g"].to_broadcast([P, D])).then_inc(const_in, 16)
            sp.dma_start(wr[:, :, 0:NGR], a["w_route_group"][0].rearrange("(k p) n -> p k n", p=P)).then_inc(const_in, 16)
            sp.dma_start(wr[:, :, NGR:NL], a["w_route_expert"][0].rearrange("(k p) n -> p k n", p=P)).then_inc(const_in, 16)
            sp.dma_start(br[:, 0:NGR], a["b_route_group"].to_broadcast([P, NGR])).then_inc(const_in, 16)
            sp.dma_start(br[:, NGR:NL], a["b_route_expert"].to_broadcast([P, NE])).then_inc(const_in, 16)
            load_tok(1)
            for t in range(TT):
                n = rows_of(t)
                sp.wait_ge(h2_ready, t + 1)
                sp.dma_start(a["s_x2"][t * P:t * P + n, :], x2[t % 2][0:n, :]).then_inc(x2_out[t % 2], 16)
                sp.dma_start(a["s_h2"][t * P:t * P + n, :], h2[t % 2][0:n, :]).then_inc(x2_out[t % 2], 16)
                if t + 2 < TT:
                    sp.wait_ge(turned, t + 1)
                    load_tok(t + 2)
            sp.wait_ge(vset, 2)
            sp.dma_start(a["s_h2"][ZROW:ZROW + 1, :], zrow[:, :]).then_inc(z_out, 16)
            sp.wait_ge(logits_read, TT)
            sp.dma_start(a["s_logit"], L[:, :, :].rearrange("p t n -> p (t n)")).then_inc(z_out, 16)
            sp.wait_ge(z_out, 32)
            sp.wait_ge(x2_out[0], 32 * ((TT + 1) // 2))
            sp.wait_ge(x2_out[1], 32 * (TT // 2))

        @block.scalar
        def _(act):
            step = Chain(act, ach)

            def pre(t):
                n = rows_of(t)
                st = stat[:, t, :]
                act.wait_ge(tok_in[t % 2], 32 * (t // 2 + 1))
                step(act.activation(junk[0:n, 0:512], at[t % 2][0:n, :], ACT.Square, accum_out=st[0:n, 0:1]))
                act.activation(st[0:n, 1:2], st[0:n, 0:1], ACT.Sqrt, bias=eps[0:n, :], scale=1.0 / CW).then_inc(roots, 1)

            act.wait_ge(vset, 1)
            act.wait_ge(row_in, 48)
            act.activation(junk[0:NB, 0:512], crow[:, :], ACT.Square, accum_out=cstat[0:NB, 0, NT:TT]).then_inc(row_summed, 1)
            act.wait_ge(conv_in, 16 * CJ)
            for h in range(2):
                part = slice(h * T // 2, (h + 1) * T // 2)
                act.activation(sq[:, :, part], cT[:, :, part], ACT.Square).then_inc(sq_ready, 1)
            act.wait_ge(row_summed, 1)
            pre(0)
            act.wait_ge(sq_sum, 1)
            act.activation(cstat[:, 1, 0:NT], M[:, 0:NT], ACT.Sqrt, bias=eps[:, :], scale=1.0 / CW).then_inc(conv_roots, 1)
            act.activation(cstat[0:NB, 1, NT:TT], cstat[0:NB, 0, NT:TT], ACT.Sqrt, bias=eps[0:NB, :], scale=1.0 / CW
                           ).then_inc(conv_roots, 1)
            act.wait_ge(conv_inv, 2)
            for t in range(TT):
                n = rows_of(t)
                st = stat[:, t, :]
                act.wait_ge(product, t + 1)
                if t:
                    act.wait_ge(y_read, t)
                for c in range(2):
                    last = act.activation(yc[0:n, c * 512:(c + 1) * 512], Pc[c][0:n, :], ACT.Copy, scale=cstat[0:n, 2, t:t + 1])
                last.then_inc(yc_ready, 1)
                if t + 1 < TT:
                    pre(t + 1)
                act.wait_ge(x2_ready, t + 1)
                step(act.activation(junk[0:n, :], x2[t % 2][0:n, :], ACT.Square, accum_out=st[0:n, 3:4]))
                act.activation(st[0:n, 4:5], st[0:n, 3:4], ACT.Sqrt, bias=eps[0:n, :], scale=1.0 / D).then_inc(root2, 1)
                act.wait_ge(h2_turned, t + 1)
                if t:
                    act.wait_ge(logits, t)
                act.activation(hT[:, 4:8, 0:n], TH[1][:, :, 0:n], ACT.Copy).then_inc(hT_a, 1)

        @block.tensor
        def _(pe):
            def turn_h2(t):
                n = rows_of(t)
                pe.wait_ge(h2_ready, t + 1)
                if t:
                    pe.wait_ge(hT_v, t)
                    pe.wait_ge(hT_a, t)
                for k in range(KT):
                    last = pe.transpose(TH[k // 4][:, k % 4, 0:n], h2[t % 2][0:n, k * P:(k + 1) * P], ident[0:n, 0:n])
                last.then_inc(h2_turned, 1)

            def route(t):
                n = rows_of(t)
                pe.wait_ge(hT_v, t + 1)
                pe.wait_ge(hT_a, t + 1)
                if t:
                    pe.wait_ge(logits_read, t)
                for k in range(KT):
                    last = pe.matmul(M[0:n, 64:64 + NL], hT[:, k, 0:n], wr[:, k, :], start=(k == 0), stop=(k == KT - 1))
                last.then_inc(logits, 1)

            def turn_attn(t):
                n = rows_of(t)
                pe.wait_ge(tok_in[t % 2], 32 * (t // 2 + 1))
                pe.wait_ge(aT_ready, t + 1)
                for j in range(CJ):
                    last = pe.transpose(TA[:, j, 0:n], at[t % 2][0:n, j * P:(j + 1) * P], ident[0:n, 0:n])
                last.then_inc(turned, 1)

            pe.wait_ge(row_in, 48)
            for j in range(CJ):
                last = pe.transpose(TA[:, j, 0:NB], crow[:, j * P:(j + 1) * P], ident[0:NB, 0:NB])
            last.then_inc(turned, 1)
            for t in range(NT):
                if t % (NT // 2) == 0:
                    pe.wait_ge(sq_ready, t // (NT // 2) + 1)
                for j in range(CJ):
                    last = pe.matmul(M[:, t:t + 1], sq[:, j, t * P:(t + 1) * P], ones[:, 0:1], start=(j == 0), stop=(j == CJ - 1))
            last.then_inc(sq_sum, 1)
            turn_attn(0)
            for t in range(TT):
                n = rows_of(t)
                if t == 0:
                    pe.wait_ge(cT_ready, 1)
                    pe.wait_ge(wo_in[0], 16)
                else:
                    pe.wait_ge(yc_ready, t)
                for j in range(CJ):
                    for c in range(2):
                        lhs = cT[:, j, t * P:(t + 1) * P] if t < NT else cTs[:, j, :]
                        pe.matmul(Pc[c][0:n, :], lhs, wo[:, j, c * 512:(c + 1) * 512], start=(j == 0), stop=(j == CJ - 1))
                pe.wait_ge(aT_ready, t + 2)
                if t:
                    pe.wait_ge(y_read, t)
                else:
                    pe.wait_ge(wo_in[1], 16)
                for j in range(CJ):
                    for c in range(2):
                        last = pe.matmul(Pa[c][0:n, :], aT[t % 2][:, j, 0:n], wo[:, CJ + j, c * 512:(c + 1) * 512],
                                         start=(j == 0), stop=(j == CJ - 1))
                last.then_inc(product, 1)
                if t == 0:
                    pe.wait_ge(const_in, 16 * NCONST)
                    pe.wait_ge(conv_roots, 1)
                if t:
                    turn_h2(t - 1)
                if t + 1 < TT:
                    turn_attn(t + 1)
                if t:
                    route(t - 1)
            turn_h2(TT - 1)
            route(TT - 1)

        @block.vector
        def _(dve):
            step = Chain(dve, vch)
            dve.memset(eps[:, :], EPS).then_inc(vset, 1)
            dve.memset(zrow[:, :], 0.0).then_inc(vset, 1)
            step(dve.memset(L[:, :, :], 0.0))
            dve.wait_ge(gain_in, 32)
            dve.wait_ge(turned, 1)
            for j in range(CJ):
                last = dve.tensor_scalar(cTs[:, j, :], TA[:, j, 0:NB], gcol[:, 0, j:j + 1], None, ALU.mult)
            last.then_inc(aT_ready, 1)

            def scale_in(t):
                n = rows_of(t)
                dve.wait_ge(turned, t + 2)
                if t >= 2:
                    dve.wait_ge(product, t - 1)
                for j in range(CJ):
                    last = dve.tensor_scalar(aT[t % 2][:, j, 0:n], TA[:, j, 0:n], gcol[:, 1, j:j + 1], None, ALU.mult)
                last.then_inc(aT_ready, 1)
                dve.wait_ge(roots, t + 1)
                dve.reciprocal(stat[0:n, t, 2:3], stat[0:n, t, 1:2]).then_inc(rinv, 1)

            dve.wait_ge(sq_ready, 2)
            for j in range(CJ):
                last = dve.tensor_scalar(cT[:, j, :], cT[:, j, :], gcol[:, 0, j:j + 1], None, ALU.mult)
            last.then_inc(cT_ready, 1)
            dve.wait_ge(conv_roots, 2)
            dve.reciprocal(cstat[:, 2, 0:NT], cstat[:, 1, 0:NT]).then_inc(conv_inv, 1)
            dve.reciprocal(cstat[0:NB, 2, NT:TT], cstat[0:NB, 1, NT:TT]).then_inc(conv_inv, 1)
            def logits_in(t):
                n = rows_of(t)
                dve.wait_ge(h2_turned, t + 1)
                dve.tensor_copy(hT[:, 0:4, 0:n], TH[0][:, :, 0:n]).then_inc(hT_v, 1)
                dve.wait_ge(logits, t + 1)
                dve.tensor_tensor(L[0:n, t, :], M[0:n, 64:64 + NL], br[0:n, :], ALU.add).then_inc(logits_read, 1)

            scale_in(0)
            dve.wait_ge(const_in, 16 * NCONST)
            for part, n in ((mod, P), (mods, NB)):
                step(dve.scalar_tensor_tensor(out=part[:, 1, :], in0=part[:, 1, :], scalar=1.0, in1=g2[0:n, :],
                                              op0=ALU.add, op1=ALU.mult))
            for t in range(TT):
                n = rows_of(t)
                m = mod if t < NT else mods
                if t:
                    logits_in(t - 1)
                xo, ho = x2[t % 2][0:n, :], h2[t % 2][0:n, :]
                if t >= 2:
                    dve.wait_ge(x2_out[t % 2], 32 * (t // 2))
                dve.wait_ge(rinv, t + 1)
                dve.wait_ge(yc_ready, t + 1)
                for c in range(2):
                    cs = slice(c * 512, (c + 1) * 512)
                    last = dve.scalar_tensor_tensor(out=x2[t % 2][0:n, cs], in0=Pa[c][0:n, :], scalar=stat[0:n, t, 2:3],
                                                    in1=yc[0:n, cs], op0=ALU.mult, op1=ALU.add)
                last.then_inc(y_read, 1)
                dve.wait_ge(y_read, t + 1)
                step(dve.tensor_tensor(xo, xo, m[0:n, 0, :], ALU.mult))
                dve.tensor_tensor(xo, xo, xt[t % 2][0:n, :], ALU.add).then_inc(x2_ready, 1)
                if t + 1 < TT:
                    scale_in(t + 1)
                dve.wait_ge(root2, t + 1)
                step(dve.reciprocal(stat[0:n, t, 5:6], stat[0:n, t, 4:5]))
                step(dve.scalar_tensor_tensor(out=ho, in0=xo, scalar=stat[0:n, t, 5:6], in1=m[0:n, 1, :],
                                              op0=ALU.mult, op1=ALU.mult))
                dve.tensor_tensor(ho, ho, m[0:n, 2, :], ALU.add).then_inc(h2_ready, 1)
            logits_in(TT - 1)


class ExpertWeights:

    def __init__(self, s, a):
        self.a = a
        self.wg = [s.sb(f"wg{i}", [P, KT, DE]) for i in range(2)]
        self.wu = [s.sb(f"wu{i}", [P, KT, DE]) for i in range(2)]
        self.wd = [s.sb(f"wd{i}", [P, DE // P, D]) for i in range(2)]
        self.gu_in = [s.sem(f"gu_in{i}") for i in range(2)]
        self.d_in = [s.sem(f"d_in{i}") for i in range(2)]

    def load_gu(self, sp, k, e):
        for dst, src in ((self.wg, "w_gate"), (self.wu, "w_up")):
            sp.dma_start(dst[k][:, :, :].rearrange("p k n -> p (k n)"),
                         self.a[src][0, bass.ds(e, 1)].rearrange("o (p k) n -> (o p) (k n)", p=P)
                         ).then_inc(self.gu_in[k], 16)

    def load_d(self, sp, k, e):
        sp.dma_start(self.wd[k][:, :, :].rearrange("p k n -> p (k n)"),
                     self.a["w_down"][0, bass.ds(e, 1)].rearrange("o (p k) n -> (o p) (k n)", p=P)
                     ).then_inc(self.d_in[k], 16)


def stage_slots(nc, a, weights):
    NL = NGR + NE
    with Scope(nc, "slt") as s:
        L = s.sb("L", [P, TT, NL])
        ones = s.sb("ones", [P, P])
        tri = s.sb("tri", [P, P])
        iota = s.sb("iota", [P, NE])
        kk = s.sb("kk", [P, 8])
        real = s.sb("real", [P, TT])
        tok = s.sb("tok", [P, TT], U32)
        empty = s.sb("empty", [P, NBLK], U32)
        gm = s.sb("gm", [P, TT, 1])
        dl = s.sb("dl", [P, TT, NGR])
        ex = s.sb("ex", [P, TT, NGR])
        pg = s.sb("pg", [P, TT, 1])
        key = s.sb("key", [P, TT, EPG])
        ohg = s.sb("ohg", [P, TT, NGR])
        sel = s.sb("sel", [P, TT, EPG, NGR])
        le = s.sb("le", [P, TT, EPG])
        m = s.sb("m", [P, 2, TT, 1])
        oh = s.sb("oh", [P, 2, TT, EPG])
        e21 = s.sb("e21", [P, TT, 1])
        den = s.sb("den", [P, TT, 1])
        oh32 = s.sb("oh32", [P, 2, TT, NGR, EPG])
        both = s.sb("both", [P, TT, NE])
        pos = s.sb("pos", [P, TT + 1, NE])
        over = s.sb("over", [P, NE, 8])
        extra = s.sb("extra", [P, NE])
        cum = [s.sb(f"cum{i}", [P, NE]) for i in range(2)]
        first = s.sb("first", [P, NE])
        shift = s.sb("shift", [P, NE])
        dest = s.sb("dest", [P, TT, NE])
        tmp = s.sb("tmp", [P, TT, NE])
        own = s.sb("own", [P, NOV, NE])
        own2 = s.sb("own2", [P, NOV, NE])
        route = s.sb("route", [P, 4, TT])
        slot = s.sb("slot", [P, 2, TT], U32)
        ov = s.sb("ov", [P, NOV + 1])
        ovi = s.sb("ovi", [P, NOV + 1], I32)
        M = s.ps("M", [P, TT + 1, NE])

        const_in = s.sem("const_in")
        ch = s.sem("ch")
        exp_in = s.sem("exp_in")
        exp_out = s.sem("exp_out")
        both_ready = s.sem("both_ready")
        counted = s.sem("counted")
        slots_ready = s.sem("slots_ready")
        empty_set = s.sem("empty_set")
        cleared = s.sem("cleared")
        filled = s.sem("filled")
        tables = s.sem("tables")
        out_done = s.sem("out_done")
        block = s.block()

        @block.sync
        def _(sp):
            sp.dma_start(L[:, :, :].rearrange("p t n -> p (t n)"), a["s_logit"]).then_inc(const_in, 16)
            sp.dma_start(ones[:, :], a["c_ones"]).then_inc(const_in, 16)
            sp.dma_start(tri[:, :], a["c_tri"]).then_inc(const_in, 16)
            sp.dma_start(iota[:, :], a["c_iota"][:, 0:NE].to_broadcast([P, NE])).then_inc(const_in, 16)
            sp.dma_start(kk[:, :], a["c_blocks"].to_broadcast([P, 8])).then_inc(const_in, 16)
            sp.dma_start(real[:, :], a["c_real"]).then_inc(const_in, 16)
            sp.dma_start(tok[:, :], a["c_tok"]).then_inc(const_in, 16)
            for k in range(2):
                weights.load_gu(sp, k, k)
                weights.load_d(sp, k, k)
            sp.wait_ge(tables, 1)
            sp.dma_start(a["s_route"], route[:, :, :].rearrange("p k t -> p (k t)")).then_inc(out_done, 16)
            sp.dma_start(a["s_ov"], ovi[0:1, :]).then_inc(out_done, 16)
            sp.wait_ge(out_done, 32)

        @block.gpsimd
        def _(pool):
            pool.memset(empty[:, :], ZROW).then_inc(empty_set, 1)
            pool.wait_ge(empty_set, 1)
            pool.dma_start(a["s_slot"].rearrange("(p k) o -> p (k o)", p=P), empty[:, :]).then_inc(cleared, 16)
            pool.wait_ge(cleared, 16)
            pool.wait_ge(const_in, 16 * 7)
            pool.wait_ge(slots_ready, 1)
            for t in range(TT):
                n = rows_of(t)
                for k in range(2):
                    pool.indirect_dma_start(a["s_slot"], bass.IndirectOffsetOnAxis(ap=slot[0:n, k, t:t + 1], axis=0),
                                            tok[0:n, t:t + 1], None).then_inc(filled, 16)
            pool.wait_ge(filled, 16 * 2 * TT)

        @block.scalar
        def _(act):
            act.wait_ge(exp_in, 1)
            act.activation(ex[:, :, :], dl[:, :, :], ACT.Exp).then_inc(exp_out, 1)
            act.wait_ge(exp_in, 2)
            act.activation(e21[:, :, :], den[:, :, :], ACT.Exp).then_inc(exp_out, 1)

        @block.tensor
        def _(pe):
            pe.wait_ge(const_in, 16 * 7)
            pe.wait_ge(both_ready, 1)
            for t in range(TT + 1):
                for u in range(t):
                    last = pe.matmul(M[:, t, :], ones[:, :], both[:, u, :], start=(u == 0),
                                     stop=(t == TT and u == TT - 1))
                if t < TT:
                    last = pe.matmul(M[:, t, :], tri[:, :], both[:, t, :], start=(t == 0), stop=True)
            last.then_inc(counted, 1)

        @block.vector
        def _(dve):
            step = Chain(dve, ch)
            TTc = dve.tensor_tensor
            dve.wait_ge(const_in, 16 * 7)
            lg = L[:, :, 0:NGR]

            def wide(x, shape):
                return x.to_broadcast(shape)

            def first_max(vals, width, top, onehot):
                io = iota[:, 0:width].rearrange("p (o n) -> p o n", o=1).to_broadcast([P, TT, width])
                k = key[:, :, 0:width]
                step(dve.tensor_reduce(top, vals, AX, ALU.max))
                step(TTc(k, vals, wide(top, [P, TT, width]), ALU.is_equal))
                step(dve.scalar_tensor_tensor(out=k, in0=k, scalar=-1000.0, in1=io, op0=ALU.mult, op1=ALU.add))
                step(dve.tensor_reduce(den[:, :, :], k, AX, ALU.min))
                step(TTc(onehot, k, wide(den[:, :, :], [P, TT, width]), ALU.is_equal))

            first_max(lg, NGR, gm[:, :, :], ohg[:, :, :])
            TTc(dl[:, :, :], lg, wide(gm[:, :, :], [P, TT, NGR]), ALU.subtract).then_inc(exp_in, 1)
            step(TTc(sel[:, :, :, :], L[:, :, NGR:NL].rearrange("p t (g e) -> p t e g", g=NGR),
                     ohg[:, :, :].rearrange("p t (o g) -> p t o g", o=1).to_broadcast([P, TT, EPG, NGR]), ALU.mult))
            step(dve.tensor_reduce(le[:, :, :], sel[:, :, :, :], AX, ALU.add))
            first_max(le[:, :, :], EPG, m[:, 0], oh[:, 0])
            step(dve.scalar_tensor_tensor(out=le[:, :, :], in0=oh[:, 0], scalar=-3e38, in1=le[:, :, :], op0=ALU.mult, op1=ALU.add))
            first_max(le[:, :, :], EPG, m[:, 1], oh[:, 1])
            TTc(den[:, :, :], m[:, 1], m[:, 0], ALU.subtract).then_inc(exp_in, 1)
            dve.wait_ge(exp_out, 2)
            step(dve.tensor_reduce(pg[:, :, :], ex[:, :, :], AX, ALU.add))
            step(dve.tensor_scalar(den[:, :, :], e21[:, :, :], 1.0, None, ALU.add))
            step(TTc(pg[:, :, :], pg[:, :, :], den[:, :, :], ALU.mult))
            w1, w2 = (route[:, 2 + k, :].rearrange("p (t o) -> p t o", o=1) for k in range(2))
            step(dve.reciprocal(w1, pg[:, :, :]))
            step(TTc(w2, w1, e21[:, :, :], ALU.mult))
            for k in range(2):
                for g in range(NGR):
                    step(TTc(oh32[:, k, :, g, :], oh[:, k], ohg[:, :, g:g + 1].to_broadcast([P, TT, EPG]), ALU.mult))
            o32 = [oh32[:, k, :, :, :].rearrange("p t g e -> p t (g e)") for k in range(2)]
            step(TTc(both[:, :, :], o32[0], o32[1], ALU.add))
            TTc(both[:, :, :], both[:, :, :], real[:, :].rearrange("p (t o) -> p t o", o=1).to_broadcast([P, TT, NE]),
                ALU.mult).then_inc(both_ready, 1)
            dve.wait_ge(counted, 1)
            step(dve.tensor_copy(pos[:, :, :], M[:, :, :]))
            step(TTc(over[:, :, :], pos[:, TT, :].rearrange("p (e o) -> p e o", o=1).to_broadcast([P, NE, 8]),
                     kk[:, :].rearrange("p (o k) -> p o k", o=1).to_broadcast([P, NE, 8]), ALU.is_gt))
            step(dve.tensor_reduce(extra[:, :], over[:, :, :], AX, ALU.add))
            src = extra
            for i, sh in enumerate((1, 2, 4, 8, 16)):
                dst = cum[i % 2]
                step(dve.tensor_copy(dst[:, 0:sh], src[:, 0:sh]))
                step(TTc(dst[:, sh:NE], src[:, sh:NE], src[:, 0:NE - sh], ALU.add))
                src = dst
            step(TTc(first[:, :], src[:, :], extra[:, :], ALU.subtract))
            step(TTc(shift[:, :], first[:, :], iota[:, :], ALU.subtract))
            step(dve.tensor_scalar(shift[:, :], shift[:, :], float(NE - 1), 128.0, ALU.add, ALU.mult))
            sh3 = shift[:, :].rearrange("p (o e) -> p o e", o=1).to_broadcast([P, TT, NE])
            e3 = iota[:, :].rearrange("p (o e) -> p o e", o=1).to_broadcast([P, TT, NE])
            p3 = pos[:, 0:TT, :]
            step(dve.tensor_scalar(tmp[:, :, :], p3, 128.0, None, ALU.is_ge))
            step(TTc(tmp[:, :, :], tmp[:, :, :], sh3, ALU.mult))
            step(TTc(tmp[:, :, :], tmp[:, :, :], p3, ALU.add))
            step(dve.scalar_tensor_tensor(out=dest[:, :, :], in0=e3, scalar=128.0, in1=tmp[:, :, :], op0=ALU.mult, op1=ALU.add))
            for k in range(2):
                step(TTc(tmp[:, :, :], dest[:, :, :], o32[k], ALU.mult))
                step(dve.tensor_reduce(route[:, k, :], tmp[:, :, :], AX, ALU.add))
            dve.tensor_copy(slot[:, :, :], route[:, 0:2, :]).then_inc(slots_ready, 1)
            j3 = iota[:, 0:NOV].rearrange("p (n o) -> p n o", o=1).to_broadcast([P, NOV, NE])
            def row(x):
                return x[:, :].rearrange("p (o e) -> p o e", o=1).to_broadcast([P, NOV, NE])
            step(TTc(own[:, :, :], j3, row(first), ALU.is_ge))
            step(TTc(own2[:, :, :], j3, row(src), ALU.is_lt))
            step(TTc(own[:, :, :], own[:, :, :], own2[:, :, :], ALU.mult))
            step(TTc(own[:, :, :], own[:, :, :], row(iota), ALU.mult))
            step(dve.tensor_reduce(ov[:, 0:NOV], own[:, :, :], AX, ALU.add))
            step(dve.tensor_copy(ov[:, NOV:NOV + 1], src[:, NE - 1:NE]))
            dve.tensor_copy(ovi[:, :], ov[:, :]).then_inc(tables, 1)


def stage_experts(nc, a, weights):
    KD = DE // P
    with Scope(nc, "moe") as s:
        ident = s.sb("ident", [P, P])
        idx = s.sb("idx", [P, NBLK], U32)
        ov = s.sb("ov", [1, NOV + 1], I32)
        wg, wu, wd = weights.wg, weights.wu, weights.wd
        gu_in, d_in = weights.gu_in, weights.d_in
        xg = [s.sb(f"xg{i}", [P, D]) for i in range(2)]
        xT = [s.sb(f"xT{i}", [P, KT, P]) for i in range(2)]
        sg = s.sb("sg", [P, DE])
        h = s.sb("h", [P, DE])
        hT = s.sb("hT", [P, KD, P])
        y = [s.sb(f"y{i}", [P, D]) for i in range(2)]
        settled = s.sb("settled", [1, 1])
        XT = [s.ps(f"XT{i}", [P, 4, P]) for i in range(2)]
        G = s.ps("G", [P, DE])
        U = s.ps("U", [P, DE])
        HT = s.ps("HT", [P, KD, P])
        Y = [s.ps(f"Y{i}", [P, 512]) for i in range(2)]

        const_in = s.sem("const_in")
        idx_in = s.sem("idx_in")
        x_in = [s.sem(f"x_in{i}") for i in range(2)]
        x_turned = s.sem("x_turned")
        xT_v = s.sem("xT_v")
        xT_a = s.sem("xT_a")
        g_done = s.sem("g_done")
        u_done = s.sem("u_done")
        silu_done = s.sem("silu_done")
        h_ready = s.sem("h_ready")
        h_turned = s.sem("h_turned")
        hT_ready = s.sem("hT_ready")
        y_done = s.sem("y_done")
        y_a = s.sem("y_a")
        y_v = s.sem("y_v")
        y_out = [s.sem(f"y_out{i}") for i in range(2)]
        block = s.block()

        def overflow(eng, body):
            blocks = eng.value_load(ov[0:1, NOV:NOV + 1], min_val=0, max_val=NOV)
            with eng.Fori(0, NOV // 2) as j:
                for k in range(2):
                    with eng.If(blocks > 2 * j + k):
                        body(2 * j + k, k, NE + 2 * j + k, NE // 2 + j)

        def gate(pe, k, n, i):
            pe.wait_ge(xT_v, n + 1)
            pe.wait_ge(xT_a, n + 1)
            pe.wait_ge(gu_in[k], 32 * i + 32)
            wait(pe, silu_done, n)
            for c in range(KT):
                last = pe.matmul(G[:, :], xT[k][:, c, :], wg[k][:, c, :], start=(c == 0), stop=(c == KT - 1))
            last.then_inc(g_done, 1)

        def up(pe, k, n):
            wait(pe, h_ready, n)
            for c in range(KT):
                last = pe.matmul(U[:, :], xT[k][:, c, :], wu[k][:, c, :], start=(c == 0), stop=(c == KT - 1))
            last.then_inc(u_done, 1)

        def turn_x(pe, k):
            for c in range(KT):
                last = pe.transpose(XT[c // 4][:, c % 4, :], xg[k][:, c:D:KT], ident[:, :])
            last.then_inc(x_turned, 1)

        def turn_h(pe, n):
            pe.wait_ge(h_ready, n + 1)
            wait(pe, hT_ready, n)
            for c in range(KD):
                last = pe.transpose(HT[:, c, :], h[:, c:DE:KD], ident[:, :])
            last.then_inc(h_turned, 1)

        def down(pe, k, n, loads):
            pe.wait_ge(hT_ready, n + 1)
            pe.wait_ge(d_in[k], 16 * loads)
            wait(pe, y_a, n)
            wait(pe, y_v, n)
            for half in range(2):
                for c in range(KD):
                    last = pe.matmul(Y[half][:, :], hT[:, c, :], wd[k][:, c, half * 512:(half + 1) * 512],
                                     start=(c == 0), stop=(c == KD - 1))
            last.then_inc(y_done, 1)

        @block.sync
        def _(sp):
            sp.dma_start(ident[:, :], a["c_ident"]).then_inc(const_in, 16)
            sp.dma_start(ov[:, :], a["s_ov"]).then_inc(const_in, 16)
            with nc.allow_non_contiguous_dma(reason="slot table, one block per column"):
                sp.dma_start(idx[:, :], a["s_slot"].rearrange("(n p) o -> p (n o)", p=P)).then_inc(idx_in, 16)

            def next_gu(k, n):
                sp.wait_ge(u_done, n - 1)
                weights.load_gu(sp, k, n)

            next_gu(0, 2)
            with sp.Fori(0, NE // 2 - 2) as i:
                next_gu(1, 2 * i + 3)
                next_gu(0, 2 * i + 4)
            next_gu(1, NE - 1)
            sp.wait_ge(const_in, 32)

            def more(b, k, n, i):
                e = sp.value_load(ov[0:1, bass.ds(b, 1)], min_val=0, max_val=NE - 1)
                sp.wait_ge(u_done, n - 1)
                weights.load_gu(sp, k, e)

            overflow(sp, more)

        @block.gpsimd
        def _(pool):
            def gather(e, k, at):
                pool.indirect_dma_start(xg[k][:, :], None, a["s_h2"],
                                        bass.IndirectOffsetOnAxis(ap=idx[:, at:at + 1], axis=0)).then_inc(x_in[k], 16)

            pool.wait_ge(idx_in, 16)
            for e in range(NE):
                if e >= 2:
                    pool.wait_ge(x_turned, e - 1)
                gather(e, e % 2, e)
            pool.wait_ge(const_in, 32)
            blocks = pool.value_load(ov[0:1, NOV:NOV + 1], min_val=0, max_val=NOV)
            for b in range(NOV):
                with pool.If(blocks > b):
                    pool.wait_ge(x_turned, NE + b - 1)
                    gather(NE + b, b % 2, NE + b)

        @block.tensor
        def _(pe):
            pe.wait_ge(const_in, 32)
            pe.wait_ge(x_in[0], 16)
            turn_x(pe, 0)

            def expert(i, k, before=True, following=True):
                n = 2 * i + k
                gate(pe, k, n, i)
                if before:
                    turn_h(pe, n - 1)
                if following:
                    pe.wait_ge(x_in[1 - k], 16 * i + 16 + 16 * k)
                    turn_x(pe, 1 - k)
                up(pe, k, n)
                if before:
                    down(pe, 1 - k, n - 1, i + k)

            expert(0, 0, before=False)
            expert(0, 1)
            with pe.Fori(1, NE // 2 - 1) as i:
                for k in range(2):
                    expert(i, k)
            expert(NE // 2 - 1, 0)
            expert(NE // 2 - 1, 1, following=False)
            turn_h(pe, NE - 1)
            down(pe, 1, NE - 1, NE // 2)

            def more(b, k, n, i):
                pe.wait_ge(x_in[k], 16 * i + 16)
                wait(pe, xT_v, n)
                wait(pe, xT_a, n)
                turn_x(pe, k)
                gate(pe, k, n, i)
                up(pe, k, n)
                turn_h(pe, n)
                down(pe, k, n, i + 1)

            overflow(pe, more)

        @block.scalar
        def _(act):
            def x_copy(k, n):
                act.wait_ge(x_turned, n + 1)
                act.activation(xT[k][:, 4:8, :], XT[1][:, :, :], ACT.Copy).then_inc(xT_a, 1)

            def silu(n):
                act.wait_ge(g_done, n + 1)
                wait(act, h_ready, n)
                act.activation(sg[:, :], G[:, :], ACT.Silu).then_inc(silu_done, 1)

            def y_copy(k, n, i):
                act.wait_ge(y_done, n + 1)
                wait(act, y_out[k], 16 * i)
                act.activation(y[k][:, 0:512], Y[0][:, :], ACT.Copy).then_inc(y_a, 1)

            def store(k, n, blk):
                act.wait_ge(y_a, n + 1)
                act.wait_ge(y_v, n + 1)
                act.dma_start(a["s_yb"][bass.ds(blk * P, P), :], y[k][:, :]).then_inc(y_out[k], 16)

            act.wait_ge(const_in, 32)
            x_copy(0, 0)

            def expert(i, k, before=True, following=True):
                n = 2 * i + k
                silu(n)
                if following:
                    x_copy(1 - k, n + 1)
                if before:
                    y_copy(1 - k, n - 1, i - 1 + k)
                    if following:
                        weights.load_d(act, 1 - k, n + 1)
                    store(1 - k, n - 1, n - 1)

            expert(0, 0, before=False)
            expert(0, 1)
            expert(1, 0)
            expert(1, 1)
            with act.Fori(2, NE // 2 - 1) as i:
                for k in range(2):
                    expert(i, k)
            expert(NE // 2 - 1, 0)
            expert(NE // 2 - 1, 1, following=False)
            y_copy(1, NE - 1, NE // 2 - 1)
            store(1, NE - 1, NE - 1)

            def more(b, k, n, i):
                e = act.value_load(ov[0:1, bass.ds(b, 1)], min_val=0, max_val=NE - 1)
                weights.load_d(act, k, e)
                x_copy(k, n)
                silu(n)
                y_copy(k, n, i)
                store(k, n, n)
                act.wait_ge(y_out[k], 16 * i + 16)
                act.activation(settled[:, :], ident[0:1, 0:1], ACT.Copy)

            act.wait_ge(y_out[0], 16 * (NE // 2))
            act.wait_ge(y_out[1], 16 * (NE // 2))
            overflow(act, more)

        @block.vector
        def _(dve):
            def x_copy(k, n):
                dve.wait_ge(x_turned, n + 1)
                dve.tensor_copy(xT[k][:, 0:4, :], XT[0][:, :, :]).then_inc(xT_v, 1)

            def hidden(n):
                dve.wait_ge(silu_done, n + 1)
                dve.wait_ge(u_done, n + 1)
                wait(dve, h_turned, n)
                dve.tensor_tensor(h[:, :], sg[:, :], U[:, :], ALU.mult).then_inc(h_ready, 1)

            def h_copy(n):
                dve.wait_ge(h_turned, n + 1)
                dve.tensor_copy(hT[:, :, :], HT[:, :, :]).then_inc(hT_ready, 1)

            def y_copy(k, n, i):
                dve.wait_ge(y_done, n + 1)
                wait(dve, y_out[k], 16 * i)
                dve.tensor_copy(y[k][:, 512:D], Y[1][:, :]).then_inc(y_v, 1)

            dve.wait_ge(const_in, 32)
            x_copy(0, 0)

            def expert(i, k, before=True, following=True):
                n = 2 * i + k
                if before:
                    h_copy(n - 1)
                if following:
                    x_copy(1 - k, n + 1)
                hidden(n)
                if before:
                    y_copy(1 - k, n - 1, i - 1 + k)

            expert(0, 0, before=False)
            expert(0, 1)
            expert(1, 0)
            expert(1, 1)
            with dve.Fori(2, NE // 2 - 1) as i:
                for k in range(2):
                    expert(i, k)
            expert(NE // 2 - 1, 0)
            expert(NE // 2 - 1, 1, following=False)
            h_copy(NE - 1)
            y_copy(1, NE - 1, NE // 2 - 1)

            def more(b, k, n, i):
                x_copy(k, n)
                hidden(n)
                h_copy(n)
                y_copy(k, n, i)

            overflow(dve, more)


def stage_combine(nc, a):
    with Scope(nc, "fin") as s:
        route = s.sb("route", [P, 4, TT])
        slot = s.sb("slot", [P, 2, TT], U32)
        mod = s.sb("mod", [P, D])
        mods = s.sb("mods", [NB, D])
        gf = s.sb("gf", [P, D])
        eps = s.sb("eps", [P, 1])
        x2 = [s.sb(f"x2{i}", [P, D]) for i in range(3)]
        y1 = [s.sb(f"y1{i}", [P, D]) for i in range(3)]
        y2 = [s.sb(f"y2{i}", [P, D]) for i in range(3)]
        f1 = [s.sb(f"f1{i}", [P, D]) for i in range(2)]
        junk = s.sb("junk", [P, D])
        stat = s.sb("stat", [P, TT, 3])
        out = [s.sb(f"out{i}", [P, D]) for i in range(2)]

        const_in = s.sem("const_in")
        slot_ready = s.sem("slot_ready")
        x_in = [s.sem(f"x_in{i}") for i in range(3)]
        y_in = [s.sem(f"y_in{i}") for i in range(3)]
        first = s.sem("first")
        summed = s.sem("summed")
        ss = s.sem("ss")
        root = s.sem("root")
        normed = s.sem("normed")
        vch = s.sem("vch")
        out_done = [s.sem(f"out_done{i}") for i in range(2)]
        block = s.block()

        def store(sp, t):
            n = rows_of(t)
            sp.wait_ge(normed, t + 1)
            dst = a["o_y_p"][0, t * P:t * P + n, :] if t < NT else a["o_y_s"][:, 0, :]
            sp.dma_start(dst, out[t % 2][0:n, :]).then_inc(out_done[t % 2], 16)

        @block.sync
        def _(sp):
            sp.dma_start(route[:, :, :].rearrange("p k t -> p (k t)"), a["s_route"]).then_inc(const_in, 16)
            sp.dma_start(mod[:, :], a["s_mod"][NB:NB + 1, 5 * D:6 * D].to_broadcast([P, D])).then_inc(const_in, 16)
            sp.dma_start(mods[:, :], a["s_mod"][0:NB, 5 * D:6 * D]).then_inc(const_in, 16)
            sp.dma_start(gf[:, :], a["final_g"].to_broadcast([P, D])).then_inc(const_in, 16)
            for t in range(TT):
                n = rows_of(t)
                if t >= 3:
                    sp.wait_ge(normed, t - 2)
                sp.dma_start(x2[t % 3][0:n, :], a["s_x2"][t * P:t * P + n, :]).then_inc(x_in[t % 3], 16)
                if t:
                    store(sp, t - 1)
            store(sp, TT - 1)
            sp.wait_ge(out_done[0], 16 * ((TT + 1) // 2))
            sp.wait_ge(out_done[1], 16 * (TT // 2))

        @block.gpsimd
        def _(pool):
            pool.wait_ge(slot_ready, 1)
            for t in range(TT):
                n = rows_of(t)
                if t >= 3:
                    pool.wait_ge(summed, t - 2)
                for k, dst in enumerate((y1, y2)):
                    pool.indirect_dma_start(dst[t % 3][0:n, :], None, a["s_yb"],
                                            bass.IndirectOffsetOnAxis(ap=slot[0:n, k, t:t + 1], axis=0)
                                            ).then_inc(y_in[t % 3], 16)

        @block.scalar
        def _(act):
            act.wait_ge(const_in, 64)

            def weigh(t):
                n = rows_of(t)
                act.wait_ge(y_in[t % 3], 32 * (t // 3 + 1))
                if t >= 2:
                    act.wait_ge(summed, t - 1)
                act.activation(f1[t % 2][0:n, :], y1[t % 3][0:n, :], ACT.Copy, scale=route[0:n, 2, t:t + 1]).then_inc(first, 1)

            weigh(0)
            for t in range(TT):
                n = rows_of(t)
                if t + 1 < TT:
                    weigh(t + 1)
                act.wait_ge(summed, t + 1)
                act.activation(junk[0:n, :], x2[t % 3][0:n, :], ACT.Square, accum_out=stat[0:n, t, 0:1]).then_inc(ss, 1)
                act.wait_ge(ss, t + 1)
                act.activation(stat[0:n, t, 1:2], stat[0:n, t, 0:1], ACT.Sqrt, bias=eps[0:n, :], scale=1.0 / D
                               ).then_inc(root, 1)

        @block.vector
        def _(dve):
            step = Chain(dve, vch)
            step(dve.memset(eps[:, :], EPS))
            dve.wait_ge(const_in, 64)
            dve.tensor_copy(slot[:, :, :], route[:, 0:2, :]).then_inc(slot_ready, 1)

            def add(t):
                n = rows_of(t)
                m = (mod if t < NT else mods)[0:n, :]
                f, x = f1[t % 2][0:n, :], x2[t % 3][0:n, :]
                dve.wait_ge(first, t + 1)
                step(dve.scalar_tensor_tensor(out=f, in0=y2[t % 3][0:n, :], scalar=route[0:n, 3, t:t + 1], in1=f,
                                              op0=ALU.mult, op1=ALU.add))
                step(dve.tensor_tensor(f, f, m, ALU.mult))
                dve.wait_ge(x_in[t % 3], 16 * (t // 3 + 1))
                dve.tensor_tensor(x, x, f, ALU.add).then_inc(summed, 1)

            def norm(t):
                n = rows_of(t)
                dve.wait_ge(root, t + 1)
                if t >= 2:
                    dve.wait_ge(out_done[t % 2], 16 * (t // 2))
                step(dve.reciprocal(stat[0:n, t, 2:3], stat[0:n, t, 1:2]))
                dve.scalar_tensor_tensor(out=out[t % 2][0:n, :], in0=x2[t % 3][0:n, :], scalar=stat[0:n, t, 2:3],
                                         in1=gf[0:n, :], op0=ALU.mult, op1=ALU.mult).then_inc(normed, 1)

            add(0)
            for t in range(TT):
                if t + 1 < TT:
                    add(t + 1)
                norm(t)


def build(nc, a):
    stage_ada(nc, a)
    stage_project(nc, a)
    stage_compress(nc, a)
    stage_prompt_attention(nc, a)
    stage_sample_attention(nc, a)
    stage_merge_route(nc, a)
    with Scope(nc, "wts") as s:
        weights = ExpertWeights(s, a)
        stage_slots(nc, a, weights)
        stage_experts(nc, a, weights)
    stage_combine(nc, a)


OUTS = [("o_y_p", (1, T, D)), ("o_y_s", (NB, 1, D)), ("o_cmp_p", (1, 1, T, 2, NG, HD)),
        ("o_cmp_s", (1, NB, 1, 2, NG, HD)), ("o_sel_p", (1, 1, T, 2, NG, HD)), ("o_sel_s", (1, NB, 1, 2, NG, HD)),
        ("o_win_p", (1, 1, 512, 2, NG, HD)), ("o_win_s", (1, NB, 512, 2, NG, HD)),
        ("o_conv_p", (1, 1, 2, CW)), ("o_conv_s", (1, NB, 2, CW))]
SCRATCH = [("s_mod", (9, 6 * D)), ("s_cT", (P, KT * 9)), ("s_convT", (CJ, P, T)), ("s_convs", (NB, CW)), ("s_z", (NTOK, TOK)),
           ("s_ck", (NB + 1, HD, NG, NCH)), ("s_cv", (NB + 1, NCH, NG * HD)),
           ("s_attn", (NTOK, NH * HD)), ("s_x2", (NTOK, D)), ("s_h2", (NTOK + 1, D)),
           ("s_logit", (P, TT * (NGR + NE))), ("s_route", (P, 4 * TT)), ("s_ov", (1, NOV + 1)),
           ("s_slot", (NBLK * P, 1)), ("s_yb", (NBLK * P, D))]


def constants():
    f = np.float32
    half = HD // 2
    inv = (f(10000.0) ** (-np.arange(half, dtype=f) / f(half))).astype(f)

    def tables(pos):
        ang = pos.astype(f)[:, None] * inv[None, :]
        c, s = np.cos(ang).astype(f), np.sin(ang).astype(f)
        return np.concatenate([c, c], 1), np.concatenate([-s, s], 1)

    c, s = tables(np.concatenate([np.arange(T), np.full(NB, PAST)]))
    out = {"c_ident": np.eye(P, dtype=f),
           "c_rope": np.stack([c, s, c / 8, s / 8]),
           "c_mod8": (np.arange(P) % 8).astype(f).reshape(P, 1)}
    c, s = tables((np.arange(NCMP) + 2) * 16 - 1)
    out["c_ropec"] = np.ascontiguousarray(np.stack([c.T, s.T], 1))
    q, k = np.arange(P)[:, None], np.arange(P)[None, :]
    out["c_diag"] = np.where(k <= q, 0, NEG).astype(f)
    out["c_far"] = np.where(k >= q, 0, NEG).astype(f)
    out["c_cmask"] = np.where(16 * (np.arange(64)[None, :] - 57) + 31 <= q, 0, NEG).astype(f)
    out["c_valid"] = (np.arange(P) >= 31).astype(f).reshape(P, 1)
    out["c_member"] = (np.arange(64)[:, None] // QG == np.arange(16)[None, :]).astype(f)
    out["c_tri64"] = (np.arange(64)[None, :] < np.arange(64)[:, None]).astype(f).reshape(1, 64, 64)
    out["c_iota"] = np.arange(P, dtype=f).reshape(1, P)
    out["c_half64"] = np.array([[0, 64]], f)
    out["c_mod64"] = (np.arange(P) % 64).astype(f).reshape(P, 1)
    out["c_ones"] = np.ones((P, P), f)
    out["c_tri"] = (np.arange(P)[:, None] < np.arange(P)[None, :]).astype(f)
    out["c_blocks"] = (np.arange(1, 9) * 128).astype(f).reshape(1, 8)
    tok = np.arange(TT)[None, :] * P + np.arange(P)[:, None]
    out["c_tok"] = tok.astype(np.uint32)
    out["c_real"] = (tok < NTOK).astype(f)
    return out


def kernel(**inputs):
    import concourse.bacc as _bacc
    from concourse.bass_utils import run_bass_kernel_spmd as _run

    nc = _bacc.Bacc("TRN2", target_bir_lowering=False, num_devices=1)
    arrays, a = {}, {}
    for name, v in list(inputs.items()) + list(constants().items()):
        v = np.ascontiguousarray(v)
        if v.ndim == 1:
            v = v.reshape(1, -1)
        arrays[f"in_{name}"] = v
        a[name] = nc.dram_tensor(f"in_{name}", v.shape, mybir.dt.from_np(v.dtype), kind="ExternalInput").ap()
    for name, shape in OUTS:
        a[name] = nc.dram_tensor(name, shape, F32, kind="ExternalOutput").ap()
    for name, shape in SCRATCH:
        a[name] = nc.dram_tensor(name, shape, {"s_ov": I32, "s_slot": U32}.get(name, F32)).ap()
    build(nc, a)
    r = _run(nc, [arrays], core_ids=[0])
    return tuple(r.results[0][name] for name, _ in OUTS)
```

```python
from contextlib import ExitStack

import concourse.bass as bass
import numpy as np
from concourse import mybir

ALU = mybir.AluOpType
ACT = mybir.ActivationFunctionType
F32 = mybir.dt.float32
I32 = mybir.dt.int32
U32 = mybir.dt.uint32
F32R = mybir.dt.float32r
AX = mybir.AxisListType.X

P = 128
D = 1024
KT = D // P
T = 1024
NT = T // P
NB = 8
PAST = 4096
CW = 512
CJ = CW // P
HD = 64
NH = 8
NG = 2
QG = NH // NG
TOK = 1304
QO, CO, SO, WO, GO = 0, 512, 768, 1024, 1280
EPS = 1e-6
NEG = -1e30
NE = 32
NGR = 4
EPG = NE // NGR
DE = 512
NTOK = T + NB
TT = NT + 1
ZROW = NTOK
NOV = 16
NBLK = NE + NOV
NPAGE = PAST // 128
ADA1 = 2 * D // 512
ADA = 6 * D // 512
NCH = PAST // 16
NCMP = NCH - 1
NSB = 15


def wait(eng, sem, value):
    if not (isinstance(value, int) and value <= 0):
        eng.wait_ge(sem, value)


def rows_of(t):
    return P if t < NT else NB


class Chain:

    def __init__(self, eng, sem):
        self.eng, self.sem, self.n = eng, sem, 0

    def __call__(self, ins):
        self.n += 1
        ins.then_inc(self.sem, 1)
        self.eng.wait_ge(self.sem, self.n)


class Scope:

    def __init__(self, nc, name):
        self.nc, self.name, self.stack, self.sems = nc, name, ExitStack(), []

    def __enter__(self):
        return self

    def __exit__(self, *a):
        self.stack.close()
        self.nc.clear_and_free_semaphores(self.sems)
        self.nc.all_engine_barrier()

    def sb(self, name, shape, dt=F32):
        return self.stack.enter_context(self.nc.sbuf_tensor(f"{self.name}_{name}", shape, dt))

    def ps(self, name, shape, dt=F32):
        return self.stack.enter_context(self.nc.psum_tensor(f"{self.name}_{name}", shape, dt))

    def sem(self, name):
        self.sems.append(self.nc.alloc_semaphore(name=f"{self.name}_{name}"))
        return self.sems[-1]

    def block(self):
        return self.stack.enter_context(self.nc.Block())


def stage_ada(nc, a):
    NC = ADA1
    NBUF = 4
    with Scope(nc, "ada") as s:
        c9 = s.sb("c9", [9, D])
        sc9 = s.sb("sc9", [9, D])
        cT = s.sb("cT", [P, KT, 9])
        ident = s.sb("ident", [P, P])
        bias = s.sb("bias", [9, 2 * D])
        g9 = s.sb("g9", [9, D])
        mrow = s.sb("mrow", [9, 2 * D])
        wa = [s.sb(f"wa{i}", [P, KT, 512]) for i in range(NBUF)]
        pT = s.ps("pT", [P, KT, 9])
        pm = [s.ps(f"pm{i}", [9, 512]) for i in range(2)]
        loaded = s.sem("loaded")
        rows_in = s.sem("rows_in")
        w_in = [s.sem(f"w_in{i}") for i in range(NBUF)]
        silu_done = s.sem("silu_done")
        cT_psum = s.sem("cT_psum")
        cT_done = s.sem("cT_done")
        prod = s.sem("prod")
        added = s.sem("added")
        scaled = s.sem("scaled")
        stored = s.sem("stored")
        block = s.block()

        @block.sync
        def _(sp):
            sp.dma_start(c9[0:NB, :], a["c_sample"]).then_inc(loaded, 16)
            sp.dma_start(c9[NB:9, :], a["c_prompt"]).then_inc(loaded, 16)
            sp.dma_start(ident[:, :], a["c_ident"]).then_inc(loaded, 16)
            for n in range(NC):
                if n >= NBUF:
                    sp.wait_ge(prod, n - NBUF + 1)
                sp.dma_start(wa[n % NBUF][:, :, :],
                             a["w_ada"][0, :, n * 512:(n + 1) * 512].rearrange("(k p) n -> p k n", p=P)
                             ).then_inc(w_in[n % NBUF], 16)
                if n == 1:
                    sp.dma_start(bias[:, :], a["b_ada"][:, 0:2 * D].to_broadcast([9, 2 * D])).then_inc(rows_in, 16)
                    sp.dma_start(g9[:, :], a["ln1_g"].to_broadcast([9, D])).then_inc(rows_in, 16)
            sp.wait_ge(cT_done, 1)
            sp.dma_start(a["s_cT"], cT[:, :, :].rearrange("p k n -> p (k n)")).then_inc(stored, 16)
            sp.wait_ge(added, NC)
            sp.wait_ge(scaled, 1)
            sp.dma_start(a["s_mod"][:, 0:2 * D], mrow[:, :]).then_inc(stored, 16)
            sp.wait_ge(stored, 32)

        @block.scalar
        def _(act):
            act.wait_ge(loaded, 48)
            act.activation(sc9[:, :], c9[:, :], ACT.Silu).then_inc(silu_done, 1)

        @block.tensor
        def _(pe):
            pe.wait_ge(loaded, 48)
            pe.wait_ge(silu_done, 1)
            for k in range(KT):
                last = pe.transpose(pT[:, k, :], sc9[:, k * P:(k + 1) * P], ident[0:9, 0:9])
            last.then_inc(cT_psum, 1)
            pe.wait_ge(cT_done, 1)
            for n in range(NC):
                pe.wait_ge(w_in[n % NBUF], 16 * (n // NBUF + 1))
                if n >= 2:
                    pe.wait_ge(added, n - 1)
                for k in range(KT):
                    last = pe.matmul(pm[n % 2][:, :], cT[:, k, :], wa[n % NBUF][:, k, :],
                                     start=(k == 0), stop=(k == KT - 1))
                last.then_inc(prod, 1)

        @block.vector
        def _(dve):
            dve.wait_ge(cT_psum, 1)
            dve.tensor_copy(cT[:, :, :], pT[:, :, :]).then_inc(cT_done, 1)
            dve.wait_ge(rows_in, 32)
            for n in range(NC):
                dve.wait_ge(prod, n + 1)
                dve.tensor_tensor(mrow[:, n * 512:(n + 1) * 512], pm[n % 2][:, :],
                                  bias[:, n * 512:(n + 1) * 512], ALU.add).then_inc(added, 1)
            dve.wait_ge(added, NC)
            dve.scalar_tensor_tensor(out=mrow[:, D:2 * D], in0=mrow[:, D:2 * D], scalar=1.0, in1=g9[:, :],
                                     op0=ALU.add, op1=ALU.mult).then_inc(scaled, 1)


def stage_project(nc, a):
    with Scope(nc, "proj") as s:
        ident = s.sb("ident", [P, P])
        x = [s.sb(f"x{i}", [P, D]) for i in range(3)]
        xn = [s.sb(f"xn{i}", [P, D]) for i in range(2)]
        junk = s.sb("junk", [P, D])
        ss = s.sb("ss", [P, 3 * TT])
        eps = s.sb("eps", [P, 1])
        hT = s.sb("hT", [P, KT, T])
        hTs = s.sb("hTs", [P, KT, NB])
        scol = s.sb("scol", [P, KT])
        bcol = s.sb("bcol", [P, KT])
        srow = s.sb("srow", [NB, 2, D])
        wc = [s.sb(f"wc{i}", [P, KT, 3, P]) for i in range(2)]
        wt = s.sb("wt", [P, KT, TOK])
        wconv = s.sb("wconv", [P, 3, CJ])
        wconvs = s.sb("wconvs", [NB, 3, CW])
        csb = [s.sb(f"csb{i}", [P, 512]) for i in range(2)]
        v = [s.sb(f"v{i}", [P, 2 + T]) for i in range(2)]
        y = s.sb("y", [P, 512])
        co = [s.sb(f"co{i}", [P, T]) for i in range(2)]
        tail = s.sb("tail", [P, CJ, 2])
        zc = s.sb("zc", [NB, 3, CW])
        st = s.sb("st", [NB, 2, CW])
        vs = s.sb("vs", [NB, CW])
        ys = s.sb("ys", [NB, 2, CW])
        z = [s.sb(f"z{i}", [P, TOK]) for i in range(2)]
        r1 = s.sb("r1", [P, 512])
        r2 = s.sb("r2", [P, 512])
        rope = [s.sb(f"rope{i}", [P, 4, HD]) for i in range(2)]
        tp = [s.ps(f"tp{i}", [P, 4, P]) for i in range(2)]
        ps = [s.ps(f"ps{i}", [P, 512]) for i in range(6)]

        ident_in = s.sem("ident_in")
        const_in = s.sem("const_in")
        x_in = [s.sem(f"x_in{i}") for i in range(3)]
        wc_in = [s.sem(f"wc_in{i}") for i in range(2)]
        wt_in = s.sem("wt_in")
        rope_in = [s.sem(f"rope_in{i}") for i in range(2)]
        summed = s.sem("summed")
        squared = s.sem("squared")
        rstd = s.sem("rstd")
        normed = s.sem("normed")
        turned = s.sem("turned")
        evac_v = s.sem("evac_v")
        evac_a = s.sem("evac_a")
        modded = s.sem("modded")
        group = s.sem("group")
        c_copied = s.sem("c_copied")
        conv_done = s.sem("conv_done")
        sconv_psum = s.sem("sconv_psum")
        sconv_copied = s.sem("sconv_copied")
        z_copied = s.sem("z_copied")
        roped = s.sem("roped")
        vch = s.sem("vch")
        tails = s.sem("tails")
        samp = s.sem("samp")
        co_out = [s.sem(f"co_out{i}") for i in range(2)]
        z_out = [s.sem(f"z_out{i}") for i in range(2)]
        end_out = s.sem("end_out")
        block = s.block()
        NG_CONV = 2 * CJ

        def load_wc(sp, j):
            for r in range(3):
                sp.dma_start(wc[j % 2][:, :, r, :],
                             a["w_in"][0, :, r * CW + j * P:r * CW + (j + 1) * P].rearrange("(k p) n -> p k n", p=P)
                             ).then_inc(wc_in[j % 2], 16)

        def outs_of(t):
            return 4 if t >= NT // 2 else 3

        def store_z(sp, t):
            n = rows_of(t)
            sp.wait_ge(roped, t + 1)
            zt = z[t % 2]
            sp.dma_start(a["s_z"][t * P:t * P + n, :], zt[0:n, :]).then_inc(z_out[t % 2], 16)
            for off, op, os in ((CO, "o_cmp_p", "o_cmp_s"), (SO, "o_sel_p", "o_sel_s")):
                dst = (a[op][0, 0, t * P:(t + 1) * P] if t < NT else a[os][0, :, 0]).rearrange("t c g d -> t (c g d)")
                sp.dma_start(dst, zt[0:n, off:off + 256]).then_inc(z_out[t % 2], 16)
            if t >= NT // 2:
                if t < NT:
                    dst = a["o_win_p"][0, 0, t * P - 512:t * P - 512 + P]
                else:
                    dst = a["o_win_s"][0, :, 511]
                sp.dma_start(dst.rearrange("t c g d -> t (c g d)"), zt[0:n, WO:WO + 256]).then_inc(z_out[t % 2], 16)

        @block.sync
        def _(sp):
            def load_x(t):
                src = a["x_prompt"][0, t * P:(t + 1) * P, :] if t < NT else a["x_sample"][:, 0, :]
                sp.dma_start(x[t % 3][0:rows_of(t), :], src).then_inc(x_in[t % 3], 16)

            load_x(0)
            sp.dma_start(ident[:, :], a["c_ident"]).then_inc(ident_in, 16)
            load_x(1)
            load_x(2)
            with nc.allow_non_contiguous_dma(reason="one column of a small vector"):
                sp.dma_start(scol[:, :], a["s_mod"][NB, D:2 * D].rearrange("(k p) -> p k", p=P)).then_inc(const_in, 16)
                sp.dma_start(bcol[:, :], a["s_mod"][NB, 0:D].rearrange("(k p) -> p k", p=P)).then_inc(const_in, 16)
                for r in range(3):
                    sp.dma_start(wconv[:, r, :], a["w_conv"][0, r].rearrange("(j p) -> p j", p=P)).then_inc(const_in, 16)
            sp.dma_start(srow[:, 0, :], a["s_mod"][0:NB, 0:D]).then_inc(const_in, 16)
            sp.dma_start(srow[:, 1, :], a["s_mod"][0:NB, D:2 * D]).then_inc(const_in, 16)
            sp.dma_start(wconvs[:, :, :].rearrange("p r n -> p (r n)"),
                         a["w_conv"].rearrange("a r n -> a (r n)").to_broadcast([NB, 3 * CW])).then_inc(const_in, 16)
            sp.dma_start(st[:, :, :], a["state_conv"][0]).then_inc(const_in, 16)
            for t in range(3, TT):
                sp.wait_ge(normed, t - 2)
                load_x(t)
                if t in (3, 4):
                    load_wc(sp, t - 3)
            sp.dma_start(wt[:, :, :], a["w_in"][0, :, 3 * CW:].rearrange("(k p) n -> p k n", p=P)).then_inc(wt_in, 16)
            for j in range(2, CJ):
                sp.wait_ge(group, 2 * j - 2)
                sp.wait_ge(sconv_psum, j - 1)
                load_wc(sp, j)
            for j in range(CJ):
                sp.wait_ge(conv_done, 2 * j + 2)
                sp.dma_start(a["s_convT"][j], co[j % 2][:, :]).then_inc(co_out[j % 2], 16)
            for t in range(TT):
                store_z(sp, t)

        @block.gpsimd
        def _(pool):
            for t in range(TT):
                n = rows_of(t)
                if t >= 2:
                    pool.wait_ge(roped, t - 1)
                rows = slice(t * P, t * P + n)
                for j in range(4):
                    src = a["c_rope"][j % 2 if j < 2 else 2 + j % 2]
                    pool.dma_start(rope[t % 2][0:n, j, :], src[rows, :]).then_inc(rope_in[t % 2], 16)
            pool.wait_ge(tails, CJ)
            with nc.allow_non_contiguous_dma(reason="two rows of conv state"):
                for r in range(2):
                    pool.dma_start(a["o_conv_p"][0, 0, r].rearrange("(j p) -> p j", p=P),
                                   tail[:, :, r]).then_inc(end_out, 16)
            pool.wait_ge(samp, 1)
            pool.dma_start(a["o_conv_s"][0, :, 0, :], st[:, 1, :]).then_inc(end_out, 16)
            pool.dma_start(a["o_conv_s"][0, :, 1, :], vs[:, :]).then_inc(end_out, 16)
            pool.dma_start(a["s_convs"], ys[:, 1, :]).then_inc(end_out, 16)
            pool.wait_ge(end_out, 16 * 5)
            for i in range(2):
                pool.wait_ge(co_out[i], 16 * (CJ // 2))
                pool.wait_ge(z_out[i], 16 * sum(outs_of(t) for t in range(i, TT, 2)))

        @block.scalar
        def _(act):
            def square(t):
                n = rows_of(t)
                act.wait_ge(x_in[t % 3], 16 * (t // 3 + 1))
                if t:
                    act.wait_ge(squared, t)
                act.activation(junk[0:n, :], x[t % 3][0:n, :], ACT.Square,
                               accum_out=ss[0:n, t:t + 1]).then_inc(summed, 1)
                act.wait_ge(summed, t + 1)
                act.activation(ss[0:n, TT + t:TT + t + 1], ss[0:n, t:t + 1], ACT.Sqrt, bias=eps[0:n, :],
                               scale=1.0 / D).then_inc(squared, 1)

            def evac(t):
                if t == 0:
                    act.wait_ge(const_in, 16 * 9)
                if t < NT:
                    act.wait_ge(turned, t + 1)
                    for k in range(4, KT):
                        last = act.activation(hT[:, k, t * P:(t + 1) * P], tp[1][:, k - 4, :], ACT.Identity,
                                              bias=bcol[:, k:k + 1], scale=scol[:, k:k + 1])
                    last.then_inc(evac_a, 1)
                else:
                    act.wait_ge(turned, TT)
                    act.activation(hTs[:, 4:8, :], tp[1][:, :, 0:NB], ACT.Copy).then_inc(evac_a, 1)

            act.wait_ge(vch, 3)
            square(0)
            for t in range(TT):
                n = rows_of(t)
                if t + 1 < TT:
                    square(t + 1)
                act.wait_ge(rstd, t + 1)
                if t >= 2:
                    act.wait_ge(turned, t - 1)
                act.activation(xn[t % 2][0:n, :], x[t % 3][0:n, :], ACT.Copy,
                               scale=ss[0:n, 2 * TT + t:2 * TT + t + 1]).then_inc(normed, 1)
                if t:
                    evac(t - 1)
            evac(TT - 1)
            for g in range(NG_CONV):
                act.wait_ge(group, g + 1)
                if g >= 2:
                    act.wait_ge(conv_done, g - 1)
                act.activation(csb[g % 2][:, :], ps[g % 2 * 3 + 1][:, :], ACT.Copy).then_inc(c_copied, 1)
                if g % 2:
                    j = g // 2
                    act.wait_ge(sconv_psum, j + 1)
                    act.activation(zc[:, :, j * P:(j + 1) * P],
                                   tp[j % 2][0:NB, 0:3, :], ACT.Copy).then_inc(sconv_copied, 1)
            for t in range(TT):
                n = rows_of(t)
                g = NG_CONV + t
                act.wait_ge(group, g + 1)
                if t >= 2:
                    act.wait_ge(z_out[t % 2], 16 * sum(outs_of(i) for i in range(t % 2, t, 2)))
                b = g % 2 * 3
                act.activation(z[t % 2][0:n, 0:512], ps[b][0:n, :], ACT.Copy)
                act.activation(z[t % 2][0:n, 512:1024], ps[b + 1][0:n, :], ACT.Copy)
                act.activation(z[t % 2][0:n, 1024:GO], ps[b + 2][0:n, 0:GO - 1024], ACT.Copy)
                act.activation(z[t % 2][0:n, GO:TOK], ps[b + 2][0:n, GO - 1024:TOK - 1024],
                               ACT.Sigmoid).then_inc(z_copied, 1)

        @block.tensor
        def _(pe):
            pe.wait_ge(ident_in, 16)
            for t in range(TT):
                n = rows_of(t)
                if t < NT:
                    pe.wait_ge(normed, t + 1)
                    src = xn[t % 2]
                else:
                    pe.wait_ge(modded, 1)
                    src = junk
                if t:
                    pe.wait_ge(evac_v, t)
                    pe.wait_ge(evac_a, t)
                for k in range(KT):
                    last = pe.transpose(tp[k // 4][:, k % 4, 0:n], src[0:n, k * P:(k + 1) * P], ident[0:n, 0:n])
                last.then_inc(turned, 1)
            pe.wait_ge(evac_v, TT)
            pe.wait_ge(evac_a, TT)
            for g in range(NG_CONV):
                j, half = g // 2, g % 2
                pe.wait_ge(wc_in[j % 2], 48 * (j // 2 + 1))
                if g >= 2:
                    pe.wait_ge(conv_done, g - 1)
                for r in range(3):
                    for k in range(KT):
                        last = pe.matmul(ps[g % 2 * 3 + r][:, :], wc[j % 2][:, k, r, :],
                                         hT[:, k, half * 512:(half + 1) * 512],
                                         start=(k == 0), stop=(k == KT - 1))
                last.then_inc(group, 1)
                if half:
                    if j >= 2:
                        pe.wait_ge(sconv_copied, j - 1)
                    for k in range(KT):
                        last = pe.matmul(tp[j % 2][0:NB, 0:3, :], hTs[:, k, :], wc[j % 2][:, k, :, :],
                                         start=(k == 0), stop=(k == KT - 1))
                    last.then_inc(sconv_psum, 1)
            pe.wait_ge(wt_in, 16)
            for t in range(TT):
                g = NG_CONV + t
                n = rows_of(t)
                if t < 2:
                    pe.wait_ge(conv_done, g - 1)
                else:
                    pe.wait_ge(z_copied, t - 1)
                for c in range(3):
                    w = min(512, TOK - c * 512)
                    for k in range(KT):
                        lhs = hT[:, k, t * P:(t + 1) * P] if t < NT else hTs[:, k, :]
                        last = pe.matmul(ps[g % 2 * 3 + c][0:n, 0:w], lhs, wt[:, k, c * 512:c * 512 + w],
                                         start=(k == 0), stop=(k == KT - 1))
                last.then_inc(group, 1)

        @block.vector
        def _(dve):
            step = Chain(dve, vch)
            for i in range(2):
                step(dve.memset(v[i][:, 0:2], 0.0))
            step(dve.memset(eps[:, :], EPS))

            def invert(t):
                n = rows_of(t)
                dve.wait_ge(squared, t + 1)
                dve.reciprocal(ss[0:n, 2 * TT + t:2 * TT + t + 1], ss[0:n, TT + t:TT + t + 1]).then_inc(rstd, 1)

            invert(0)
            dve.wait_ge(const_in, 16 * 9)
            for t in range(TT):
                n = rows_of(t)
                if t + 1 < TT:
                    invert(t + 1)
                if t < NT:
                    dve.wait_ge(turned, t + 1)
                    for k in range(4):
                        last = dve.tensor_scalar(hT[:, k, t * P:(t + 1) * P], tp[0][:, k, :],
                                                 scol[:, k:k + 1], bcol[:, k:k + 1], ALU.mult, ALU.add)
                    last.then_inc(evac_v, 1)
                else:
                    dve.wait_ge(normed, TT)
                    step(dve.tensor_tensor(junk[0:n, :], xn[t % 2][0:n, :], srow[:, 1, :], ALU.mult))
                    dve.tensor_tensor(junk[0:n, :], junk[0:n, :], srow[:, 0, :], ALU.add).then_inc(modded, 1)
                    dve.wait_ge(turned, TT)
                    dve.tensor_copy(hTs[:, 0:4, :], tp[0][:, :, 0:NB]).then_inc(evac_v, 1)
            for g in range(NG_CONV):
                j, half = g // 2, g % 2
                vj, lo = v[j % 2], half * 512
                if j >= 2 and not half:
                    dve.wait_ge(co_out[j % 2], 16)
                dve.wait_ge(c_copied, g + 1)
                step(dve.tensor_tensor(vj[:, 2 + lo:2 + lo + 512], csb[g % 2][:, :], ps[g % 2 * 3 + 2][:, :], ALU.mult))
                step(dve.tensor_scalar(y[:, :], vj[:, lo:lo + 512], wconv[:, 0, j:j + 1], None, ALU.mult))
                for r in (1, 2):
                    step(dve.scalar_tensor_tensor(out=y[:, :], in0=vj[:, lo + r:lo + r + 512], scalar=wconv[:, r, j:j + 1],
                                                  in1=y[:, :], op0=ALU.mult, op1=ALU.add))
                if half:
                    dve.tensor_copy(tail[:, j, :], vj[:, T:T + 2]).then_inc(tails, 1)
                dve.tensor_tensor(co[j % 2][:, lo:lo + 512], y[:, :], ps[g % 2 * 3][:, :], ALU.mult).then_inc(conv_done, 1)
                dve.wait_ge(conv_done, g + 1)
            dve.wait_ge(sconv_copied, CJ)
            step(dve.tensor_tensor(vs[:, :], zc[:, 1, :], zc[:, 2, :], ALU.mult))
            step(dve.tensor_tensor(ys[:, 0, :], st[:, 0, :], wconvs[:, 0, :], ALU.mult))
            step(dve.tensor_tensor(ys[:, 1, :], st[:, 1, :], wconvs[:, 1, :], ALU.mult))
            step(dve.tensor_tensor(ys[:, 0, :], ys[:, 0, :], ys[:, 1, :], ALU.add))
            step(dve.tensor_tensor(ys[:, 1, :], vs[:, :], wconvs[:, 2, :], ALU.mult))
            step(dve.tensor_tensor(ys[:, 0, :], ys[:, 0, :], ys[:, 1, :], ALU.add))
            dve.tensor_tensor(ys[:, 1, :], ys[:, 0, :], zc[:, 0, :], ALU.mult).then_inc(samp, 1)

            for t in range(TT):
                n = rows_of(t)
                dve.wait_ge(z_copied, t + 1)
                dve.wait_ge(rope_in[t % 2], 64 * (t // 2 + 1))
                zt, rt = z[t % 2], rope[t % 2]
                parts = ([(zt[0:n, QO:512].rearrange("p (h d) -> p h d", d=HD), 8, 2)]
                         + [(zt[0:n, o:o + 128].rearrange("p (h d) -> p h d", d=HD), 2, 0) for o in (SO, WO)])
                for i, (zv, h, tab) in enumerate(parts):
                    cos = rt[0:n, tab:tab + 1, :].to_broadcast([n, h, HD])
                    sin = rt[0:n, tab + 1:tab + 2, :].to_broadcast([n, h, HD])
                    a1 = r1[0:n, 0:h * HD].rearrange("p (h d) -> p h d", d=HD)
                    a2 = r2[0:n, 0:h * HD].rearrange("p (h d) -> p h d", d=HD)
                    dve.tensor_tensor(a1, zv, cos, ALU.mult)
                    dve.tensor_tensor(a2[:, :, 0:32], zv[:, :, 32:64], sin[:, :, 0:32], ALU.mult)
                    step(dve.tensor_tensor(a2[:, :, 32:64], zv[:, :, 0:32], sin[:, :, 32:64], ALU.mult))
                    if i < 2:
                        step(dve.tensor_tensor(zv, a1, a2, ALU.add))
                dve.tensor_tensor(zv, a1, a2, ALU.add).then_inc(roped, 1)
                dve.wait_ge(roped, t + 1)


def stage_compress(nc, a):
    PCH = T // 16
    with Scope(nc, "cmp") as s:
        ident = s.sb("ident", [P, P])
        pt = s.sb("pt", [P, 2 * NB], I32)
        c8 = s.sb("c8", [P, 1])
        idxf = s.sb("idxf", [P, 2 * NB])
        idx = s.sb("idx", [P, 2 * NB], U32)
        x = [s.sb(f"x{h}", [P, 16 * 4 * HD]) for h in range(2)]
        xs = [s.sb(f"xs{h}", [P, 4, 16, HD]) for h in range(2)]
        xh = s.sb("xh", [P, 4, 8, NCH], F32R)
        xl = s.sb("xl", [P, 4, 8, NCH], F32R)
        w1 = s.sb("w1", [P, 32, P])
        wh = s.sb("wh", [P, 32, P], F32R)
        wl = s.sb("wl", [P, 32, P], F32R)
        pos = s.sb("pos", [P, 32])
        b1 = s.sb("b1", [P, 2])
        bias = s.sb("bias", [P, 2])
        w2 = s.sb("w2", [P, 2, HD])
        w2r = s.sb("w2r", [P, HD])
        b2 = s.sb("b2", [HD, 2])
        b2v = s.sb("b2v", [P, HD])
        rope = s.sb("rope", [HD, 2, NCMP])
        raw = [s.sb(f"raw{i}", [P, NCMP]) for i in range(2)]
        hid = s.sb("hid", [P, 4, NCMP])
        t1 = s.sb("t1", [HD, NCMP])
        t2 = s.sb("t2", [HD, NCMP])
        ck = s.sb("ck", [HD, NG, NCMP])
        cv = s.sb("cv", [P, 2, NG, HD])
        junk = s.sb("junk", [P, 4])
        bank = [s.ps(f"bank{i}", [P, 4, P]) for i in range(4)]
        hp = [s.ps(f"hp{i}", [P, 2, NCH]) for i in range(2)]
        kp = s.ps("kp", [HD, 2, 256])
        vp = s.ps("vp", [P, 2, HD])

        pt_in = s.sem("pt_in")
        const_in = s.sem("const_in")
        idx_ready = s.sem("idx_ready")
        w2r_ready = s.sem("w2r_ready")
        bias_psum = s.sem("bias_psum")
        bias_ready = s.sem("bias_ready")
        x_in = [s.sem(f"x_in{h}") for h in range(2)]
        shuffled_v = s.sem("shuffled_v")
        shuffled_a = s.sem("shuffled_a")
        w_high = s.sem("w_high")
        w_split = s.sem("w_split")
        turned = s.sem("turned")
        high = s.sem("high")
        free = s.sem("free")
        hid_psum = s.sem("hid_psum")
        added = s.sem("added")
        raw_ready = s.sem("raw_ready")
        hid_ready = s.sem("hid_ready")
        k_psum = s.sem("k_psum")
        k_free = s.sem("k_free")
        v_psum = s.sem("v_psum")
        v_free = s.sem("v_free")
        tsum = s.sem("tsum")
        out_done = [s.sem(f"out_done{i}") for i in range(2)]
        win_out = s.sem("win_out")
        block = s.block()
        NCONST = 10

        def store(sp, b, i):
            sp.wait_ge(k_free, i * 2 + 3)
            sp.dma_start(a["s_ck"][bass.ds(b, 1), :, :, 0:NCMP].rearrange("o d g n -> (o d) g n"),
                         ck[:, :, :]).then_inc(out_done[0], 16)
            sp.wait_ge(v_free, i * 2 + 3)
            for h, n in ((0, P), (1, NCMP - P)):
                sp.dma_start(a["s_cv"][bass.ds(b, 1), h * P:h * P + n, :].rearrange("o n c -> (o n) c"),
                             cv[0:n, h, :, :].rearrange("p g d -> p (g d)")).then_inc(out_done[1], 16)

        def steps(halves, following):
            turn = [("turn", 8 * h + grp) for h in range(len(halves)) for grp in range(8)]
            nxt = [("shuffle", h) for h in range(len(following))]
            if len(halves) == 1:
                return turn + [("product", c) for c in range(4)]
            return (turn[0:8] + nxt[0:1] + turn[8:12] + [("product", 0)] + turn[12:14] + [("product", 1)]
                    + turn[14:16] + nxt[1:2] + [("product", 2), ("product", 3)])

        def piece(n):
            return n % 8 // 2, 4 * (n % 2), n // 8 * P

        def shuffle(eng, op, parts, i, h, n, done):
            eng.wait_ge(x_in[h], 16 * i + 16)
            wait(eng, turned, 16 * i + 8 * h - 8 if not (isinstance(i, int) and i == 0) else 0)
            src = x[h][0:n, :].rearrange("p (s c d) -> p c s d", s=16, d=HD)
            for c in parts:
                last = op(xs[h][0:n, c, :, :], src[:, c])
            last.then_inc(done, 1)

        @block.sync
        def _(sp):
            sp.dma_start(c8[:, :], a["c_mod8"]).then_inc(pt_in, 16)
            with nc.allow_non_contiguous_dma(reason="columns of small tables"):
                for c in range(8):
                    sp.dma_start(pt[c:P:8, :], a["page_table"].rearrange("b (h g) -> g (b h)", g=16)).then_inc(pt_in, 16)
                sp.dma_start(pos[:, :], a["cmp_pos"][0].rearrange("c (t l) d -> (l d) (c t)", l=2)).then_inc(const_in, 16)
                sp.dma_start(b1[:, :], a["cmp_b1"][0].rearrange("c h -> h c")).then_inc(const_in, 16)
                kb = a["cmp_b2"][0, 0:1, :].rearrange("a d -> d a")
                sp.dma_start(b2[:, 0:1], kb).then_inc(const_in, 16)
                sp.dma_start(b2[0:32, 1:2], kb[32:64, :]).then_inc(const_in, 16)
                sp.dma_start(b2[32:64, 1:2], kb[0:32, :]).then_inc(const_in, 16)
            sp.dma_start(ident[:, :], a["c_ident"]).then_inc(const_in, 16)
            sp.dma_start(rope[:, :, :], a["c_ropec"]).then_inc(const_in, 16)
            sp.dma_start(b2v[:, :], a["cmp_b2"][0, 1:2, :].to_broadcast([P, HD])).then_inc(const_in, 16)
            sp.dma_start(w2[:, :, :], a["cmp_w2"][0].rearrange("c h d -> h c d")).then_inc(const_in, 16)
            sp.dma_start(w1[:, :, :], a["cmp_w1"][0].rearrange("c (t l) d h -> (l d) (c t) h", l=2)).then_inc(const_in, 16)
            sp.dma_start(a["o_win_s"][0, :, 0:511].rearrange("b (x y) c g d -> b x (y c g d)", y=7),
                         a["cache_win_kv"][0, :, 1:512].rearrange("b (x y) c g d -> b x (y c g d)", y=7)
                         ).then_inc(win_out, 16)
            store(sp, 0, 0)
            with sp.Fori(1, NB) as b:
                store(sp, b, b)
            sp.wait_ge(k_free, 2 * NB + 3)
            sp.dma_start(a["s_ck"][NB, :, :, 0:PCH - 1], ck[:, :, 0:PCH - 1]).then_inc(out_done[0], 16)
            sp.wait_ge(v_free, 2 * NB + 3)
            sp.dma_start(a["s_cv"][NB, 0:PCH - 1, :], cv[0:PCH - 1, 0, :, :]).then_inc(out_done[1], 16)
            sp.wait_ge(out_done[0], 16 * (NB + 1))
            sp.wait_ge(out_done[1], 32 * NB + 16)
            sp.wait_ge(win_out, 16)

        @block.gpsimd
        def _(pool):
            chunks = a["cache_cmp_kv"][0].rearrange("n (c s) k g d -> (n c) (s k g d)", s=16)

            def gather(b, h):
                pool.indirect_dma_start(x[h][:, :], None, chunks,
                                        bass.IndirectOffsetOnAxis(ap=idx[:, 2 * b + h:2 * b + h + 1], axis=0)
                                        ).then_inc(x_in[h], 16)

            pool.wait_ge(idx_ready, 1)
            gather(0, 0)
            gather(0, 1)
            for b in range(NB):
                for h in range(2):
                    if b + 1 < NB or h == 0:
                        pool.wait_ge(shuffled_v, 2 * b + h + 1)
                        pool.wait_ge(shuffled_a, 2 * b + h + 1)
                    if b + 1 < NB:
                        gather(b + 1, h)
                    elif h == 0:
                        pool.dma_start(x[0][0:PCH, :], a["o_cmp_p"][0, 0].rearrange("(n s) k g d -> n (s k g d)", s=16)
                                       ).then_inc(x_in[0], 16)

        @block.scalar
        def _(act):

            def copy(o, x_):
                return act.activation(o, x_, ACT.Copy)

            for h in range(2):
                shuffle(act, copy, (2, 3), 0, h, P, shuffled_a)
            act.wait_ge(const_in, 16 * NCONST)
            act.activation(wh[:, :, :], w1[:, :, :], ACT.Copy).then_inc(w_high, 1)
            act.wait_ge(bias_ready, 1)

            def body(i, halves, n, following):
                for what, k in steps(halves, following):
                    if what == "turn":
                        c, t0, n0 = piece(k)
                        act.wait_ge(turned, 16 * i + k + 1)
                        copy(xh[:, c, t0:t0 + 4, n0:n0 + halves[k // 8]], bank[k % 4][:, :, 0:halves[k // 8]]).then_inc(high, 1)
                    elif what == "shuffle":
                        shuffle(act, copy, (2, 3), i + 1, k, following[k], shuffled_a)
                    else:
                        act.wait_ge(raw_ready, 4 * i + k + 1)
                        act.activation(hid[:, k, 0:n], raw[k % 2][:, 0:n], ACT.Gelu_apprx_tanh,
                                       bias=bias[:, k // 2:k // 2 + 1]).then_inc(hid_ready, 1)

            body(0, (P, P), NCMP, (P, P))
            with act.Fori(1, NB - 1) as i:
                body(i, (P, P), NCMP, (P, P))
            body(NB - 1, (P, P), NCMP, (PCH,))
            body(NB, (PCH,), PCH - 1, ())

        @block.vector
        def _(dve):
            dve.memset(junk[:, 0:1], 0.0).then_inc(tsum, 1)
            dve.wait_ge(tsum, 1)
            dve.wait_ge(pt_in, 16 * 9)
            dve.tensor_scalar(idxf[:, :], pt[:, :], 8.0, c8[:, 0:1], ALU.mult, ALU.add).then_inc(tsum, 1)
            dve.wait_ge(tsum, 2)
            dve.tensor_copy(idx[:, :], idxf[:, :]).then_inc(idx_ready, 1)
            for h in range(2):
                shuffle(dve, dve.tensor_copy, (0, 1), 0, h, P, shuffled_v)
            dve.wait_ge(const_in, 16 * NCONST)
            dve.tensor_copy(w2r[:, 0:32], w2[:, 0, 32:64])
            dve.tensor_copy(w2r[:, 32:64], w2[:, 0, 0:32]).then_inc(w2r_ready, 1)
            dve.wait_ge(w_high, 1)
            dve.tensor_tensor(wl[:, :, :], w1[:, :, :], wh[:, :, :], ALU.subtract).then_inc(w_split, 1)
            dve.wait_ge(bias_psum, 1)
            dve.tensor_tensor(bias[:, :], hp[0][:, 0, 0:2], b1[:, :], ALU.add).then_inc(bias_ready, 1)
            for sem, k in ((free, 4), (k_free, 1), (v_free, 1)):
                for j in range(k):
                    dve.memset(junk[:, 0:1], 0.0).then_inc(sem, 1)
                    dve.wait_ge(sem, j + 1)

            def keys(i, g, n):
                if g == 0:
                    wait(dve, out_done[0], i * 16)
                dve.wait_ge(k_psum, i * 2 + g + 1)
                dve.scalar_tensor_tensor(out=t1[:, 0:n], in0=kp[:, 0, 0:n], scalar=b2[:, 0:1], in1=rope[:, 0, 0:n],
                                         op0=ALU.add, op1=ALU.mult).then_inc(tsum, 1)
                dve.scalar_tensor_tensor(out=t2[:, 0:n], in0=kp[:, 1, 0:n], scalar=b2[:, 1:2], in1=rope[:, 1, 0:n],
                                         op0=ALU.add, op1=ALU.mult).then_inc(tsum, 1)
                dve.wait_ge(tsum, i * 4 + 2 * g + 4)
                dve.tensor_tensor(ck[:, g, 0:n], t1[:, 0:n], t2[:, 0:n], ALU.add).then_inc(k_free, 1)
                dve.wait_ge(k_free, i * 2 + g + 2)

            def body(i, halves, n, following):
                for what, k in steps(halves, following):
                    if what == "turn":
                        c, t0, n0 = piece(k)
                        w = halves[k // 8]
                        part = (slice(None), c, slice(t0, t0 + 4), slice(n0, n0 + w))
                        dve.wait_ge(high, 16 * i + k + 1)
                        dve.tensor_tensor(xl[part], bank[k % 4][:, :, 0:w], xh[part], ALU.subtract).then_inc(free, 1)
                    elif what == "shuffle":
                        shuffle(dve, dve.tensor_copy, (0, 1), i + 1, k, following[k], shuffled_v)
                    else:
                        if k >= 2:
                            keys(i, k - 2, n)
                        dve.wait_ge(hid_psum, 4 * i + k + 1)
                        wait(dve, hid_ready, 4 * i + k - 1)
                        dve.tensor_copy(raw[k % 2][:, 0:n], hp[k % 2][:, 0, 0:n]).then_inc(added, 1)
                        dve.wait_ge(added, 4 * i + k + 1)
                        dve.tensor_tensor(raw[k % 2][:, 0:n], raw[k % 2][:, 0:n], hp[k % 2][:, 1, 1:n + 1],
                                          ALU.add).then_inc(raw_ready, 1)
                wait(dve, out_done[1], i * 32)
                for g in range(NG):
                    dve.wait_ge(v_psum, i * 2 + g + 1)
                    for h in range(len(halves)):
                        w = min(P, n - h * P)
                        last = dve.tensor_tensor(cv[0:w, h, g, :], vp[0:w, h, :], b2v[0:w, :], ALU.add)
                    last.then_inc(v_free, 1)

            body(0, (P, P), NCMP, (P, P))
            with dve.Fori(1, NB - 1) as i:
                body(i, (P, P), NCMP, (P, P))
            body(NB - 1, (P, P), NCMP, (PCH,))
            body(NB, (PCH,), PCH - 1, ())

        @block.tensor
        def _(pe):
            pe.wait_ge(const_in, 16 * NCONST)
            for c in range(2):
                for t in range(16):
                    last = pe.matmul(hp[0][:, 0, c:c + 1], w1[:, 16 * c + t, :], pos[:, 16 * c + t:16 * c + t + 1],
                                     start=(t == 0), stop=(t == 15))
            last.then_inc(bias_psum, 1)
            pe.wait_ge(bias_ready, 1)
            pe.wait_ge(w2r_ready, 1)
            pe.wait_ge(w_split, 1)

            def body(i, halves, n):
                def second(c):
                    pe.wait_ge(hid_ready, i * 4 + c + 1)
                    if c < 2:
                        pe.wait_ge(k_free, i * 2 + c + 1)
                        pe.matmul(kp[:, 0, 0:n], w2[:, 0, :], hid[:, c, 0:n], start=True, stop=True)
                        pe.matmul(kp[:, 1, 0:n], w2r[:, :], hid[:, c, 0:n], start=True, stop=True).then_inc(k_psum, 1)
                    else:
                        pe.wait_ge(v_free, i * 2 + c - 1)
                        for h in range(len(halves)):
                            w = min(P, n - h * P)
                            last = pe.matmul(vp[0:w, h, :], hid[:, c, h * P:h * P + w], w2[:, 1, :], start=True, stop=True)
                        last.then_inc(v_psum, 1)

                for what, k in steps(halves, ()):
                    h = k // 8
                    if what == "turn":
                        w = halves[h]
                        c, t0, n0 = piece(k)
                        if k % 8 == 0:
                            pe.wait_ge(shuffled_v, i * 2 + h + 1)
                            pe.wait_ge(shuffled_a, i * 2 + h + 1)
                        pe.wait_ge(free, 16 * i + k + 1)
                        for r in range(4):
                            pair = xs[h][0:w, c, 2 * (t0 + r):2 * (t0 + r) + 2, :].rearrange("p l d -> p (l d)")
                            last = pe.transpose(bank[k % 4][:, r, 0:w], pair, ident[0:w, 0:w])
                        last.then_inc(turned, 1)
                    else:
                        cols = len(halves) * halves[0]
                        pe.wait_ge(free, 16 * i + 8 * len(halves) + 2 * k - 2)
                        wait(pe, raw_ready, 4 * i + k - 1)
                        for r in range(2):
                            for t in range(8):
                                w = 16 * (k // 2) + 8 * r + t
                                for m, (lhs, rhs) in enumerate(((wh, xh), (wl, xh), (wh, xl))):
                                    last = pe.matmul(hp[k % 2][:, r, 0:cols], lhs[:, w, :], rhs[:, k, t, 0:cols],
                                                     start=(t == 0 and m == 0), stop=(t == 7 and m == 2))
                        last.then_inc(hid_psum, 1)
                        if k:
                            second(k - 1)
                second(3)

            body(0, (P, P), NCMP)
            with pe.Fori(1, NB) as i:
                body(i, (P, P), NCMP)
            body(NB, (PCH,), PCH - 1)


class SampleInputs:
    NR, NP_, NKV, NSEL = NB * NH, NB * NG, 4, 64

    def __init__(self, s):
        NR, NP_ = self.NR, self.NP_
        self.ident = s.sb("ident", [P, P])
        self.q = s.sb("q", [NR, 2, HD])
        self.new = s.sb("new", [NR, 2, 2, HD])
        self.gate = s.sb("gate", [NR, 3])
        self.cw = s.sb("cw", [P, NB, 4, 4 * HD])
        self.kvs = s.sb("kvs", [P, self.NKV, 8 * 4 * HD])
        self.tri = self.kvs[0:NP_, 0:2, :].rearrange("p i c -> p (i c)").rearrange("p (n m) -> p n m", n=self.NSEL)
        self.member = s.sb("member", [NR, NP_])
        self.slots = s.sb("slots", [NP_, 16])
        self.ptr = s.sb("ptr", [NP_, NPAGE], I32)
        self.half8 = s.sb("half8", [NP_, 2])
        self.ones = s.sb("ones", [NP_, P])
        self.p8 = s.sb("p8", [P, 1])
        self.slot8 = s.sb("slot8", [P, 16])
        self.const_in = s.sem("const_in")
        self.row_in = s.sem("row_in")
        self.cw_in = s.sem("cw_in")

    def load(self, nc, a, sp):
        NR, NP_, NSEL = self.NR, self.NP_, self.NSEL
        for c in range(2):
            sp.dma_start(self.q[:, c, :], a["s_z"][T:NTOK, 0:512].rearrange("b (h d) -> b h d", d=HD)).then_inc(self.row_in, 16)
        with nc.allow_non_contiguous_dma(reason="gates of a row"):
            for k in range(3):
                sp.dma_start(self.gate[:, k:k + 1], a["s_z"][T:NTOK, GO + 8 * k:GO + 8 * k + 8].rearrange("b (h o) -> b h o", o=1)
                             ).then_inc(self.row_in, 16)
        for b in range(NB):
            for g in range(NG):
                src = a["s_z"][T + b:T + b + 1, SO:SO + 512].rearrange("o (n g d) -> o n g d", g=NG, d=HD)[:, :, g, :]
                r = (b * NG + g) * QG
                sp.dma_start(self.new[r:r + QG, :, :, :].rearrange("p a b d -> p (a b) d"),
                             src.to_broadcast([QG, 4, HD])).then_inc(self.row_in, 16)
        sp.dma_start(self.ident[:, :], a["c_ident"]).then_inc(self.const_in, 16)
        sp.dma_start(self.member[:, :], a["c_member"]).then_inc(self.const_in, 16)
        sp.dma_start(self.tri, a["c_tri64"].to_broadcast([NP_, NSEL, NSEL])).then_inc(self.const_in, 16)
        sp.dma_start(self.slots[:, :], a["c_iota"][:, 0:16].to_broadcast([NP_, 16])).then_inc(self.const_in, 16)
        sp.dma_start(self.half8[:, :], a["c_half8"].to_broadcast([NP_, 2])).then_inc(self.const_in, 16)
        sp.dma_start(self.p8[:, :], a["c_mod8"]).then_inc(self.const_in, 16)
        sp.dma_start(self.slot8[:, :], a["c_slot8"]).then_inc(self.const_in, 16)
        sp.dma_start(self.ones[:, :], a["c_ones"][0:NP_, :]).then_inc(self.const_in, 16)
        for g in range(NG):
            sp.dma_start(self.ptr[g:NP_:NG, :], a["page_table"]).then_inc(self.const_in, 16)
        for b in range(NB):
            sp.dma_start(self.cw[:, b, :, :], a["cache_win_kv"][0, b].rearrange("(t p) k g d -> p t (k g d)", p=P)
                         ).then_inc(self.cw_in, 16)


SEL, WIN, CMP = range(3)


def score_chunks(i):
    out = []
    for h in range(NH):
        for k0 in range(0, (i + 1) * P, 512):
            out.append((SEL, h, k0, min(512, (i + 1) * P - k0)))
        j0 = max(0, i - 4) * P
        for k0 in range(j0, (i + 1) * P, 512):
            out.append((WIN, h, k0, min(512, (i + 1) * P - k0)))
        out.append((CMP, h, 0, min(T // 16 - 1, 8 * i + 7)))
    return out


def key_tiles(i):
    out = []
    for br in (CMP, SEL, WIN):
        for g in range(NG):
            tiles = {SEL: range(i + 1), WIN: range(max(0, i - 4), i + 1), CMP: range(1)}[br]
            out.append((br, g, list(tiles)))
    return out


def stage_prompt_attention(nc, a, sample):
    banks = [("k", br, g, half) for br in (SEL, WIN) for g in range(NG) for half in range(2)]
    first_of = []
    for i in range(NT):
        first_of.append(len(banks))
        banks += [("q", i, half) for half in range(2)]
        banks += [("s", i) + c for c in score_chunks(i)]
        banks += [("m", i)]
    first_of.append(len(banks))
    tiles, groups, tile_of, group_of = [], [], [], []
    for i in range(NT):
        tile_of.append(len(tiles))
        group_of.append(len(groups))
        for br, g, js in key_tiles(i):
            for j in js:
                masked = br == CMP or j == i or (br == WIN and j == i - 4)
                tiles.append((i, br, g, j, len(groups), j == js[0], j == js[-1], masked))
            groups.append((i, br, g))
    tile_of.append(len(tiles))
    group_of.append(len(groups))
    masks_before = [sum(t[7] for t in tiles[:n]) for n in range(len(tiles) + 1)]
    NSP, NST, NPT = 3, 2, 4
    NMR = 32 + 3 * NH
    order = [("fill", n) for n in range(first_of[0])]
    for step in range(NT + 1):
        fills = list(range(first_of[step], first_of[step + 1])) if step < NT else []
        lo, hi = (tile_of[step - 1], tile_of[step]) if step else (0, 0)
        order += [("fill", n) for n in fills[:4]]
        body, last_fill = fills[4:-1], fills[-1:]
        spread, done, backs = max(1, hi - lo - 2), 0, []
        for n in range(lo, hi + 2):
            if n < hi:
                order.append(("scores", n))
            if n - 2 >= lo:
                order.append(("values", n - 2))
                if tiles[n - 2][6]:
                    backs.append((n + 2, tiles[n - 2][4]))
            while backs and backs[0][0] <= n:
                order.append(("back", backs.pop(0)[1]))
            upto = min(len(body), len(body) * (n - lo + 1) // spread)
            order += [("fill", b) for b in body[done:upto]]
            done = max(done, upto)
        order += [("fill", b) for b in body[done:]]
        order += [("back", grp) for _, grp in backs]
        order += [("fill", n) for n in last_fill]

    with Scope(nc, "att") as s:
        ident = s.sb("ident", [P, P])
        zk = s.sb("zk", [P, NT, 2, NG, 2 * HD])
        zv = s.sb("zv", [P, NT, 2, NG * HD])
        kT = [s.sb(f"kT{br}", [2 * HD, NG, T], F32R) for br in range(2)]
        ckt = s.sb("ckt", [2 * HD, NG, T // 16])
        ckT = s.sb("ckT", [2 * HD, NG, T // 16], F32R)
        va = s.sb("va", [P, NT, 2, NG, HD + 1])
        cv = s.sb("cv", [T // 16, NG * HD])
        cva = s.sb("cva", [T // 16, NG, HD + 1])
        q = [s.sb(f"q{i}", [P, NH, 2 * HD]) for i in range(2)]
        gate = s.sb("gate", [P, NT, 24])
        qh = [s.sb(f"qh{i}", [2 * HD, NH, P], F32R) for i in range(2)]
        ql = [s.sb(f"ql{i}", [2 * HD, NH, P], F32R) for i in range(2)]
        pick = s.sb("pick", [NMR, 3 * NH, P], F32R)
        diag = s.sb("diag", [P, P])
        far = s.sb("far", [P, P])
        cmask = s.sb("cmask", [P, 64])
        valid = s.sb("valid", [P, 1])
        masked = s.sb("masked", [P, 4, 2, P])
        cand = s.sb("cand", [P, 24, 4])
        mx = s.sb("mx", [P, 24])
        negm = s.sb("negm", [P, NMR])
        nmT = [s.sb(f"nmT{i}", [NMR, P], F32R) for i in range(2)]
        pT = [s.sb(f"pT{i}", [P, QG, P]) for i in range(NPT)]
        ot = [s.sb(f"ot{i}", [HD + 1, QG, P]) for i in range(2)]
        den = s.sb("den", [P, QG, 1])
        part = s.sb("part", [P, QG, HD])
        acc = [s.sb(f"acc{i}", [P, NH, HD]) for i in range(2)]
        sp_ = [s.ps(f"sp{i}", [P, 512]) for i in range(NSP)]
        st = [s.ps(f"st{i}", [P, 512]) for i in range(NST)]
        op = [s.ps(f"op{i}", [HD + 1, 512]) for i in range(2)]
        ob = s.ps("ob", [P, QG, HD + 1])

        zero = s.sb("zero", [P, D])

        const_in = s.sem("const_in")
        yb_out = s.sem("yb_out")
        k_in = s.sem("k_in")
        kv_in = s.sem("kv_in")
        q_in = [s.sem(f"q_in{i}") for i in range(2)]
        ready = s.sem("ready")
        bank_full = s.sem("bank_full")
        bank_free = s.sem("bank_free")
        neg_ready = s.sem("neg_ready")
        vch = s.sem("vch")
        st_full = s.sem("st_full")
        exp_done = s.sem("exp_done")
        mask_done = s.sem("mask_done")
        pv_done = s.sem("pv_done")
        ot_ready = s.sem("ot_ready")
        ob_full = s.sem("ob_full")
        ob_free = s.sem("ob_free")
        acc_done = s.sem("acc_done")
        att_out = [s.sem(f"att_out{i}") for i in range(2)]
        split = s.sem("split")
        block = s.block()
        NKV_IN = 6

        @block.sync
        def _(sp):
            def load_q(i):
                for c in range(2):
                    sp.dma_start(q[i % 2][:, :, c * HD:(c + 1) * HD],
                                 a["s_z"][i * P:(i + 1) * P, 0:512].rearrange("t (h d) -> t h d", d=HD)
                                 ).then_inc(q_in[i % 2], 16)

            sp.dma_start(ident[:, :], a["c_ident"]).then_inc(k_in, 16)
            for br in range(2):
                for g in range(NG):
                    at = SO + 256 * br + g * HD
                    for c in range(2):
                        sp.dma_start(zk[:, :, br, g, c * HD:(c + 1) * HD],
                                     a["s_z"][0:T, at:at + HD].rearrange("(t p) d -> p t d", p=P)).then_inc(k_in, 16)
            load_q(0)
            for br in range(2):
                at = SO + 256 * br + 128
                sp.dma_start(zv[:, :, br, :], a["s_z"][0:T, at:at + 128].rearrange("(t p) n -> p t n", p=P)).then_inc(kv_in, 16)
            for c in range(2):
                sp.dma_start(ckt[c * HD:(c + 1) * HD, :, 0:T // 16 - 1], a["s_ck"][NB, :, :, 0:T // 16 - 1]).then_inc(kv_in, 16)
            sp.dma_start(cv[0:T // 16 - 1, :], a["s_cv"][NB, 0:T // 16 - 1, :]).then_inc(kv_in, 16)
            sp.dma_start(gate[:, :, :], a["s_z"][0:T, GO:GO + 24].rearrange("(t p) n -> p t n", p=P)).then_inc(kv_in, 16)
            load_q(1)
            sp.dma_start(diag[:, :], a["c_diag"]).then_inc(const_in, 16)
            sp.dma_start(far[:, :], a["c_far"]).then_inc(const_in, 16)
            sp.dma_start(cmask[:, :], a["c_cmask"]).then_inc(const_in, 16)
            sp.dma_start(valid[:, :], a["c_valid"]).then_inc(const_in, 16)
            sample.load(nc, a, sp)
            sp.wait_ge(ready, 3)
            for b in range(NE, NBLK):
                sp.dma_start(a["s_yb"][b * P:(b + 1) * P, :], zero[:, :]).then_inc(yb_out, 16)
            for i in range(NT):
                sp.wait_ge(bank_free, first_of[i + 1])
                if i + 2 < NT:
                    load_q(i + 2)
                if i >= 1:
                    sp.wait_ge(acc_done, i)
                    sp.dma_start(a["s_attn"][(i - 1) * P:i * P, :], acc[(i - 1) % 2][:, :, :].rearrange("p h d -> p (h d)")
                                 ).then_inc(att_out[(i - 1) % 2], 16)
            sp.wait_ge(acc_done, NT)
            sp.dma_start(a["s_attn"][T - P:T, :], acc[(NT - 1) % 2][:, :, :].rearrange("p h d -> p (h d)")
                         ).then_inc(att_out[(NT - 1) % 2], 16)
            sp.wait_ge(yb_out, 16 * NOV)
            sp.wait_ge(att_out[0], 16 * (NT // 2))
            sp.wait_ge(att_out[1], 16 * (NT // 2))

        @block.gpsimd
        def _(pool):
            ones = Chain(pool, ready)
            ones(pool.memset(va[:, :, :, :, HD:HD + 1], 1.0))
            ones(pool.memset(cva[:, :, HD:HD + 1], 1.0))
            ones(pool.memset(zero[:, :], 0.0))
            for what, n in order:
                if what == "scores" and tiles[n][7]:
                    i, br, g, j, grp, first, final, is_masked = tiles[n]
                    pool.wait_ge(exp_done, n + 1)
                    rows = min(T // 16 - 1, 8 * i + 7) if br == CMP else P
                    pt = pT[n % NPT][0:rows, :, :]
                    if br == CMP:
                        base, mult, sgn = i * P - 31, -16, 1
                    elif j == i:
                        base, mult, sgn = 0, -1, 1
                    else:
                        base, mult, sgn = 0, 1, -1
                    pool.affine_select(out=pt, in_=pt, compare_op=ALU.is_ge, fill=0.0, base=base,
                                       pattern=[[0, QG], [sgn, P]], channel_multiplier=mult).then_inc(mask_done, 1)

        @block.scalar
        def _(act):
            for what, n in order:
                if what == "scores":
                    i, br = tiles[n][0:2]
                    rows = min(T // 16 - 1, 8 * i + 7) if br == CMP else P
                    act.wait_ge(st_full, n + 1)
                    if n >= NPT:
                        act.wait_ge(pv_done, n - NPT + 1)
                    act.activation(pT[n % NPT][0:rows, :, :].rearrange("p h q -> p (h q)"), st[n % NST][0:rows, :],
                                   ACT.Exp).then_inc(exp_done, 1)
                elif what == "values" and tiles[n][6]:
                    grp = tiles[n][4]
                    act.wait_ge(pv_done, n + 1)
                    if grp >= 2:
                        act.wait_ge(ob_full, grp - 1)
                    act.activation(ot[grp % 2][:, :, :].rearrange("p h q -> p (h q)"), op[grp % 2][:, :], ACT.Copy
                                   ).then_inc(ot_ready, 1)

        @block.tensor
        def _(pe):
            pe.wait_ge(k_in, 16 * 9)

            def fill(n):
                b = banks[n]
                dst = sp_[n % NSP]
                if n >= NSP:
                    pe.wait_ge(bank_free, n - NSP + 1)
                if b[0] == "k":
                    _, br, g, half = b
                    for t in range(4):
                        last = pe.transpose(dst[:, t * P:(t + 1) * P], zk[:, half * 4 + t, br, g, :], ident[:, :])
                elif b[0] == "q":
                    _, i, half = b
                    if half == 0:
                        pe.wait_ge(q_in[i % 2], 32 * (i // 2 + 1))
                    for t in range(4):
                        h = half * 4 + t
                        last = pe.transpose(dst[:, t * P:(t + 1) * P], q[i % 2][:, h, :], ident[:, :])
                elif b[0] == "s":
                    _, i, br, h, k0, w = b
                    keys = ckT if br == CMP else kT[br]
                    if n < first_of[i] + 4:
                        pe.wait_ge(bank_free, first_of[i] + 2)
                    if n == first_of[0] + 2:
                        pe.wait_ge(split, 2)
                    w += w % 2
                    pe.matmul(dst[:, 0:w], qh[i % 2][:, h, :], keys[:, h // QG, k0:k0 + w], start=True, stop=False)
                    last = pe.matmul(dst[:, 0:w], ql[i % 2][:, h, :], keys[:, h // QG, k0:k0 + w], start=False, stop=True)
                else:
                    pe.wait_ge(neg_ready, b[1] + 1)
                    last = pe.transpose(dst[0:NMR, 0:P], negm[:, :], ident[:, :])
                last.then_inc(bank_full, 1)

            def turn_back(grp):
                pe.wait_ge(ot_ready, grp + 1)
                if grp:
                    pe.wait_ge(ob_free, grp)
                for h in range(QG):
                    last = pe.transpose(ob[:, h, :], ot[grp % 2][:, h, :], ident[0:HD + 1, 0:HD + 1])
                last.then_inc(ob_full, 1)

            def scores(n):
                i, br, g, j, grp, first, final, is_masked = tiles[n]
                if n >= NST:
                    pe.wait_ge(exp_done, n - NST + 1)
                if br == CMP:
                    rows = 8 * i + 8
                    lhs = ckT[:, g, 0:rows]
                else:
                    rows = P
                    lhs = kT[br][:, g, j * P:(j + 1) * P]
                heads = slice(QG * g, QG * g + QG)
                pe.matmul(st[n % NST][0:rows, :], lhs, qh[i % 2][:, heads, :], start=True, stop=False)
                pe.matmul(st[n % NST][0:rows, :], lhs, ql[i % 2][:, heads, :], start=False, stop=False)
                for h in range(QG):
                    last = pe.matmul(st[n % NST][0:rows, h * P:(h + 1) * P], pick[:, br * NH + QG * g + h, 0:rows],
                                     nmT[i % 2][:, :], start=False, stop=(h == QG - 1))
                last.then_inc(st_full, 1)

            def values(n):
                i, br, g, j, grp, first, final, is_masked = tiles[n]
                pe.wait_ge(exp_done, n + 1)
                if is_masked:
                    pe.wait_ge(mask_done, masks_before[n + 1])
                if first and grp >= 2:
                    pe.wait_ge(ot_ready, grp - 1)
                if br == CMP:
                    rows = min(T // 16 - 1, 8 * i + 7)
                    lhs = cva[0:rows, g, :]
                else:
                    rows = P
                    lhs = va[:, j, br, g, :]
                mm = pe.matmul(op[grp % 2][:, :], lhs, pT[n % NPT][0:rows, :, :], start=first, stop=final)
                mm.then_inc(pv_done, 1)

            for what, n in order:
                if what == "fill":
                    fill(n)
                elif what == "scores":
                    i = tiles[n][0]
                    if n == tile_of[i]:
                        pe.wait_ge(bank_free, first_of[i + 1])
                    scores(n)
                elif what == "values":
                    values(n)
                else:
                    turn_back(n)

        @block.vector
        def _(dve):
            step_ = Chain(dve, vch)
            def split_keys(dst, src):
                step_(dve.tensor_copy(dst[:, :], src[:, :]))
                return dve.tensor_tensor(dst[HD:2 * HD, :], src[HD:2 * HD, :], dst[HD:2 * HD, :], ALU.subtract)

            def prepare():
                dve.wait_ge(const_in, 64)
                dve.wait_ge(kv_in, 16 * NKV_IN)
                dve.wait_ge(ready, 2)
                for br in range(2):
                    step_(dve.tensor_copy(va[:, :, br, :, 0:HD], zv[:, :, br, :].rearrange("p t (g d) -> p t g d", g=NG)))
                step_(dve.tensor_copy(cva[0:T // 16 - 1, :, 0:HD], cv[0:T // 16 - 1, :].rearrange("p (g d) -> p g d", g=NG)))
                step_(dve.memset(cand[:, :, :], -3e38))
                step_(dve.memset(negm[:, :], 0.0))
                one_of = [ident[0:NMR, c:c + 3 * NH].rearrange("p (n o) -> p n o", o=1).to_broadcast([NMR, 3 * NH, P])
                          for c in (0, 32)]
                dve.tensor_tensor(pick[:, :, :], one_of[0], one_of[1], ALU.add).then_inc(split, 1)
                step_(dve.memset(ckt[:, :, T // 16 - 1:], 0.0))
                for g in range(NG):
                    last = split_keys(ckT[:, g, :], ckt[:, g, :])
                last.then_inc(split, 1)

            def empty(n):
                b = banks[n]
                src = sp_[n % NSP]
                dve.wait_ge(bank_full, n + 1)
                if b[0] == "k":
                    _, br, g, half = b
                    last = split_keys(kT[br][:, g, half * 512:(half + 1) * 512], src)
                elif b[0] == "q":
                    _, i, half = b
                    h4, l4 = (x[i % 2][:, half * 4:half * 4 + 4, :].rearrange("p h q -> p (h q)") for x in (qh, ql))
                    step_(dve.tensor_copy(h4, src[:, :]))
                    last = dve.tensor_tensor(l4, src[:, :], h4, ALU.subtract)
                elif b[0] == "s":
                    _, i, br, h, k0, w = b
                    col = cand[:, br * NH + h, :]
                    c = 0
                    if br == CMP:
                        spans = [(0, w, cmask[:, 57 - 8 * i:57 - 8 * i + w])]
                    else:
                        spans = []
                        lo, hi = 0, w
                        if br == WIN and i >= 4 and k0 == (i - 4) * P:
                            spans.append((0, P, far[:, :]))
                            lo = P
                        if k0 + w == (i + 1) * P:
                            spans.append((w - P, w, diag[:, :]))
                            hi = w - P
                        if hi > lo:
                            spans.append((lo, hi, None))
                    base = 2 if br == SEL and k0 or (br == WIN and i >= 4 and k0 > (i - 4) * P) else 0
                    dve.wait_ge(bank_free, n - 3)
                    for x0, x1, m in spans:
                        if m is None:
                            last = dve.tensor_reduce(col[:, base + c:base + c + 1], src[:, x0:x1], AX, ALU.max)
                        else:
                            last = dve.tensor_tensor_reduce(masked[:, n % 4, c % 2, 0:x1 - x0], src[:, x0:x1], m, 1.0, -3e38,
                                                            ALU.add, ALU.max, col[:, base + c:base + c + 1])
                        c += 1
                else:
                    nm = nmT[b[1] % 2]
                    step_(dve.tensor_copy(nm[:, :], src[0:NMR, 0:P]))
                    last = dve.tensor_tensor(nm[32:NMR, :], src[32:NMR, 0:P], nm[32:NMR, :], ALU.subtract)
                last.then_inc(bank_free, 1)

            def combine(grp):
                i, br, g = groups[grp]
                dve.wait_ge(ob_full, grp + 1)
                step_(dve.tensor_scalar(den[:, :, :], ob[:, :, HD:HD + 1], 1e-30, None, ALU.max))
                step_(dve.reciprocal(den[:, :, :], den[:, :, :]))
                kind = {CMP: 0, SEL: 1, WIN: 2}[br]
                w = gate[:, i, kind * NH + g * QG:kind * NH + (g + 1) * QG].rearrange("p (h o) -> p h o", o=1)
                step_(dve.tensor_tensor(den[:, :, :], den[:, :, :], w, ALU.mult))
                dst = acc[i % 2][:, g * QG:(g + 1) * QG, :]
                if br == CMP:
                    if i >= 2 and g == 0:
                        dve.wait_ge(att_out[i % 2], 16 * (i // 2))
                    dve.tensor_tensor(dst, ob[:, :, 0:HD], den[:, :, :].to_broadcast([P, QG, HD]), ALU.mult).then_inc(ob_free, 1)
                    dve.wait_ge(ob_free, grp + 1)
                else:
                    dve.tensor_tensor(part[:, :, :], ob[:, :, 0:HD], den[:, :, :].to_broadcast([P, QG, HD]),
                                      ALU.mult).then_inc(ob_free, 1)
                    dve.wait_ge(ob_free, grp + 1)
                    if br == WIN and g == NG - 1:
                        dve.tensor_tensor(dst, dst, part[:, :, :], ALU.add).then_inc(acc_done, 1)
                        dve.wait_ge(acc_done, i + 1)
                    else:
                        step_(dve.tensor_tensor(dst, dst, part[:, :, :], ALU.add))

            for what, n in order:
                if what == "fill":
                    if n == first_of[0]:
                        prepare()
                    if banks[n][0] == "m":
                        step = banks[n][1]
                        dve.wait_ge(bank_free, n)
                        step_(dve.tensor_reduce(mx[:, :], cand[:, :, :], AX, ALU.max))
                        step_(dve.memset(cand[:, :, :], -3e38))
                        if step == 0:
                            step_(dve.tensor_scalar(mx[:, CMP * NH:], mx[:, CMP * NH:], valid[:, 0:1], None, ALU.mult))
                        step_(dve.tensor_scalar(negm[:, 0:3 * NH], mx[:, :], -1.0, None, ALU.mult))
                        dve.tensor_scalar(negm[:, 32:NMR], mx[:, :], -1.0, None, ALU.mult).then_inc(neg_ready, 1)
                    empty(n)
                elif what == "back":
                    combine(n)


def stage_sample_attention(nc, a, given):
    NR = NB * NH
    NP_ = NB * NG
    NW = 512
    NS = NSB * 64
    NSEL = 64
    NKV = 4
    widths = (NCMP, NS, NW)
    SP = NSB * 8
    tile_rows = (P, SP, P)
    spans = tuple([(c, min(r, n - c)) for c in range(0, n, r)] for n, r in zip(widths, tile_rows))
    C_, S_, W_ = range(3)
    with Scope(nc, "smp") as s:
        ident, member, slots, half8, p8, slot8, ones, ptr = (given.ident, given.member, given.slots, given.half8,
                                                             given.p8, given.slot8, given.ones, given.ptr)
        q, new, gate, cw, kvs = given.q, given.new, given.gate, given.cw, given.kvs
        const_in, row_in, cw_in = given.const_in, given.row_in, given.cw_in
        qseq = s.sb("qseq", [2 * HD, NB * (NR + 2 * QG)])
        qblk = s.sb("qblk", [HD, NP_ * (NR + QG)])
        ck = [s.sb(f"ck{i}", [NG * HD, NCMP]) for i in range(2)]
        cv = s.sb("cv", [P, NB, 2, NG * HD])
        kv = [kvs[:, i, :].rearrange("p (t c) -> p t c", c=4 * HD) for i in range(NKV)]
        vs = s.sb("vs", [P, NP_, 8, HD])
        kT = [s.sb(f"kT{i}", [NG * HD, 8 * P]) for i in range(2)]
        pr = [s.sb(f"pr{i}", [NR, n]) for i, n in enumerate(widths)]
        pT = s.sb("pT", [P, 8, NR])
        pn = s.sb("pn", [NR, NCMP])
        stat = s.sb("stat", [NR, 3, 8])
        prod = s.sb("prod", [NR, HD])
        imp = s.sb("imp", [NP_, 264])
        sc = s.sb("sc", [NP_, 65])
        bigs = vs[0:NP_, :, :, :].rearrange("p u t d -> p (u t d)")
        big1, big2 = (bigs[:, i * NSEL * NSEL:(i + 1) * NSEL * NSEL].rearrange("p (n m) -> p n m", n=NSEL)
                      for i in range(2))
        tri = kvs[0:NP_, 0:2, :].rearrange("p i c -> p (i c)").rearrange("p (n m) -> p n m", n=NSEL)
        cT = s.sb("cT", [P, KT, 9])
        ones9 = s.sb("ones9", [1, 9])
        wa = [s.sb(f"wa{i}", [P, KT, 512]) for i in range(2)]
        ba = [s.sb(f"ba{i}", [1, 512]) for i in range(2)]
        mrow = [s.sb(f"mrow{i}", [9, 512]) for i in range(2)]
        rank = s.sb("rank", [NP_, NSEL])
        base = s.sb("base", [NP_, NPAGE, 2])
        slotb = s.sb("slotb", [NP_, 16])
        spread = s.sb("spread", [NP_, NP_, 16])
        chosen = s.sb("chosen", [P, NP_, 16])
        idxf = s.sb("idxf", [P, NP_])
        idx = s.sb("idx", [P, NP_], U32)
        oT = s.sb("oT", [HD, 3, NR])
        o = s.sb("o", [NR, 3, HD])
        A = [s.ps(f"A{i}", [NG * HD, 4, P]) for i in range(2)]
        SC = s.ps("SC", [NR, 512])
        SW = s.ps("SW", [NR, 512])
        SS = [s.ps(f"SS{i}", [NR, 512]) for i in range(2)]
        O = s.ps("O", [HD, 3, NR])
        M = s.ps("M", [P, 512])

        ck_in = [s.sem(f"ck_in{i}") for i in range(2)]
        cv_in = s.sem("cv_in")
        q_turned = s.sem("q_turned")
        qblk_ready = s.sem("qblk_ready")
        c_read = s.sem("c_read")
        keys_full = s.sem("keys_full")
        keys_v = s.sem("keys_v")
        keys_a = s.sem("keys_a")
        keys_read = s.sem("keys_read")
        neg_ready = [s.sem(f"neg_ready{i}") for i in range(3)]
        probs = [s.sem(f"probs{i}") for i in range(3)]
        pn_ready = s.sem("pn_ready")
        imp_psum = s.sem("imp_psum")
        spread_ready = s.sem("spread_ready")
        idx_psum = s.sem("idx_psum")
        idx_ready = s.sem("idx_ready")
        kv_in = [s.sem(f"kv_in{i}") for i in range(NKV)]
        v_kept = s.sem("v_kept")
        pT_psum = s.sem("pT_psum")
        pT_ready = s.sem("pT_ready")
        o_psum = s.sem("o_psum")
        oT_ready = s.sem("oT_ready")
        back_psum = s.sem("back_psum")
        cT_in = s.sem("cT_in")
        wa_in = [s.sem(f"wa_in{i}") for i in range(2)]
        ones_set = s.sem("ones_set")
        mod_psum = s.sem("mod_psum")
        mod_ready = s.sem("mod_ready")
        mod_out = [s.sem(f"mod_out{i}") for i in range(2)]
        vch = s.sem("vch")
        done = s.sem("done")
        out_done = s.sem("out_done")
        block = s.block()
        NROW = 5 + NP_
        MOD1 = 4
        mod_after = (3, 6, 9, 12)

        def mod_bank(m):
            return SC if m % 2 == 0 else SS[0] if m < MOD1 else SW

        def key_unit(pe, u, src, n_tiles, rows):
            for half in range(2):
                if u or half:
                    pe.wait_ge((keys_v, keys_a)[half], u)
                for t in range(n_tiles // 2):
                    tt = half * (n_tiles // 2) + t
                    keys = src(tt)
                    last = pe.transpose(A[half][0:keys.shape[1], t, 0:rows], keys, ident[0:rows, 0:rows])
                last.then_inc(keys_full, 1)

        @block.sync
        def _(sp):
            for b in range(NB):
                if b >= 2:
                    sp.wait_ge(c_read, b - 1)
                for g in range(NG):
                    sp.dma_start(ck[b % 2][g * HD:(g + 1) * HD, :], a["s_ck"][b, :, g, 0:NCMP]).then_inc(ck_in[b % 2], 16)
            for h, (c0, n) in enumerate(spans[C_]):
                sp.dma_start(cv[0:n, :, h, :], a["s_cv"][0:NB, c0:c0 + n, :].rearrange("b n c -> n b c")).then_inc(cv_in, 16)
            sp.dma_start(cT[:, :, :].rearrange("p k n -> p (k n)"), a["s_cT"]).then_inc(cT_in, 16)
            for m in range(ADA - ADA1):
                if m >= 2:
                    sp.wait_ge(mod_psum, m - 1)
                n = slice((ADA1 + m) * 512, (ADA1 + m + 1) * 512)
                sp.dma_start(wa[m % 2][:, :, :], a["w_ada"][0, :, n].rearrange("(k p) n -> p k n", p=P)
                             ).then_inc(wa_in[m % 2], 16)
                sp.dma_start(ba[m % 2][:, :], a["b_ada"][:, n]).then_inc(wa_in[m % 2], 16)
            sp.wait_ge(mod_out[0], 16 * (ADA - ADA1) // 2)
            sp.wait_ge(mod_out[1], 16 * (ADA - ADA1) // 2)
            sp.wait_ge(done, 1)
            sp.dma_start(a["s_attn"][T:NTOK, :].rearrange("b (h d) -> b h d", d=HD), o[:, 0, :]).then_inc(out_done, 16)
            sp.wait_ge(out_done, 16)

        @block.gpsimd
        def _(pool):
            rows = a["cache_sel_kv"][0].rearrange("n (r s) k g d -> (n r) (s k g d)", s=8)
            pool.wait_ge(idx_ready, 1)
            for u in range(NP_):
                if u >= NKV:
                    pool.wait_ge(v_kept, u - NKV + 1)
                    pool.wait_ge(keys_full, 2 * (NB + u - NKV + 1))
                pool.indirect_dma_start(kv[u % NKV][0:SP, :, :].rearrange("p t c -> p (t c)"), None, rows,
                                        bass.IndirectOffsetOnAxis(ap=idx[0:SP, u:u + 1], axis=0)
                                        ).then_inc(kv_in[u % NKV], 16)

        @block.tensor
        def _(pe):
            pe.wait_ge(const_in, 16 * 10)
            pe.wait_ge(row_in, 16 * NROW)
            pe.transpose(M[:, 0:NR], q[:, :, :].rearrange("p c d -> p (c d)"), ident[0:NR, 0:NR]).then_inc(q_turned, 1)
            pe.wait_ge(qblk_ready, 1)
            blk = [qblk[:, u * NR:(u + 1) * NR] for u in range(NP_)]
            seq = [qseq[:, b * NR:(b + 1) * NR] for b in range(NB)]
            for b in range(NB):
                pe.wait_ge(ck_in[b % 2], 32 * (b // 2 + 1))
                pe.matmul(SC[:, 0:NCMP], seq[b], ck[b % 2][:, :], start=(b == 0), stop=(b == NB - 1)).then_inc(c_read, 1)
            pe.wait_ge(pn_ready, 1)
            pe.matmul(M[0:NP_, 0:NCMP], member[:, :], pn[:, :], start=True, stop=True).then_inc(imp_psum, 1)
            pe.wait_ge(cw_in, 16 * NB)

            def score_unit(u, out, width):
                pe.wait_ge(keys_v, u + 1)
                pe.wait_ge(keys_a, u + 1)
                rows, lhs, first, final = ((NG * HD, seq[u], u == 0, u == NB - 1) if u < NB else
                                           (HD, blk[u - NB], u == NB, u == NB + NP_ - 1))
                w = width // len(out)
                for j, bank in enumerate(out):
                    last = pe.matmul(bank[:, 0:w], lhs, kT[u % 2][0:rows, j * w:(j + 1) * w], start=first, stop=final)
                last.then_inc(keys_read, 1)

            def win_src(u):
                return lambda t: cw[:, u, t, 0:NG * HD]

            def sel_src(u):
                return lambda t: kv[u % NKV][0:SP, t, (u % NG) * HD:(u % NG + 1) * HD]

            for u in range(NB):
                key_unit(pe, u, win_src(u), 4, P)
                if u:
                    score_unit(u - 1, [SW], NW)
            score_unit(NB - 1, [SW], NW)

            def condition(m):
                bank = mod_bank(m)
                pe.wait_ge(wa_in[m % 2], 32 * (m // 2 + 1))
                if m >= 2:
                    pe.wait_ge(mod_ready, m - 1)
                for k in range(KT):
                    pe.matmul(bank[0:9, :], cT[:, k, :], wa[m % 2][:, k, :], start=(k == 0), stop=False)
                pe.matmul(bank[0:9, :], ones9[:, :], ba[m % 2][:, :], start=False, stop=True).then_inc(mod_psum, 1)

            pe.wait_ge(cT_in, 16)
            pe.wait_ge(ones_set, 1)
            condition(0)
            pe.wait_ge(spread_ready, 1)
            pe.matmul(M[:, 0:256], ones[:, :], spread[:, :, :].rearrange("p u s -> p (u s)"),
                      start=True, stop=True).then_inc(idx_psum, 1)
            for m in range(1, MOD1):
                condition(m)

            def values(k, br):
                pe.wait_ge(probs[br], 1)
                for i, (c0, n) in enumerate(spans[br]):
                    last = pe.transpose(M[0:n, i * NR:(i + 1) * NR], pr[br][:, c0:c0 + n], ident[0:NR, 0:NR])
                last.then_inc(pT_psum, 1)
                pe.wait_ge(pT_ready, k + 1)
                for u in range(NP_):
                    b, g = u // NG, u % NG
                    for i, (c0, n) in enumerate(spans[br]):
                        if br == C_:
                            v = cv[0:n, b, i, g * HD:(g + 1) * HD]
                        elif br == W_:
                            v = cw[0:n, b, i, 128 + g * HD:128 + (g + 1) * HD]
                        else:
                            v = vs[0:n, u, i, :]
                        last = pe.matmul(O[:, br, u * QG:(u + 1) * QG], v, pT[0:n, i, u * QG:(u + 1) * QG],
                                         start=(i == 0), stop=(i == len(spans[br]) - 1))
                last.then_inc(o_psum, 1)

            pe.wait_ge(idx_ready, 1)
            pe.wait_ge(cv_in, 32)
            values(0, C_)
            values(1, W_)
            for u in range(NP_):
                pe.wait_ge(kv_in[u % NKV], 16 * (u // NKV + 1))
                key_unit(pe, NB + u, sel_src(u), 8, SP)
                if u == 1:
                    pe.wait_ge(mod_ready, MOD1)
                if u:
                    score_unit(NB + u - 1, SS, NS)
                if u in mod_after:
                    condition(MOD1 + mod_after.index(u))
            score_unit(NB + NP_ - 1, SS, NS)
            pe.wait_ge(v_kept, NP_)
            values(2, S_)
            pe.wait_ge(oT_ready, 1)
            for br in range(3):
                last = pe.transpose(M[0:NR, br * HD:(br + 1) * HD], oT[:, br, :], ident[0:HD, 0:HD])
            last.then_inc(back_psum, 1)

        @block.scalar
        def _(act):
            def copy_keys(u, half):
                act.wait_ge(keys_full, 2 * u + 1 + half)
                if u >= 2:
                    act.wait_ge(keys_read, u - 1)
                rows = NG * HD if u < NB else HD
                n, k = (P, 2) if u < NB else (SP, 4)
                act.activation(kT[u % 2][0:rows, half * n * k:(half + 1) * n * k].rearrange("p (t n) -> p t n", n=n),
                               A[half][0:rows, 0:k, 0:n], ACT.Copy).then_inc((keys_v, keys_a)[half], 1)

            def exps(br, parts):
                act.wait_ge(neg_ready[br], 1)
                st = stat[:, br, :]
                c = 0
                for j, (src, w) in enumerate(parts):
                    last = act.activation(pr[br][:, c:c + w], src[:, 0:w], ACT.Exp, bias=st[:, 2:3],
                                          accum_out=st[:, 4 + j:5 + j])
                    c += w
                if br != C_:
                    last = act.activation(st[:, 3:4], st[:, 0:1], ACT.Exp, bias=st[:, 2:3])
                last.then_inc(probs[br], 1)

            exps(C_, [(SC, NCMP)])
            for u in range(NB):
                for half in range(2):
                    copy_keys(u, half)

            def keep_mod(m):
                act.wait_ge(mod_psum, m + 1)
                if m >= 2:
                    act.wait_ge(mod_out[m % 2], 16 * (m // 2))
                act.activation(mrow[m % 2][:, :], mod_bank(m)[0:9, :], ACT.Copy).then_inc(mod_ready, 1)
                act.wait_ge(mod_ready, m + 1)
                act.dma_start(a["s_mod"][:, (ADA1 + m) * 512:(ADA1 + m + 1) * 512], mrow[m % 2][:, :]
                              ).then_inc(mod_out[m % 2], 16)

            for m in range(MOD1):
                keep_mod(m)
            exps(W_, [(SW, NW)])
            for u in range(NP_):
                act.wait_ge(kv_in[u % NKV], 16 * (u // NKV + 1))
                last = act.activation(vs[0:SP, u, :, :], kv[u % NKV][0:SP, :, 128 + (u % NG) * HD:128 + (u % NG + 1) * HD],
                                      ACT.Copy)
                last.then_inc(v_kept, 1)
                copy_keys(NB + u, 1)
                if u in mod_after:
                    keep_mod(MOD1 + mod_after.index(u))
            exps(S_, [(SS[0], NS // 2), (SS[1], NS // 2)])

        @block.vector
        def _(dve):
            step = Chain(dve, vch)
            dve.memset(ones9[:, :], 1.0).then_inc(ones_set, 1)
            step(dve.memset(qblk[:, :], 0.0))
            step(dve.memset(qseq[:, :], 0.0))
            step(dve.memset(imp[:, :], 0.0))
            step(dve.memset(stat[:, :, :], 0.0))
            dve.wait_ge(q_turned, 1)
            for g in range(NG):
                r = slice(g * HD, (g + 1) * HD)
                step(dve.tensor_copy(qseq[r, :].rearrange("p (b w) -> p b w", w=NR + 2 * QG)[:, :, g * QG:(g + 1) * QG],
                                     M[r, 0:NR].rearrange("p (b w) -> p b w", w=2 * QG)[:, :, g * QG:(g + 1) * QG]))
            dve.tensor_copy(qblk[:, :].rearrange("p (u w) -> p u w", w=NR + QG)[:, :, 0:QG],
                            M[0:HD, 0:NR].rearrange("p (u w) -> p u w", w=QG)).then_inc(qblk_ready, 1)
            for br, k in ((S_, 0), (W_, 1)):
                step(dve.tensor_tensor(prod[:, :], q[:, 0, :], new[:, k, 0, :], ALU.mult))
                step(dve.tensor_reduce(stat[:, br, 0:1], prod[:, :], AX, ALU.add))

            def peak(br, parts):
                st = stat[:, br, :]
                c = 1
                for src, w in parts:
                    step(dve.tensor_reduce(st[:, c:c + 1], src[:, 0:w], AX, ALU.max))
                    c += 1
                if len(parts) == 2:
                    step(dve.tensor_tensor(st[:, 1:2], st[:, 1:2], st[:, 2:3], ALU.max))
                if br != C_:
                    step(dve.tensor_tensor(st[:, 1:2], st[:, 1:2], st[:, 0:1], ALU.max))
                dve.tensor_scalar(st[:, 2:3], st[:, 1:2], -1.0, None, ALU.mult).then_inc(neg_ready[br], 1)

            def copy_keys(u):
                dve.wait_ge(keys_full, 2 * u + 1)
                if u >= 2:
                    dve.wait_ge(keys_read, u - 1)
                dve.tensor_copy(kT[u % 2][0:HD, 0:4 * SP].rearrange("p (t n) -> p t n", n=SP), A[0][0:HD, :, 0:SP]
                                ).then_inc(keys_v, 1)

            dve.wait_ge(c_read, NB)
            peak(C_, [(SC, NCMP)])
            dve.wait_ge(probs[C_], 1)
            step(dve.reciprocal(stat[:, C_, 6:7], stat[:, C_, 4:5]))
            dve.tensor_scalar(pn[:, :], pr[C_][:, :], stat[:, C_, 6:7], None, ALU.mult).then_inc(pn_ready, 1)
            dve.wait_ge(imp_psum, 1)
            step(dve.tensor_copy(imp[:, 1:1 + NCMP], M[0:NP_, 0:NCMP]))
            quads = imp[:, :].rearrange("p (n r) -> p n r", r=4)
            step(dve.tensor_reduce(sc[:, :], quads[:, 0:65, :], AX, ALU.add))
            step(dve.tensor_tensor(sc[:, :], sc[:, :], quads[:, 1:66, 0], ALU.add))
            for j in (0, 63):
                step(dve.memset(sc[:, j:j + 1], 1e4))
            s_i = sc[:, 0:NSEL].rearrange("p (o n) -> p o n", o=1).to_broadcast([NP_, NSEL, NSEL])
            s_j = sc[:, 0:NSEL].rearrange("p (n o) -> p n o", o=1).to_broadcast([NP_, NSEL, NSEL])
            step(dve.tensor_tensor(big1[:, :, :], s_i, s_j, ALU.is_equal))
            step(dve.tensor_tensor(big1[:, :, :], big1[:, :, :], tri[:, :, :], ALU.mult))
            step(dve.tensor_tensor(big2[:, :, :], s_i, s_j, ALU.is_gt))
            step(dve.tensor_tensor(big1[:, :, :], big1[:, :, :], big2[:, :, :], ALU.add))
            step(dve.tensor_reduce(rank[:, :], big1[:, :, :], AX, ALU.add))
            for k in range(2):
                step(dve.tensor_scalar(base[:, :, k], ptr[:, :], 16.0, half8[:, k:k + 1], ALU.mult, ALU.add))
            r_j = rank[:, :].rearrange("p (o n) -> p o n", o=1).to_broadcast([NP_, 16, NSEL])
            slot = slots[:, :].rearrange("p (n o) -> p n o", o=1).to_broadcast([NP_, 16, NSEL])
            b_j = base[:, :, :].rearrange("p (o n) k -> p o (n k)", o=1).to_broadcast([NP_, 16, NSEL])
            step(dve.tensor_tensor(big1[:, 0:16, :], r_j, slot, ALU.is_equal))
            step(dve.tensor_tensor(big1[:, 0:16, :], big1[:, 0:16, :], b_j, ALU.mult))
            step(dve.tensor_reduce(slotb[:, :], big1[:, 0:16, :], AX, ALU.add))
            diag = ident[0:NP_, 0:NP_].rearrange("p (u o) -> p u o", o=1).to_broadcast([NP_, NP_, 16])
            sb_u = slotb[:, :].rearrange("p (o s) -> p o s", o=1).to_broadcast([NP_, NP_, 16])
            dve.tensor_tensor(spread[:, :, :], sb_u, diag, ALU.mult).then_inc(spread_ready, 1)
            dve.wait_ge(idx_psum, 1)
            step(dve.tensor_tensor(chosen[:, :, :], M[:, 0:256].rearrange("p (u s) -> p u s", u=NP_),
                                   slot8[:, :].rearrange("p (o s) -> p o s", o=1).to_broadcast([P, NP_, 16]), ALU.mult))
            step(dve.tensor_reduce(idxf[:, :], chosen[:, :, :], AX, ALU.add))
            step(dve.tensor_scalar(idxf[:, :], idxf[:, :], p8[:, 0:1], None, ALU.add))
            dve.tensor_copy(idx[:, :], idxf[:, :]).then_inc(idx_ready, 1)

            def turn_probs(k, br):
                dve.wait_ge(pT_psum, k + 1)
                if k:
                    dve.wait_ge(o_psum, k)
                n = len(spans[br])
                rows = tile_rows[br]
                full = n if spans[br][-1][1] == rows else n - 1
                last = dve.tensor_copy(pT[0:rows, 0:full, :], M[0:rows, 0:full * NR].rearrange("p (c r) -> p c r", r=NR))
                if full < n:
                    w = spans[br][-1][1]
                    last = dve.tensor_copy(pT[0:w, full, :], M[0:w, full * NR:n * NR])
                last.then_inc(pT_ready, 1)

            dve.wait_ge(keys_read, NB)
            peak(W_, [(SW, NW)])
            turn_probs(0, C_)
            turn_probs(1, W_)
            for u in range(NP_):
                copy_keys(NB + u)
            dve.wait_ge(keys_read, NB + NP_)
            peak(S_, [(SS[0], NS // 2), (SS[1], NS // 2)])
            turn_probs(2, S_)
            for br in range(3):
                st = stat[:, br, :]
                dve.wait_ge(probs[br], 1)
                if br == S_:
                    step(dve.tensor_tensor(st[:, 4:5], st[:, 4:5], st[:, 5:6], ALU.add))
                if br != C_:
                    step(dve.tensor_tensor(st[:, 4:5], st[:, 4:5], st[:, 3:4], ALU.add))
                step(dve.reciprocal(st[:, 5:6], st[:, 4:5]))
                step(dve.tensor_tensor(st[:, 6:7], st[:, 5:6], gate[:, br:br + 1], ALU.mult))
            dve.wait_ge(o_psum, 3)
            dve.tensor_copy(oT[:, :, :], O[:, :, :]).then_inc(oT_ready, 1)
            dve.wait_ge(back_psum, 1)
            step(dve.tensor_copy(o[:, :, :].rearrange("p k d -> p (k d)"), M[0:NR, 0:3 * HD]))
            for br, k in ((S_, 0), (W_, 1)):
                step(dve.scalar_tensor_tensor(out=o[:, br, :], in0=new[:, k, 1, :], scalar=stat[:, br, 3:4],
                                              in1=o[:, br, :], op0=ALU.mult, op1=ALU.add))
            step(dve.tensor_scalar(o[:, C_, :], o[:, C_, :], stat[:, C_, 6:7], None, ALU.mult))
            step(dve.scalar_tensor_tensor(out=o[:, C_, :], in0=o[:, S_, :], scalar=stat[:, S_, 6:7], in1=o[:, C_, :],
                                          op0=ALU.mult, op1=ALU.add))
            dve.scalar_tensor_tensor(out=o[:, C_, :], in0=o[:, W_, :], scalar=stat[:, W_, 6:7], in1=o[:, C_, :],
                                     op0=ALU.mult, op1=ALU.add).then_inc(done, 1)


def stage_merge_route(nc, a):
    NL = NGR + NE
    with Scope(nc, "mrg") as s:
        ident = s.sb("ident", [P, P])
        ones = s.sb("ones", [P, P])
        wo = s.sb("wo", [P, KT, D])
        wr = s.sb("wr", [P, KT, NL])
        br = s.sb("br", [P, NL])
        gcol = s.sb("gcol", [P, 2, CJ])
        mod = s.sb("mod", [P, 3, D])
        mods = s.sb("mods", [NB, 3, D])
        g2 = s.sb("g2", [P, D])
        eps = s.sb("eps", [P, 1])
        cT = s.sb("cT", [P, CJ, T])
        crow = s.sb("crow", [NB, CW])
        cTs = s.sb("cTs", [P, CJ, NB])
        at = [s.sb(f"at{i}", [P, 512]) for i in range(2)]
        aT = [s.sb(f"aT{i}", [P, CJ, P]) for i in range(2)]
        sq = s.sb("sq", [P, CJ, T])
        junk = s.sb("junk", [P, D])
        cstat = s.sb("cstat", [P, 3, TT])
        stat = s.sb("stat", [P, TT, 6])
        xt = [s.sb(f"xt{i}", [P, D]) for i in range(2)]
        yc = s.sb("yc", [P, D])
        x2 = [s.sb(f"x2{i}", [P, D]) for i in range(2)]
        h2 = [s.sb(f"h2{i}", [P, D]) for i in range(2)]
        hT = s.sb("hT", [P, KT, P])
        L = s.sb("L", [P, TT, NL])
        zrow = s.sb("zrow", [1, D])
        Pc = [s.ps(f"Pc{i}", [P, 512]) for i in range(2)]
        Pa = [s.ps(f"Pa{i}", [P, 512]) for i in range(2)]
        TA = s.ps("TA", [P, CJ, P])
        TH = [s.ps(f"TH{i}", [P, 4, P]) for i in range(2)]
        M = s.ps("M", [P, 512])

        const_in = s.sem("const_in")
        wo_in = [s.sem(f"wo_in{i}") for i in range(2)]
        tok_in = [s.sem(f"tok_in{i}") for i in range(2)]
        vset = s.sem("vset")
        conv_in = s.sem("conv_in")
        gain_in = s.sem("gain_in")
        row_in = s.sem("row_in")
        sq_ready = s.sem("sq_ready")
        sq_sum = s.sem("sq_sum")
        row_summed = s.sem("row_summed")
        conv_roots = s.sem("conv_roots")
        conv_inv = s.sem("conv_inv")
        roots = s.sem("roots")
        root2 = s.sem("root2")
        turned = s.sem("turned")
        aT_ready = s.sem("aT_ready")
        cT_ready = s.sem("cT_ready")
        product = s.sem("product")
        rinv = s.sem("rinv")
        yc_ready = s.sem("yc_ready")
        x2_ready = s.sem("x2_ready")
        y_read = s.sem("y_read")
        h2_ready = s.sem("h2_ready")
        h2_turned = s.sem("h2_turned")
        hT_v = s.sem("hT_v")
        hT_a = s.sem("hT_a")
        logits = s.sem("logits")
        logits_read = s.sem("logits_read")
        ach = s.sem("ach")
        vch = s.sem("vch")
        x2_out = [s.sem(f"x2_out{i}") for i in range(2)]
        z_out = s.sem("z_out")
        block = s.block()
        NCONST = 11

        @block.sync
        def _(sp):
            def load_tok(t):
                n = rows_of(t)
                src = a["x_prompt"][0, t * P:t * P + n, :] if t < NT else a["x_sample"][:, 0, :]
                sp.dma_start(at[t % 2][0:n, :], a["s_attn"][t * P:t * P + n, :]).then_inc(tok_in[t % 2], 16)
                sp.dma_start(xt[t % 2][0:n, :], src).then_inc(tok_in[t % 2], 16)

            sp.dma_start(crow[:, :], a["s_convs"]).then_inc(row_in, 16)
            sp.dma_start(ident[:, :], a["c_ident"]).then_inc(row_in, 16)
            sp.dma_start(ones[:, :], a["c_ones"]).then_inc(row_in, 16)
            for j in range(CJ):
                sp.dma_start(cT[:, j, :], a["s_convT"][j]).then_inc(conv_in, 16)
                if j == 0:
                    with nc.allow_non_contiguous_dma(reason="gains by channel"):
                        sp.dma_start(gcol[:, 0, :], a["g_out_conv"][0].rearrange("(j p) -> p j", p=P)).then_inc(gain_in, 16)
                        sp.dma_start(gcol[:, 1, :], a["g_out_attn"][0].rearrange("(j p) -> p j", p=P)).then_inc(gain_in, 16)
            load_tok(0)
            for half in range(2):
                sp.dma_start(wo[:, half * CJ:(half + 1) * CJ, :],
                             a["w_out"][0, half * CW:(half + 1) * CW].rearrange("(k p) n -> p k n", p=P)).then_inc(wo_in[half], 16)
            for j, seg in enumerate((2, 4, 3)):
                sp.dma_start(mod[:, j, :], a["s_mod"][NB:NB + 1, seg * D:(seg + 1) * D].to_broadcast([P, D])).then_inc(const_in, 16)
                sp.dma_start(mods[:, j, :], a["s_mod"][0:NB, seg * D:(seg + 1) * D]).then_inc(const_in, 16)
            sp.dma_start(g2[:, :], a["ln2_g"].to_broadcast([P, D])).then_inc(const_in, 16)
            sp.dma_start(wr[:, :, 0:NGR], a["w_route_group"][0].rearrange("(k p) n -> p k n", p=P)).then_inc(const_in, 16)
            sp.dma_start(wr[:, :, NGR:NL], a["w_route_expert"][0].rearrange("(k p) n -> p k n", p=P)).then_inc(const_in, 16)
            sp.dma_start(br[:, 0:NGR], a["b_route_group"].to_broadcast([P, NGR])).then_inc(const_in, 16)
            sp.dma_start(br[:, NGR:NL], a["b_route_expert"].to_broadcast([P, NE])).then_inc(const_in, 16)
            load_tok(1)
            for t in range(TT):
                n = rows_of(t)
                sp.wait_ge(h2_ready, t + 1)
                sp.dma_start(a["s_x2"][t * P:t * P + n, :], x2[t % 2][0:n, :]).then_inc(x2_out[t % 2], 16)
                sp.dma_start(a["s_h2"][t * P:t * P + n, :], h2[t % 2][0:n, :]).then_inc(x2_out[t % 2], 16)
                if t + 2 < TT:
                    sp.wait_ge(turned, t + 1)
                    load_tok(t + 2)
            sp.wait_ge(vset, 2)
            sp.dma_start(a["s_h2"][ZROW:ZROW + 1, :], zrow[:, :]).then_inc(z_out, 16)
            sp.wait_ge(logits_read, TT)
            sp.dma_start(a["s_logit"], L[:, :, :].rearrange("p t n -> p (t n)")).then_inc(z_out, 16)
            sp.wait_ge(z_out, 32)
            sp.wait_ge(x2_out[0], 32 * ((TT + 1) // 2))
            sp.wait_ge(x2_out[1], 32 * (TT // 2))

        @block.scalar
        def _(act):
            step = Chain(act, ach)

            def pre(t):
                n = rows_of(t)
                st = stat[:, t, :]
                act.wait_ge(tok_in[t % 2], 32 * (t // 2 + 1))
                step(act.activation(junk[0:n, 0:512], at[t % 2][0:n, :], ACT.Square, accum_out=st[0:n, 0:1]))
                act.activation(st[0:n, 1:2], st[0:n, 0:1], ACT.Sqrt, bias=eps[0:n, :], scale=1.0 / CW).then_inc(roots, 1)

            act.wait_ge(vset, 1)
            act.wait_ge(row_in, 48)
            act.activation(junk[0:NB, 0:512], crow[:, :], ACT.Square, accum_out=cstat[0:NB, 0, NT:TT]).then_inc(row_summed, 1)
            act.wait_ge(conv_in, 16 * CJ)
            for h in range(2):
                part = slice(h * T // 2, (h + 1) * T // 2)
                act.activation(sq[:, :, part], cT[:, :, part], ACT.Square).then_inc(sq_ready, 1)
            act.wait_ge(row_summed, 1)
            pre(0)
            act.wait_ge(sq_sum, 1)
            act.activation(cstat[:, 1, 0:NT], M[:, 0:NT], ACT.Sqrt, bias=eps[:, :], scale=1.0 / CW).then_inc(conv_roots, 1)
            act.activation(cstat[0:NB, 1, NT:TT], cstat[0:NB, 0, NT:TT], ACT.Sqrt, bias=eps[0:NB, :], scale=1.0 / CW
                           ).then_inc(conv_roots, 1)
            act.wait_ge(conv_inv, 2)
            for t in range(TT):
                n = rows_of(t)
                st = stat[:, t, :]
                act.wait_ge(product, t + 1)
                if t:
                    act.wait_ge(y_read, t)
                for c in range(2):
                    last = act.activation(yc[0:n, c * 512:(c + 1) * 512], Pc[c][0:n, :], ACT.Copy, scale=cstat[0:n, 2, t:t + 1])
                last.then_inc(yc_ready, 1)
                if t + 1 < TT:
                    pre(t + 1)
                act.wait_ge(x2_ready, t + 1)
                step(act.activation(junk[0:n, :], x2[t % 2][0:n, :], ACT.Square, accum_out=st[0:n, 3:4]))
                act.activation(st[0:n, 4:5], st[0:n, 3:4], ACT.Sqrt, bias=eps[0:n, :], scale=1.0 / D).then_inc(root2, 1)
                act.wait_ge(h2_turned, t + 1)
                if t:
                    act.wait_ge(logits, t)
                act.activation(hT[:, 4:8, 0:n], TH[1][:, :, 0:n], ACT.Copy).then_inc(hT_a, 1)

        @block.tensor
        def _(pe):
            def turn_h2(t):
                n = rows_of(t)
                pe.wait_ge(h2_ready, t + 1)
                if t:
                    pe.wait_ge(hT_v, t)
                    pe.wait_ge(hT_a, t)
                for k in range(KT):
                    last = pe.transpose(TH[k // 4][:, k % 4, 0:n], h2[t % 2][0:n, k * P:(k + 1) * P], ident[0:n, 0:n])
                last.then_inc(h2_turned, 1)

            def route(t):
                n = rows_of(t)
                pe.wait_ge(hT_v, t + 1)
                pe.wait_ge(hT_a, t + 1)
                if t:
                    pe.wait_ge(logits_read, t)
                for k in range(KT):
                    last = pe.matmul(M[0:n, 64:64 + NL], hT[:, k, 0:n], wr[:, k, :], start=(k == 0), stop=(k == KT - 1))
                last.then_inc(logits, 1)

            def turn_attn(t):
                n = rows_of(t)
                pe.wait_ge(tok_in[t % 2], 32 * (t // 2 + 1))
                pe.wait_ge(aT_ready, t + 1)
                for j in range(CJ):
                    last = pe.transpose(TA[:, j, 0:n], at[t % 2][0:n, j * P:(j + 1) * P], ident[0:n, 0:n])
                last.then_inc(turned, 1)

            pe.wait_ge(row_in, 48)
            for j in range(CJ):
                last = pe.transpose(TA[:, j, 0:NB], crow[:, j * P:(j + 1) * P], ident[0:NB, 0:NB])
            last.then_inc(turned, 1)
            for t in range(NT):
                if t % (NT // 2) == 0:
                    pe.wait_ge(sq_ready, t // (NT // 2) + 1)
                for j in range(CJ):
                    last = pe.matmul(M[:, t:t + 1], sq[:, j, t * P:(t + 1) * P], ones[:, 0:1], start=(j == 0), stop=(j == CJ - 1))
            last.then_inc(sq_sum, 1)
            turn_attn(0)
            for t in range(TT):
                n = rows_of(t)
                if t == 0:
                    pe.wait_ge(cT_ready, 1)
                    pe.wait_ge(wo_in[0], 16)
                else:
                    pe.wait_ge(yc_ready, t)
                for j in range(CJ):
                    for c in range(2):
                        lhs = cT[:, j, t * P:(t + 1) * P] if t < NT else cTs[:, j, :]
                        pe.matmul(Pc[c][0:n, :], lhs, wo[:, j, c * 512:(c + 1) * 512], start=(j == 0), stop=(j == CJ - 1))
                pe.wait_ge(aT_ready, t + 2)
                if t:
                    pe.wait_ge(y_read, t)
                else:
                    pe.wait_ge(wo_in[1], 16)
                for j in range(CJ):
                    for c in range(2):
                        last = pe.matmul(Pa[c][0:n, :], aT[t % 2][:, j, 0:n], wo[:, CJ + j, c * 512:(c + 1) * 512],
                                         start=(j == 0), stop=(j == CJ - 1))
                last.then_inc(product, 1)
                if t == 0:
                    pe.wait_ge(const_in, 16 * NCONST)
                    pe.wait_ge(conv_roots, 1)
                if t:
                    turn_h2(t - 1)
                if t + 1 < TT:
                    turn_attn(t + 1)
                if t:
                    route(t - 1)
            turn_h2(TT - 1)
            route(TT - 1)

        @block.vector
        def _(dve):
            step = Chain(dve, vch)
            dve.memset(eps[:, :], EPS).then_inc(vset, 1)
            dve.memset(zrow[:, :], 0.0).then_inc(vset, 1)
            step(dve.memset(L[:, :, :], 0.0))
            dve.wait_ge(gain_in, 32)
            dve.wait_ge(turned, 1)
            for j in range(CJ):
                last = dve.tensor_scalar(cTs[:, j, :], TA[:, j, 0:NB], gcol[:, 0, j:j + 1], None, ALU.mult)
            last.then_inc(aT_ready, 1)

            def scale_in(t):
                n = rows_of(t)
                dve.wait_ge(turned, t + 2)
                if t >= 2:
                    dve.wait_ge(product, t - 1)
                for j in range(CJ):
                    last = dve.tensor_scalar(aT[t % 2][:, j, 0:n], TA[:, j, 0:n], gcol[:, 1, j:j + 1], None, ALU.mult)
                last.then_inc(aT_ready, 1)
                dve.wait_ge(roots, t + 1)
                dve.reciprocal(stat[0:n, t, 2:3], stat[0:n, t, 1:2]).then_inc(rinv, 1)

            dve.wait_ge(sq_ready, 2)
            for j in range(CJ):
                last = dve.tensor_scalar(cT[:, j, :], cT[:, j, :], gcol[:, 0, j:j + 1], None, ALU.mult)
            last.then_inc(cT_ready, 1)
            dve.wait_ge(conv_roots, 2)
            dve.reciprocal(cstat[:, 2, 0:NT], cstat[:, 1, 0:NT]).then_inc(conv_inv, 1)
            dve.reciprocal(cstat[0:NB, 2, NT:TT], cstat[0:NB, 1, NT:TT]).then_inc(conv_inv, 1)
            def logits_in(t):
                n = rows_of(t)
                dve.wait_ge(h2_turned, t + 1)
                dve.tensor_copy(hT[:, 0:4, 0:n], TH[0][:, :, 0:n]).then_inc(hT_v, 1)
                dve.wait_ge(logits, t + 1)
                dve.tensor_tensor(L[0:n, t, :], M[0:n, 64:64 + NL], br[0:n, :], ALU.add).then_inc(logits_read, 1)

            scale_in(0)
            dve.wait_ge(const_in, 16 * NCONST)
            for part, n in ((mod, P), (mods, NB)):
                step(dve.scalar_tensor_tensor(out=part[:, 1, :], in0=part[:, 1, :], scalar=1.0, in1=g2[0:n, :],
                                              op0=ALU.add, op1=ALU.mult))
            for t in range(TT):
                n = rows_of(t)
                m = mod if t < NT else mods
                if t:
                    logits_in(t - 1)
                xo, ho = x2[t % 2][0:n, :], h2[t % 2][0:n, :]
                if t >= 2:
                    dve.wait_ge(x2_out[t % 2], 32 * (t // 2))
                dve.wait_ge(rinv, t + 1)
                dve.wait_ge(yc_ready, t + 1)
                for c in range(2):
                    cs = slice(c * 512, (c + 1) * 512)
                    last = dve.scalar_tensor_tensor(out=x2[t % 2][0:n, cs], in0=Pa[c][0:n, :], scalar=stat[0:n, t, 2:3],
                                                    in1=yc[0:n, cs], op0=ALU.mult, op1=ALU.add)
                last.then_inc(y_read, 1)
                dve.wait_ge(y_read, t + 1)
                step(dve.tensor_tensor(xo, xo, m[0:n, 0, :], ALU.mult))
                dve.tensor_tensor(xo, xo, xt[t % 2][0:n, :], ALU.add).then_inc(x2_ready, 1)
                if t + 1 < TT:
                    scale_in(t + 1)
                dve.wait_ge(root2, t + 1)
                step(dve.reciprocal(stat[0:n, t, 5:6], stat[0:n, t, 4:5]))
                step(dve.scalar_tensor_tensor(out=ho, in0=xo, scalar=stat[0:n, t, 5:6], in1=m[0:n, 1, :],
                                              op0=ALU.mult, op1=ALU.mult))
                dve.tensor_tensor(ho, ho, m[0:n, 2, :], ALU.add).then_inc(h2_ready, 1)
            logits_in(TT - 1)


class ExpertWeights:

    def __init__(self, s, a):
        self.a = a
        self.wg = [s.sb(f"wg{i}", [P, KT, DE]) for i in range(2)]
        self.wu = [s.sb(f"wu{i}", [P, KT, DE]) for i in range(2)]
        self.wd = [s.sb(f"wd{i}", [P, DE // P, D]) for i in range(2)]
        self.gu_in = [s.sem(f"gu_in{i}") for i in range(2)]
        self.d_in = [s.sem(f"d_in{i}") for i in range(2)]

    def load_gu(self, sp, k, e):
        for dst, src in ((self.wg, "w_gate"), (self.wu, "w_up")):
            sp.dma_start(dst[k][:, :, :].rearrange("p k n -> p (k n)"),
                         self.a[src][0, bass.ds(e, 1)].rearrange("o (p k) n -> (o p) (k n)", p=P)
                         ).then_inc(self.gu_in[k], 16)

    def load_d(self, sp, k, e):
        sp.dma_start(self.wd[k][:, :, :].rearrange("p k n -> p (k n)"),
                     self.a["w_down"][0, bass.ds(e, 1)].rearrange("o (p k) n -> (o p) (k n)", p=P)
                     ).then_inc(self.d_in[k], 16)


def stage_slots(nc, a, weights):
    NL = NGR + NE
    with Scope(nc, "slt") as s:
        L = s.sb("L", [P, TT, NL])
        ones = s.sb("ones", [P, P])
        tri = s.sb("tri", [P, P])
        iota = s.sb("iota", [P, NE])
        kk = s.sb("kk", [P, 8])
        real = s.sb("real", [P, TT])
        tok = s.sb("tok", [P, TT], U32)
        empty = s.sb("empty", [P, NBLK], U32)
        gm = s.sb("gm", [P, TT, 1])
        dl = s.sb("dl", [P, TT, NGR])
        ex = s.sb("ex", [P, TT, NGR])
        pg = s.sb("pg", [P, TT, 1])
        key = s.sb("key", [P, TT, EPG])
        ohg = s.sb("ohg", [P, TT, NGR])
        sel = s.sb("sel", [P, TT, EPG, NGR])
        le = s.sb("le", [P, TT, EPG])
        m = s.sb("m", [P, 2, TT, 1])
        oh = s.sb("oh", [P, 2, TT, EPG])
        e21 = s.sb("e21", [P, TT, 1])
        den = s.sb("den", [P, TT, 1])
        oh32 = s.sb("oh32", [P, 2, TT, NGR, EPG])
        both = s.sb("both", [P, TT, NE])
        pos = s.sb("pos", [P, TT + 1, NE])
        over = s.sb("over", [P, NE, 8])
        extra = s.sb("extra", [P, NE])
        cum = [s.sb(f"cum{i}", [P, NE]) for i in range(2)]
        first = s.sb("first", [P, NE])
        shift = s.sb("shift", [P, NE])
        dest = s.sb("dest", [P, TT, NE])
        tmp = s.sb("tmp", [P, TT, NE])
        own = s.sb("own", [P, NOV, NE])
        own2 = s.sb("own2", [P, NOV, NE])
        route = s.sb("route", [P, 4, TT])
        slot = s.sb("slot", [P, 2, TT], U32)
        ov = s.sb("ov", [P, NOV + 1])
        ovi = s.sb("ovi", [P, NOV + 1], I32)
        before = s.sb("before", [P, TT + 1, NE])
        M = s.ps("M", [P, TT, NE])
        C = s.ps("C", [P, TT, NE])

        const_in = s.sem("const_in")
        ch = s.sem("ch")
        exp_in = s.sem("exp_in")
        exp_out = s.sem("exp_out")
        both_ready = s.sem("both_ready")
        counted = s.sem("counted")
        slots_ready = s.sem("slots_ready")
        empty_set = s.sem("empty_set")
        cleared = s.sem("cleared")
        filled = s.sem("filled")
        tables = s.sem("tables")
        out_done = s.sem("out_done")
        block = s.block()

        @block.sync
        def _(sp):
            sp.dma_start(L[:, :, :].rearrange("p t n -> p (t n)"), a["s_logit"]).then_inc(const_in, 16)
            sp.dma_start(ones[:, :], a["c_ones"]).then_inc(const_in, 16)
            sp.dma_start(tri[:, :], a["c_tri"]).then_inc(const_in, 16)
            sp.dma_start(iota[:, :], a["c_iota"][:, 0:NE].to_broadcast([P, NE])).then_inc(const_in, 16)
            sp.dma_start(kk[:, :], a["c_blocks"].to_broadcast([P, 8])).then_inc(const_in, 16)
            sp.dma_start(real[:, :], a["c_real"]).then_inc(const_in, 16)
            sp.dma_start(tok[:, :], a["c_tok"]).then_inc(const_in, 16)
            for k in range(2):
                weights.load_gu(sp, k, k)
                weights.load_d(sp, k, k)
            sp.wait_ge(tables, 1)
            sp.dma_start(a["s_route"], route[:, :, :].rearrange("p k t -> p (k t)")).then_inc(out_done, 16)
            sp.dma_start(a["s_ov"], ovi[0:1, :]).then_inc(out_done, 16)
            sp.wait_ge(out_done, 32)

        @block.gpsimd
        def _(pool):
            pool.memset(empty[:, :], ZROW).then_inc(empty_set, 1)
            pool.wait_ge(empty_set, 1)
            pool.dma_start(a["s_slot"].rearrange("(p k) o -> p (k o)", p=P), empty[:, :]).then_inc(cleared, 16)
            pool.wait_ge(cleared, 16)
            pool.wait_ge(const_in, 16 * 7)
            pool.wait_ge(slots_ready, 1)
            for t in range(TT):
                n = rows_of(t)
                for k in range(2):
                    pool.indirect_dma_start(a["s_slot"], bass.IndirectOffsetOnAxis(ap=slot[0:n, k, t:t + 1], axis=0),
                                            tok[0:n, t:t + 1], None).then_inc(filled, 16)
            pool.wait_ge(filled, 16 * 2 * TT)

        @block.scalar
        def _(act):
            act.wait_ge(exp_in, 1)
            act.activation(ex[:, :, :], dl[:, :, :], ACT.Exp).then_inc(exp_out, 1)
            act.wait_ge(exp_in, 2)
            act.activation(e21[:, :, :], den[:, :, :], ACT.Exp).then_inc(exp_out, 1)

        @block.tensor
        def _(pe):
            pe.wait_ge(const_in, 16 * 7)
            pe.wait_ge(both_ready, 1)
            pe.matmul(C[:, :, :], ones[:, :], both[:, :, :], start=True, stop=True)
            last = pe.matmul(M[:, :, :], tri[:, :], both[:, :, :], start=True, stop=True)
            last.then_inc(counted, 1)

        @block.vector
        def _(dve):
            step = Chain(dve, ch)
            TTc = dve.tensor_tensor
            dve.wait_ge(const_in, 16 * 7)
            lg = L[:, :, 0:NGR]

            def wide(x, shape):
                return x.to_broadcast(shape)

            def first_max(vals, width, top, onehot):
                io = iota[:, 0:width].rearrange("p (o n) -> p o n", o=1).to_broadcast([P, TT, width])
                k = key[:, :, 0:width]
                step(dve.tensor_reduce(top, vals, AX, ALU.max))
                step(TTc(k, vals, wide(top, [P, TT, width]), ALU.is_equal))
                step(dve.scalar_tensor_tensor(out=k, in0=k, scalar=-1000.0, in1=io, op0=ALU.mult, op1=ALU.add))
                step(dve.tensor_reduce(den[:, :, :], k, AX, ALU.min))
                step(TTc(onehot, k, wide(den[:, :, :], [P, TT, width]), ALU.is_equal))

            step(dve.memset(before[:, 0, :], 0.0))
            first_max(lg, NGR, gm[:, :, :], ohg[:, :, :])
            TTc(dl[:, :, :], lg, wide(gm[:, :, :], [P, TT, NGR]), ALU.subtract).then_inc(exp_in, 1)
            step(TTc(sel[:, :, :, :], L[:, :, NGR:NL].rearrange("p t (g e) -> p t e g", g=NGR),
                     ohg[:, :, :].rearrange("p t (o g) -> p t o g", o=1).to_broadcast([P, TT, EPG, NGR]), ALU.mult))
            step(dve.tensor_reduce(le[:, :, :], sel[:, :, :, :], AX, ALU.add))
            first_max(le[:, :, :], EPG, m[:, 0], oh[:, 0])
            step(dve.scalar_tensor_tensor(out=le[:, :, :], in0=oh[:, 0], scalar=-3e38, in1=le[:, :, :], op0=ALU.mult, op1=ALU.add))
            first_max(le[:, :, :], EPG, m[:, 1], oh[:, 1])
            TTc(den[:, :, :], m[:, 1], m[:, 0], ALU.subtract).then_inc(exp_in, 1)
            dve.wait_ge(exp_out, 2)
            step(dve.tensor_reduce(pg[:, :, :], ex[:, :, :], AX, ALU.add))
            step(dve.tensor_scalar(den[:, :, :], e21[:, :, :], 1.0, None, ALU.add))
            step(TTc(pg[:, :, :], pg[:, :, :], den[:, :, :], ALU.mult))
            w1, w2 = (route[:, 2 + k, :].rearrange("p (t o) -> p t o", o=1) for k in range(2))
            step(dve.reciprocal(w1, pg[:, :, :]))
            step(TTc(w2, w1, e21[:, :, :], ALU.mult))
            for k in range(2):
                for g in range(NGR):
                    step(TTc(oh32[:, k, :, g, :], oh[:, k], ohg[:, :, g:g + 1].to_broadcast([P, TT, EPG]), ALU.mult))
            o32 = [oh32[:, k, :, :, :].rearrange("p t g e -> p t (g e)") for k in range(2)]
            step(TTc(both[:, :, :], o32[0], o32[1], ALU.add))
            TTc(both[:, :, :], both[:, :, :], real[:, :].rearrange("p (t o) -> p t o", o=1).to_broadcast([P, TT, NE]),
                ALU.mult).then_inc(both_ready, 1)
            dve.wait_ge(counted, 1)
            for t in range(TT):
                step(TTc(before[:, t + 1, :], before[:, t, :], C[:, t, :], ALU.add))
            step(TTc(pos[:, 0:TT, :], before[:, 0:TT, :], M[:, :, :], ALU.add))
            step(dve.tensor_copy(pos[:, TT, :], before[:, TT, :]))
            step(TTc(over[:, :, :], pos[:, TT, :].rearrange("p (e o) -> p e o", o=1).to_broadcast([P, NE, 8]),
                     kk[:, :].rearrange("p (o k) -> p o k", o=1).to_broadcast([P, NE, 8]), ALU.is_gt))
            step(dve.tensor_reduce(extra[:, :], over[:, :, :], AX, ALU.add))
            src = extra
            for i, sh in enumerate((1, 2, 4, 8, 16)):
                dst = cum[i % 2]
                step(dve.tensor_copy(dst[:, 0:sh], src[:, 0:sh]))
                step(TTc(dst[:, sh:NE], src[:, sh:NE], src[:, 0:NE - sh], ALU.add))
                src = dst
            step(TTc(first[:, :], src[:, :], extra[:, :], ALU.subtract))
            step(TTc(shift[:, :], first[:, :], iota[:, :], ALU.subtract))
            step(dve.tensor_scalar(shift[:, :], shift[:, :], float(NE - 1), 128.0, ALU.add, ALU.mult))
            sh3 = shift[:, :].rearrange("p (o e) -> p o e", o=1).to_broadcast([P, TT, NE])
            e3 = iota[:, :].rearrange("p (o e) -> p o e", o=1).to_broadcast([P, TT, NE])
            p3 = pos[:, 0:TT, :]
            step(dve.tensor_scalar(tmp[:, :, :], p3, 128.0, None, ALU.is_ge))
            step(TTc(tmp[:, :, :], tmp[:, :, :], sh3, ALU.mult))
            step(TTc(tmp[:, :, :], tmp[:, :, :], p3, ALU.add))
            step(dve.scalar_tensor_tensor(out=dest[:, :, :], in0=e3, scalar=128.0, in1=tmp[:, :, :], op0=ALU.mult, op1=ALU.add))
            for k in range(2):
                step(TTc(tmp[:, :, :], dest[:, :, :], o32[k], ALU.mult))
                step(dve.tensor_reduce(route[:, k, :], tmp[:, :, :], AX, ALU.add))
            dve.tensor_copy(slot[:, :, :], route[:, 0:2, :]).then_inc(slots_ready, 1)
            j3 = iota[:, 0:NOV].rearrange("p (n o) -> p n o", o=1).to_broadcast([P, NOV, NE])
            def row(x):
                return x[:, :].rearrange("p (o e) -> p o e", o=1).to_broadcast([P, NOV, NE])
            step(TTc(own[:, :, :], j3, row(first), ALU.is_ge))
            step(TTc(own2[:, :, :], j3, row(src), ALU.is_lt))
            step(TTc(own[:, :, :], own[:, :, :], own2[:, :, :], ALU.mult))
            step(TTc(own[:, :, :], own[:, :, :], row(iota), ALU.mult))
            step(dve.tensor_reduce(ov[:, 0:NOV], own[:, :, :], AX, ALU.add))
            step(dve.tensor_copy(ov[:, NOV:NOV + 1], src[:, NE - 1:NE]))
            dve.tensor_copy(ovi[:, :], ov[:, :]).then_inc(tables, 1)


def stage_experts(nc, a, weights):
    KD = DE // P
    with Scope(nc, "moe") as s:
        ident = s.sb("ident", [P, P])
        idx = s.sb("idx", [P, NBLK], U32)
        ov = s.sb("ov", [1, NOV + 1], I32)
        wg, wu, wd = weights.wg, weights.wu, weights.wd
        gu_in, d_in = weights.gu_in, weights.d_in
        xg = [s.sb(f"xg{i}", [P, D]) for i in range(2)]
        xT = [s.sb(f"xT{i}", [P, KT, P]) for i in range(2)]
        sg = s.sb("sg", [P, DE])
        h = s.sb("h", [P, DE])
        hT = s.sb("hT", [P, KD, P])
        y = [s.sb(f"y{i}", [P, D]) for i in range(2)]
        settled = s.sb("settled", [1, 1])
        XT = [s.ps(f"XT{i}", [P, 4, P]) for i in range(2)]
        G = s.ps("G", [P, DE])
        U = s.ps("U", [P, DE])
        HT = s.ps("HT", [P, KD, P])
        Y = [s.ps(f"Y{i}", [P, 512]) for i in range(2)]

        const_in = s.sem("const_in")
        idx_in = s.sem("idx_in")
        x_in = [s.sem(f"x_in{i}") for i in range(2)]
        x_turned = s.sem("x_turned")
        xT_v = s.sem("xT_v")
        xT_a = s.sem("xT_a")
        g_done = s.sem("g_done")
        u_done = s.sem("u_done")
        silu_done = s.sem("silu_done")
        h_ready = s.sem("h_ready")
        h_turned = s.sem("h_turned")
        hT_ready = s.sem("hT_ready")
        y_done = s.sem("y_done")
        y_a = s.sem("y_a")
        y_v = s.sem("y_v")
        y_out = [s.sem(f"y_out{i}") for i in range(2)]
        block = s.block()

        def overflow(eng, body):
            blocks = eng.value_load(ov[0:1, NOV:NOV + 1], min_val=0, max_val=NOV)
            with eng.Fori(0, NOV // 2) as j:
                for k in range(2):
                    with eng.If(blocks > 2 * j + k):
                        body(2 * j + k, k, NE + 2 * j + k, NE // 2 + j)

        def gate(pe, k, n, i):
            pe.wait_ge(xT_v, n + 1)
            pe.wait_ge(xT_a, n + 1)
            pe.wait_ge(gu_in[k], 32 * i + 32)
            wait(pe, silu_done, n)
            for c in range(KT):
                last = pe.matmul(G[:, :], xT[k][:, c, :], wg[k][:, c, :], start=(c == 0), stop=(c == KT - 1))
            last.then_inc(g_done, 1)

        def up(pe, k, n):
            wait(pe, h_ready, n)
            for c in range(KT):
                last = pe.matmul(U[:, :], xT[k][:, c, :], wu[k][:, c, :], start=(c == 0), stop=(c == KT - 1))
            last.then_inc(u_done, 1)

        def turn_x(pe, k):
            for c in range(KT):
                last = pe.transpose(XT[c // 4][:, c % 4, :], xg[k][:, c:D:KT], ident[:, :])
            last.then_inc(x_turned, 1)

        def turn_h(pe, n):
            pe.wait_ge(h_ready, n + 1)
            wait(pe, hT_ready, n)
            for c in range(KD):
                last = pe.transpose(HT[:, c, :], h[:, c:DE:KD], ident[:, :])
            last.then_inc(h_turned, 1)

        def down(pe, k, n, loads):
            pe.wait_ge(hT_ready, n + 1)
            pe.wait_ge(d_in[k], 16 * loads)
            wait(pe, y_a, n)
            wait(pe, y_v, n)
            for half in range(2):
                for c in range(KD):
                    last = pe.matmul(Y[half][:, :], hT[:, c, :], wd[k][:, c, half * 512:(half + 1) * 512],
                                     start=(c == 0), stop=(c == KD - 1))
            last.then_inc(y_done, 1)

        @block.sync
        def _(sp):
            sp.dma_start(ident[:, :], a["c_ident"]).then_inc(const_in, 16)
            sp.dma_start(ov[:, :], a["s_ov"]).then_inc(const_in, 16)
            with nc.allow_non_contiguous_dma(reason="slot table, one block per column"):
                sp.dma_start(idx[:, :], a["s_slot"].rearrange("(n p) o -> p (n o)", p=P)).then_inc(idx_in, 16)

            def next_gu(k, n):
                sp.wait_ge(u_done, n - 1)
                weights.load_gu(sp, k, n)

            next_gu(0, 2)
            with sp.Fori(0, NE // 2 - 2) as i:
                next_gu(1, 2 * i + 3)
                next_gu(0, 2 * i + 4)
            next_gu(1, NE - 1)
            sp.wait_ge(const_in, 32)

            def more(b, k, n, i):
                e = sp.value_load(ov[0:1, bass.ds(b, 1)], min_val=0, max_val=NE - 1)
                sp.wait_ge(u_done, n - 1)
                weights.load_gu(sp, k, e)

            overflow(sp, more)

        @block.gpsimd
        def _(pool):
            def gather(e, k, at):
                pool.indirect_dma_start(xg[k][:, :], None, a["s_h2"],
                                        bass.IndirectOffsetOnAxis(ap=idx[:, at:at + 1], axis=0)).then_inc(x_in[k], 16)

            pool.wait_ge(idx_in, 16)
            for e in range(NE):
                if e >= 2:
                    pool.wait_ge(x_turned, e - 1)
                gather(e, e % 2, e)
            pool.wait_ge(const_in, 32)
            blocks = pool.value_load(ov[0:1, NOV:NOV + 1], min_val=0, max_val=NOV)
            for b in range(NOV):
                with pool.If(blocks > b):
                    pool.wait_ge(x_turned, NE + b - 1)
                    gather(NE + b, b % 2, NE + b)

        @block.tensor
        def _(pe):
            pe.wait_ge(const_in, 32)
            pe.wait_ge(x_in[0], 16)
            turn_x(pe, 0)

            def expert(i, k, before=True, following=True):
                n = 2 * i + k
                gate(pe, k, n, i)
                if before:
                    turn_h(pe, n - 1)
                if following:
                    pe.wait_ge(x_in[1 - k], 16 * i + 16 + 16 * k)
                    turn_x(pe, 1 - k)
                up(pe, k, n)
                if before:
                    down(pe, 1 - k, n - 1, i + k)

            expert(0, 0, before=False)
            expert(0, 1)
            with pe.Fori(1, NE // 2 - 1) as i:
                for k in range(2):
                    expert(i, k)
            expert(NE // 2 - 1, 0)
            expert(NE // 2 - 1, 1, following=False)
            turn_h(pe, NE - 1)
            down(pe, 1, NE - 1, NE // 2)

            def more(b, k, n, i):
                pe.wait_ge(x_in[k], 16 * i + 16)
                wait(pe, xT_v, n)
                wait(pe, xT_a, n)
                turn_x(pe, k)
                gate(pe, k, n, i)
                up(pe, k, n)
                turn_h(pe, n)
                down(pe, k, n, i + 1)

            overflow(pe, more)

        @block.scalar
        def _(act):
            def x_copy(k, n):
                act.wait_ge(x_turned, n + 1)
                act.activation(xT[k][:, 4:8, :], XT[1][:, :, :], ACT.Copy).then_inc(xT_a, 1)

            def silu(n):
                act.wait_ge(g_done, n + 1)
                wait(act, h_ready, n)
                act.activation(sg[:, :], G[:, :], ACT.Silu).then_inc(silu_done, 1)

            def y_copy(k, n, i):
                act.wait_ge(y_done, n + 1)
                wait(act, y_out[k], 16 * i)
                act.activation(y[k][:, 0:512], Y[0][:, :], ACT.Copy).then_inc(y_a, 1)

            def store(k, n, blk):
                act.wait_ge(y_a, n + 1)
                act.wait_ge(y_v, n + 1)
                act.dma_start(a["s_yb"][bass.ds(blk * P, P), :], y[k][:, :]).then_inc(y_out[k], 16)

            act.wait_ge(const_in, 32)
            x_copy(0, 0)

            def expert(i, k, before=True, following=True):
                n = 2 * i + k
                silu(n)
                if following:
                    x_copy(1 - k, n + 1)
                if before:
                    y_copy(1 - k, n - 1, i - 1 + k)
                    if following:
                        weights.load_d(act, 1 - k, n + 1)
                    store(1 - k, n - 1, n - 1)

            expert(0, 0, before=False)
            expert(0, 1)
            expert(1, 0)
            expert(1, 1)
            with act.Fori(2, NE // 2 - 1) as i:
                for k in range(2):
                    expert(i, k)
            expert(NE // 2 - 1, 0)
            expert(NE // 2 - 1, 1, following=False)
            y_copy(1, NE - 1, NE // 2 - 1)
            store(1, NE - 1, NE - 1)

            def more(b, k, n, i):
                e = act.value_load(ov[0:1, bass.ds(b, 1)], min_val=0, max_val=NE - 1)
                weights.load_d(act, k, e)
                x_copy(k, n)
                silu(n)
                y_copy(k, n, i)
                store(k, n, n)
                act.wait_ge(y_out[k], 16 * i + 16)
                act.activation(settled[:, :], ident[0:1, 0:1], ACT.Copy)

            act.wait_ge(y_out[0], 16 * (NE // 2))
            act.wait_ge(y_out[1], 16 * (NE // 2))
            overflow(act, more)

        @block.vector
        def _(dve):
            def x_copy(k, n):
                dve.wait_ge(x_turned, n + 1)
                dve.tensor_copy(xT[k][:, 0:4, :], XT[0][:, :, :]).then_inc(xT_v, 1)

            def hidden(n):
                dve.wait_ge(silu_done, n + 1)
                dve.wait_ge(u_done, n + 1)
                wait(dve, h_turned, n)
                dve.tensor_tensor(h[:, :], sg[:, :], U[:, :], ALU.mult).then_inc(h_ready, 1)

            def h_copy(n):
                dve.wait_ge(h_turned, n + 1)
                dve.tensor_copy(hT[:, :, :], HT[:, :, :]).then_inc(hT_ready, 1)

            def y_copy(k, n, i):
                dve.wait_ge(y_done, n + 1)
                wait(dve, y_out[k], 16 * i)
                dve.tensor_copy(y[k][:, 512:D], Y[1][:, :]).then_inc(y_v, 1)

            dve.wait_ge(const_in, 32)
            x_copy(0, 0)

            def expert(i, k, before=True, following=True):
                n = 2 * i + k
                if before:
                    h_copy(n - 1)
                if following:
                    x_copy(1 - k, n + 1)
                hidden(n)
                if before:
                    y_copy(1 - k, n - 1, i - 1 + k)

            expert(0, 0, before=False)
            expert(0, 1)
            expert(1, 0)
            expert(1, 1)
            with dve.Fori(2, NE // 2 - 1) as i:
                for k in range(2):
                    expert(i, k)
            expert(NE // 2 - 1, 0)
            expert(NE // 2 - 1, 1, following=False)
            h_copy(NE - 1)
            y_copy(1, NE - 1, NE // 2 - 1)

            def more(b, k, n, i):
                x_copy(k, n)
                hidden(n)
                h_copy(n)
                y_copy(k, n, i)

            overflow(dve, more)


def stage_combine(nc, a):
    with Scope(nc, "fin") as s:
        route = s.sb("route", [P, 4, TT])
        slot = s.sb("slot", [P, 2, TT], U32)
        mod = s.sb("mod", [P, D])
        mods = s.sb("mods", [NB, D])
        gf = s.sb("gf", [P, D])
        eps = s.sb("eps", [P, 1])
        x2 = [s.sb(f"x2{i}", [P, D]) for i in range(TT)]
        y1 = [s.sb(f"y1{i}", [P, D]) for i in range(TT)]
        y2 = [s.sb(f"y2{i}", [P, D]) for i in range(TT)]
        f1 = [s.sb(f"f1{i}", [P, D]) for i in range(2)]
        junk = s.sb("junk", [P, D])
        stat = s.sb("stat", [P, TT, 3])
        out = [s.sb(f"out{i}", [P, D]) for i in range(2)]

        route_in = s.sem("route_in")
        const_in = s.sem("const_in")
        slot_ready = s.sem("slot_ready")
        x_in = [s.sem(f"x_in{i}") for i in range(TT)]
        y_in = [s.sem(f"y_in{i}") for i in range(TT)]
        first = s.sem("first")
        summed = s.sem("summed")
        ss = s.sem("ss")
        root = s.sem("root")
        normed = s.sem("normed")
        vch = s.sem("vch")
        out_done = [s.sem(f"out_done{i}") for i in range(2)]
        block = s.block()

        def store(sp, t):
            n = rows_of(t)
            sp.wait_ge(normed, t + 1)
            dst = a["o_y_p"][0, t * P:t * P + n, :] if t < NT else a["o_y_s"][:, 0, :]
            sp.dma_start(dst, out[t % 2][0:n, :]).then_inc(out_done[t % 2], 16)

        @block.sync
        def _(sp):
            sp.dma_start(route[:, :, :].rearrange("p k t -> p (k t)"), a["s_route"]).then_inc(route_in, 16)
            for t in range(TT):
                n = rows_of(t)
                sp.dma_start(x2[t][0:n, :], a["s_x2"][t * P:t * P + n, :]).then_inc(x_in[t], 16)
                if t == 0:
                    sp.dma_start(mod[:, :], a["s_mod"][NB:NB + 1, 5 * D:6 * D].to_broadcast([P, D])).then_inc(const_in, 16)
                    sp.dma_start(mods[:, :], a["s_mod"][0:NB, 5 * D:6 * D]).then_inc(const_in, 16)
                    sp.dma_start(gf[:, :], a["final_g"].to_broadcast([P, D])).then_inc(const_in, 16)
            for t in range(TT):
                store(sp, t)
            sp.wait_ge(out_done[0], 16 * ((TT + 1) // 2))
            sp.wait_ge(out_done[1], 16 * (TT // 2))

        @block.gpsimd
        def _(pool):
            pool.wait_ge(slot_ready, 1)
            for t in range(TT):
                n = rows_of(t)
                for k, dst in enumerate((y1, y2)):
                    pool.indirect_dma_start(dst[t][0:n, :], None, a["s_yb"],
                                            bass.IndirectOffsetOnAxis(ap=slot[0:n, k, t:t + 1], axis=0)
                                            ).then_inc(y_in[t], 16)

        @block.scalar
        def _(act):
            act.wait_ge(route_in, 16)

            def weigh(t):
                n = rows_of(t)
                act.wait_ge(y_in[t], 32)
                if t >= 2:
                    act.wait_ge(summed, t - 1)
                act.activation(f1[t % 2][0:n, :], y1[t][0:n, :], ACT.Copy, scale=route[0:n, 2, t:t + 1]).then_inc(first, 1)

            weigh(0)
            for t in range(TT):
                n = rows_of(t)
                if t + 1 < TT:
                    weigh(t + 1)
                act.wait_ge(summed, t + 1)
                act.activation(junk[0:n, :], x2[t][0:n, :], ACT.Square, accum_out=stat[0:n, t, 0:1]).then_inc(ss, 1)
                act.wait_ge(ss, t + 1)
                act.activation(stat[0:n, t, 1:2], stat[0:n, t, 0:1], ACT.Sqrt, bias=eps[0:n, :], scale=1.0 / D
                               ).then_inc(root, 1)

        @block.vector
        def _(dve):
            step = Chain(dve, vch)
            step(dve.memset(eps[:, :], EPS))
            dve.wait_ge(route_in, 16)
            dve.tensor_copy(slot[:, :, :], route[:, 0:2, :]).then_inc(slot_ready, 1)
            dve.wait_ge(const_in, 48)

            def add(t):
                n = rows_of(t)
                m = (mod if t < NT else mods)[0:n, :]
                f, x = f1[t % 2][0:n, :], x2[t][0:n, :]
                dve.wait_ge(first, t + 1)
                step(dve.scalar_tensor_tensor(out=f, in0=y2[t][0:n, :], scalar=route[0:n, 3, t:t + 1], in1=f,
                                              op0=ALU.mult, op1=ALU.add))
                step(dve.tensor_tensor(f, f, m, ALU.mult))
                dve.wait_ge(x_in[t], 16)
                dve.tensor_tensor(x, x, f, ALU.add).then_inc(summed, 1)

            def norm(t):
                n = rows_of(t)
                dve.wait_ge(root, t + 1)
                if t >= 2:
                    dve.wait_ge(out_done[t % 2], 16 * (t // 2))
                step(dve.reciprocal(stat[0:n, t, 2:3], stat[0:n, t, 1:2]))
                dve.scalar_tensor_tensor(out=out[t % 2][0:n, :], in0=x2[t][0:n, :], scalar=stat[0:n, t, 2:3],
                                         in1=gf[0:n, :], op0=ALU.mult, op1=ALU.mult).then_inc(normed, 1)

            add(0)
            for t in range(TT):
                if t + 1 < TT:
                    add(t + 1)
                norm(t)


def build(nc, a):
    stage_ada(nc, a)
    stage_project(nc, a)
    stage_compress(nc, a)
    with Scope(nc, "smi") as s:
        sample = SampleInputs(s)
        stage_prompt_attention(nc, a, sample)
        stage_sample_attention(nc, a, sample)
    stage_merge_route(nc, a)
    with Scope(nc, "wts") as s:
        weights = ExpertWeights(s, a)
        stage_slots(nc, a, weights)
        stage_experts(nc, a, weights)
    stage_combine(nc, a)


OUTS = [("o_y_p", (1, T, D)), ("o_y_s", (NB, 1, D)), ("o_cmp_p", (1, 1, T, 2, NG, HD)),
        ("o_cmp_s", (1, NB, 1, 2, NG, HD)), ("o_sel_p", (1, 1, T, 2, NG, HD)), ("o_sel_s", (1, NB, 1, 2, NG, HD)),
        ("o_win_p", (1, 1, 512, 2, NG, HD)), ("o_win_s", (1, NB, 512, 2, NG, HD)),
        ("o_conv_p", (1, 1, 2, CW)), ("o_conv_s", (1, NB, 2, CW))]
SCRATCH = [("s_mod", (9, 6 * D)), ("s_cT", (P, KT * 9)), ("s_convT", (CJ, P, T)), ("s_convs", (NB, CW)), ("s_z", (NTOK, TOK)),
           ("s_ck", (NB + 1, HD, NG, NCH)), ("s_cv", (NB + 1, NCH, NG * HD)),
           ("s_attn", (NTOK, NH * HD)), ("s_x2", (NTOK, D)), ("s_h2", (NTOK + 1, D)),
           ("s_logit", (P, TT * (NGR + NE))), ("s_route", (P, 4 * TT)), ("s_ov", (1, NOV + 1)),
           ("s_slot", (NBLK * P, 1)), ("s_yb", (NBLK * P, D))]


def constants():
    f = np.float32
    half = HD // 2
    inv = (f(10000.0) ** (-np.arange(half, dtype=f) / f(half))).astype(f)

    def tables(pos):
        ang = pos.astype(f)[:, None] * inv[None, :]
        c, s = np.cos(ang).astype(f), np.sin(ang).astype(f)
        return np.concatenate([c, c], 1), np.concatenate([-s, s], 1)

    c, s = tables(np.concatenate([np.arange(T), np.full(NB, PAST)]))
    out = {"c_ident": np.eye(P, dtype=f),
           "c_rope": np.stack([c, s, c / 8, s / 8]),
           "c_mod8": (np.arange(P) % 8).astype(f).reshape(P, 1)}
    c, s = tables((np.arange(NCMP) + 2) * 16 - 1)
    out["c_ropec"] = np.ascontiguousarray(np.stack([c.T, s.T], 1))
    q, k = np.arange(P)[:, None], np.arange(P)[None, :]
    out["c_diag"] = np.where(k <= q, 0, NEG).astype(f)
    out["c_far"] = np.where(k >= q, 0, NEG).astype(f)
    out["c_cmask"] = np.where(16 * (np.arange(64)[None, :] - 57) + 31 <= q, 0, NEG).astype(f)
    out["c_valid"] = (np.arange(P) >= 31).astype(f).reshape(P, 1)
    out["c_member"] = (np.arange(64)[:, None] // QG == np.arange(16)[None, :]).astype(f)
    out["c_tri64"] = (np.arange(64)[None, :] < np.arange(64)[:, None]).astype(f).reshape(1, 64, 64)
    out["c_iota"] = np.arange(P, dtype=f).reshape(1, P)
    out["c_half8"] = np.array([[0, 8]], f)
    out["c_slot8"] = (np.arange(P)[:, None] // 8 == np.arange(16)[None, :]).astype(f)
    out["c_ones"] = np.ones((P, P), f)
    out["c_tri"] = (np.arange(P)[:, None] < np.arange(P)[None, :]).astype(f)
    out["c_blocks"] = (np.arange(1, 9) * 128).astype(f).reshape(1, 8)
    tok = np.arange(TT)[None, :] * P + np.arange(P)[:, None]
    out["c_tok"] = tok.astype(np.uint32)
    out["c_real"] = (tok < NTOK).astype(f)
    return out


def kernel(**inputs):
    import concourse.bacc as _bacc
    from concourse.bass_utils import run_bass_kernel_spmd as _run

    nc = _bacc.Bacc("TRN2", target_bir_lowering=False, num_devices=1)
    arrays, a = {}, {}
    for name, v in list(inputs.items()) + list(constants().items()):
        v = np.ascontiguousarray(v)
        if v.ndim == 1:
            v = v.reshape(1, -1)
        arrays[f"in_{name}"] = v
        a[name] = nc.dram_tensor(f"in_{name}", v.shape, mybir.dt.from_np(v.dtype), kind="ExternalInput").ap()
    for name, shape in OUTS:
        a[name] = nc.dram_tensor(name, shape, F32, kind="ExternalOutput").ap()
    for name, shape in SCRATCH:
        a[name] = nc.dram_tensor(name, shape, {"s_ov": I32, "s_slot": U32}.get(name, F32)).ap()
    build(nc, a)
    r = _run(nc, [arrays], core_ids=[0])
    return tuple(r.results[0][name] for name, _ in OUTS)
```
